# Optimizing a Trainium2 kernel written in Bass

```python
import math
import jax, jax.numpy as jnp
from jax import lax
import numpy as np

D_MODEL = 1024
BATCH = 1
SEQ = 128
DEPTH = 2
DEC_BATCH = 1
DEC_SEQ = 256
PAST_LEN = 128

GRID_W = 64
NA_W = D_MODEL // 4
NA_HEADS = 4
NA_DH = NA_W // NA_HEADS
NA_WIN_R = 8
NA_WIN_C = 16
DF_W = D_MODEL // 4
DF_HEADS = 4
DF_DV = DF_W // DF_HEADS
DF_DQK = DF_DV // 2
ML_W = D_MODEL // 2
ML_HEADS = 4
ML_DH = ML_W // ML_HEADS
ML_CHUNK = 128
MIX_W = NA_W + DF_W + ML_W
IN_COLS = 3 * NA_W + 2 * DF_HEADS * 2 * DF_DQK + DF_W + 4 * ML_W + 4 * ML_HEADS
N_EXPERTS = 32
TOP_K = 4
D_EXPERT = D_MODEL // 4
D_SHARED = D_EXPERT
ROUTED_SCALE = 2.5
ROPE_BASE = 10000.0
Q_BLOCK = 128
EPS = 1e-6

kernel_name = "hybrid_na_mlstm_diffattn_moe_dit_step"

F32 = jnp.float32

def rmsnorm(x, g):
    xf = x.astype(F32)
    y = xf * lax.rsqrt(jnp.mean(xf * xf, axis=-1, keepdims=True) + EPS)
    return (y * g.astype(F32)).astype(x.dtype)

def heads(a, n):
    B, L, _ = a.shape
    return a.reshape(B, L, n, -1).transpose(0, 2, 1, 3)

def merge(a):
    B, H, L, d = a.shape
    return a.transpose(0, 2, 1, 3).reshape(B, L, H * d)

def diff_heads(a):
    B, L, _ = a.shape
    return a.reshape(B, L, DF_HEADS, 2, DF_DQK).transpose(0, 2, 3, 1, 4)

def in_splits():
    sizes = [NA_W] * 3 + [DF_HEADS * 2 * DF_DQK] * 2 + [DF_W] + [ML_W] * 4
    return [int(s) for s in np.cumsum(sizes)]

def rope_2d(x):
    L, d = x.shape[-2], x.shape[-1]
    t = jnp.arange(L)
    row, col = t // GRID_W, t % GRID_W
    da = d // 2
    nf = da // 2
    inv = 1.0 / (ROPE_BASE ** (jnp.arange(nf, dtype=F32) / nf))
    xf = x.astype(F32)

    def rot(xa, pos):
        ang = pos.astype(F32)[:, None] * inv
        cs, sn = jnp.cos(ang), jnp.sin(ang)
        x1, x2 = xa[..., :nf], xa[..., nf:]
        return jnp.concatenate([x1 * cs - x2 * sn, x1 * sn + x2 * cs], axis=-1)

    return jnp.concatenate([rot(xf[..., :da], row), rot(xf[..., da:], col)], axis=-1).astype(x.dtype)

def block_attn(q, k, v):
    B, H, Lq, d = q.shape
    nb = Lq // Q_BLOCK
    qb = jnp.moveaxis(q.reshape(B, H, nb, Q_BLOCK, d), 2, 0)
    scale = d ** -0.5

    def f(qi):
        s = jnp.einsum('bhqd,bhkd->bhqk', qi, k).astype(F32) * scale
        p = jax.nn.softmax(s, axis=-1).astype(v.dtype)
        return jnp.einsum('bhqk,bhkd->bhqd', p, v)

    o = lax.map(f, qb)
    return jnp.moveaxis(o, 0, 2).reshape(B, H, Lq, v.shape[-1])

def diff_attn(q, k, v, lam):
    B, H, _, Lq, d = q.shape
    nb = Lq // Q_BLOCK
    qb = jnp.moveaxis(q.reshape(B, H, 2, nb, Q_BLOCK, d), 3, 0)
    scale = d ** -0.5

    def f(qi):
        s = jnp.einsum('bhaqd,bhakd->bhaqk', qi, k).astype(F32) * scale
        p = jax.nn.softmax(s, axis=-1)
        w = (p[:, :, 0] - lam * p[:, :, 1]).astype(v.dtype)
        return jnp.einsum('bhqk,bhkd->bhqd', w, v)

    o = lax.map(f, qb)
    return jnp.moveaxis(o, 0, 2).reshape(B, H, Lq, v.shape[-1])

def na_latent(q, k, v, kc, vc, rpb):
    B, H, L, d = q.shape
    rows = L // GRID_W
    wr = min(NA_WIN_R, rows)
    scale = d ** -0.5
    k5 = k.reshape(B, H, rows, GRID_W, d)
    v5 = v.reshape(B, H, rows, GRID_W, d)
    qr = jnp.moveaxis(q.reshape(B, H, rows, GRID_W, d), 2, 0)
    cols = jnp.arange(GRID_W)
    col_idx = jnp.clip(cols - NA_WIN_C // 2, 0, GRID_W - NA_WIN_C)[:, None] + jnp.arange(NA_WIN_C)
    col_off = col_idx - cols[:, None] + NA_WIN_C - 1
    nloc = wr * NA_WIN_C

    def row_fn(args):
        r, qi = args
        rs = jnp.clip(r - wr // 2, 0, rows - wr)
        kw = lax.dynamic_slice_in_dim(k5, rs, wr, axis=2)[:, :, :, col_idx]
        vw = lax.dynamic_slice_in_dim(v5, rs, wr, axis=2)[:, :, :, col_idx]
        row_off = rs + jnp.arange(wr) - r + NA_WIN_R - 1
        bias = rpb[:, row_off][:, :, col_off]
        s_loc = (jnp.einsum('bhqd,bhrqjd->bhqrj', qi, kw).astype(F32) * scale
                 + jnp.transpose(bias, (0, 2, 1, 3)).astype(F32))
        s_ctx = jnp.einsum('bhqd,bhcd->bhqc', qi, kc).astype(F32) * scale
        p = jax.nn.softmax(jnp.concatenate([s_loc.reshape(B, H, GRID_W, nloc), s_ctx], axis=-1), axis=-1)
        p = p.astype(v.dtype)
        return (jnp.einsum('bhqrj,bhrqjd->bhqd', p[..., :nloc].reshape(B, H, GRID_W, wr, NA_WIN_C), vw)
                + jnp.einsum('bhqc,bhcd->bhqd', p[..., nloc:], vc))

    o = lax.map(row_fn, (jnp.arange(rows), qr))
    return jnp.moveaxis(o, 0, 2).reshape(B, H, L, d)

def mlstm_chunked(q, k, v, ig, lf, C0, n0, m0):
    B, H, L, dk = q.shape
    dv = v.shape[-1]
    nc = L // ML_CHUNK

    def chunks(a):
        a = a.astype(F32)
        return jnp.moveaxis(a.reshape(B, H, nc, ML_CHUNK, *a.shape[3:]), 2, 0)

    tril = jnp.tril(jnp.ones((ML_CHUNK, ML_CHUNK), dtype=bool))

    def step(carry, inp):
        C, n, m = carry
        qc, kc, vc, ic, fc = inp
        b = jnp.cumsum(fc, axis=-1)
        logD = jnp.where(tril, b[..., :, None] - b[..., None, :] + ic[..., None, :], -jnp.inf)
        m_t = jnp.maximum(b + m[..., None], jnp.max(logD, axis=-1))
        Dw = jnp.exp(logD - m_t[..., None])
        w0 = jnp.exp(b + m[..., None] - m_t)
        S = jnp.einsum('bhtd,bhsd->bhts', qc, kc) * Dw
        num = w0[..., None] * jnp.einsum('bhtd,bhde->bhte', qc, C) + jnp.einsum('bhts,bhse->bhte', S, vc)
        den = w0 * jnp.einsum('bhtd,bhd->bht', qc, n) + jnp.sum(S, axis=-1)
        h = num / jnp.maximum(jnp.abs(den), jnp.exp(-m_t))[..., None]
        m_new = m_t[..., -1]
        ws = jnp.exp(b[..., -1:] - b + ic - m_new[..., None])
        decay = jnp.exp(b[..., -1] + m - m_new)
        C = decay[..., None, None] * C + jnp.einsum('bhsd,bhse->bhde', ws[..., None] * kc, vc)
        n = decay[..., None] * n + jnp.einsum('bhs,bhsd->bhd', ws, kc)
        return (C, n, m_new), h

    carry0 = (C0.astype(F32), n0.astype(F32), m0.astype(F32))
    (C, n, m), hs = lax.scan(step, carry0, (chunks(q), chunks(k), chunks(v), chunks(ig), chunks(lf)))
    h = jnp.moveaxis(hs, 0, 2).reshape(B, H, L, dv)
    return h.astype(v.dtype), (C, n, m)

def mlstm_bidir(q, k, v, gates, C0, n0, m0):
    ig_f, fg_f, ig_b, fg_b = gates[0], gates[1], gates[2], gates[3]
    flip = lambda a: jnp.flip(a, axis=2)
    hf, (Cf, nf, mf) = mlstm_chunked(q, k, v, ig_f, jax.nn.log_sigmoid(fg_f), C0[:, 0], n0[:, 0], m0[:, 0])
    hb, (Cb, nb, mb) = mlstm_chunked(flip(q), flip(k), flip(v), flip(ig_b), flip(jax.nn.log_sigmoid(fg_b)),
                                     C0[:, 1], n0[:, 1], m0[:, 1])
    h = hf + flip(hb)
    return h, jnp.stack([Cf, Cb], axis=1), jnp.stack([nf, nb], axis=1), jnp.stack([mf, mb], axis=1)

def mixers(h, lp, lam_init, ctx):
    B, L, _ = h.shape
    p = h @ lp['w_in']
    naq, nak, nav, dfq, dfk, dfv, mq, mk, mv, mo, mg = jnp.split(p, in_splits(), axis=-1)
    naq = rmsnorm(heads(naq, NA_HEADS), lp['na_qn'])
    nak = rmsnorm(heads(nak, NA_HEADS), lp['na_kn'])
    nav = heads(nav, NA_HEADS)
    dfq = rmsnorm(diff_heads(dfq), lp['df_qn'])
    dfk = rmsnorm(diff_heads(dfk), lp['df_kn'])
    dfv = heads(dfv, DF_HEADS)
    mq = heads(mq, ML_HEADS)
    mk = heads(mk, ML_HEADS) * (ML_DH ** -0.5)
    mv = heads(mv, ML_HEADS)
    mo = heads(mo, ML_HEADS)
    gates = (mg.reshape(B, L, 4, ML_HEADS).transpose(2, 0, 3, 1).astype(F32)
             + lp['ml_gate_b'].astype(F32)[:, None, :, None])
    lam_v = lp['df_lam'].astype(F32)
    lam = jnp.exp(jnp.sum(lam_v[0] * lam_v[1])) - jnp.exp(jnp.sum(lam_v[2] * lam_v[3])) + lam_init

    if ctx is None:
        na_o = block_attn(naq, nak, nav)
        df_o = diff_attn(dfq, dfk, dfv, lam)
        C0 = jnp.zeros((B, 2, ML_HEADS, ML_DH, ML_DH), F32)
        n0 = jnp.zeros((B, 2, ML_HEADS, ML_DH), F32)
        m0 = jnp.zeros((B, 2, ML_HEADS), F32)
    else:
        ck_na, cv_na, ck_df, cv_df, C0, n0, m0 = ctx
        na_o = na_latent(naq, nak, nav, ck_na.astype(naq.dtype), cv_na.astype(nav.dtype), lp['na_rpb'])
        k_all = jnp.concatenate([rope_2d(dfk), ck_df.astype(dfk.dtype)], axis=3)
        v_all = jnp.concatenate([dfv, cv_df.astype(dfv.dtype)], axis=2)
        df_o = diff_attn(rope_2d(dfq), k_all, v_all, lam)
    ml_h, Cn, nn_, mn = mlstm_bidir(mq, mk, mv, gates, C0, n0, m0)

    df_o = rmsnorm(df_o, lp['df_subln']) * (1.0 - lam_init)
    ml_o = rmsnorm(ml_h, lp['ml_outn']) * jax.nn.sigmoid(mo)
    out = jnp.concatenate([merge(na_o), merge(df_o), merge(ml_o)], axis=-1) @ lp['w_out']
    new_ctx = (nak, nav, dfk, dfv, Cn, nn_, mn) if ctx is None else None
    return out, new_ctx

def moe(h, lp):
    shp = h.shape
    t = h.reshape(-1, shp[-1])
    s = jax.nn.sigmoid((t @ lp['w_router']).astype(F32))
    _, idx = lax.top_k(s + lp['b_router'].astype(F32), TOP_K)
    s_sel = jnp.take_along_axis(s, idx, axis=-1)
    wts = s_sel / jnp.sum(s_sel, axis=-1, keepdims=True) * ROUTED_SCALE
    gates = jnp.sum(jax.nn.one_hot(idx, N_EXPERTS, dtype=F32) * wts[..., None], axis=1).astype(t.dtype)
    hid = jax.nn.silu(jnp.einsum('td,edf->tef', t, lp['w_exp1'])) * jnp.einsum('td,edf->tef', t, lp['w_exp3'])
    routed = jnp.einsum('tef,efd->td', hid * gates[:, :, None], lp['w_exp2'])
    shared = (jax.nn.silu(t @ lp['w_sh1']) * (t @ lp['w_sh3'])) @ lp['w_sh2']
    return (routed + shared).reshape(shp)

def trunk_layer(x, cond, ctx, lp, lam_init):
    mod = (jax.nn.silu(cond) @ lp['w_ada'] + lp['b_ada'])[:, None, :]
    sh1, sc1, g1, sh2, sc2, g2 = jnp.split(mod, 6, axis=-1)
    h = rmsnorm(x, lp['g_norm1']) * (1 + sc1) + sh1
    mix, new_ctx = mixers(h, lp, lam_init, ctx)
    x = x + g1 * mix
    h = rmsnorm(x, lp['g_norm2']) * (1 + sc2) + sh2
    x = x + g2 * moe(h, lp)
    return x, new_ctx

def setup_inputs(seed: int = 0) -> dict:
    key = jax.random.key(seed)
    ks = iter(jax.random.split(key, 48))
    nrm = lambda shape, scale: jax.random.normal(next(ks), shape, F32) * scale
    D = D_MODEL
    ig = nrm((DEPTH, 2, ML_HEADS), 0.1)
    fg = jnp.linspace(3.0, 6.0, ML_HEADS)[None, None, :] + nrm((DEPTH, 2, ML_HEADS), 0.1)
    ml_gate_b = jnp.stack([ig[:, 0], fg[:, 0], ig[:, 1], fg[:, 1]], axis=1)
    return {
        'x_prompt': nrm((BATCH, SEQ, D), 1.0),
        'x_sample': nrm((DEC_BATCH, DEC_SEQ, D), 1.0),
        'cache_na_k': nrm((DEC_BATCH, DEPTH, NA_HEADS, PAST_LEN, NA_DH), 1.0),
        'cache_na_v': nrm((DEC_BATCH, DEPTH, NA_HEADS, PAST_LEN, NA_DH), 1.0),
        'cache_df_k': nrm((DEC_BATCH, DEPTH, DF_HEADS, 2, PAST_LEN, DF_DQK), 1.0),
        'cache_df_v': nrm((DEC_BATCH, DEPTH, DF_HEADS, PAST_LEN, DF_DV), 1.0),
        'state_ml_C': nrm((DEC_BATCH, DEPTH, 2, ML_HEADS, ML_DH, ML_DH), 0.3),
        'state_ml_n': nrm((DEC_BATCH, DEPTH, 2, ML_HEADS, ML_DH), 0.3),
        'state_ml_m': nrm((DEC_BATCH, DEPTH, 2, ML_HEADS), 0.5),
        'c': nrm((DEC_BATCH, D), 1.0),
        'c_ctx': nrm((D,), 1.0),
        'w_ada': nrm((DEPTH, D, 6 * D), 0.5 * D ** -0.5),
        'b_ada': nrm((DEPTH, 6 * D), 0.02),
        'g_norm1': 1.0 + nrm((DEPTH, D), 0.05),
        'g_norm2': 1.0 + nrm((DEPTH, D), 0.05),
        'w_in': nrm((DEPTH, D, IN_COLS), D ** -0.5),
        'w_out': nrm((DEPTH, MIX_W, D), MIX_W ** -0.5),
        'na_qn': 1.0 + nrm((DEPTH, NA_DH), 0.05),
        'na_kn': 1.0 + nrm((DEPTH, NA_DH), 0.05),
        'na_rpb': nrm((DEPTH, NA_HEADS, 2 * NA_WIN_R - 1, 2 * NA_WIN_C - 1), 0.02),
        'df_qn': 1.0 + nrm((DEPTH, DF_DQK), 0.05),
        'df_kn': 1.0 + nrm((DEPTH, DF_DQK), 0.05),
        'df_lam': nrm((DEPTH, 4, DF_DQK), 0.1),
        'df_subln': 1.0 + nrm((DEPTH, DF_DV), 0.05),
        'ml_gate_b': ml_gate_b,
        'ml_outn': 1.0 + nrm((DEPTH, ML_DH), 0.05),
        'w_router': nrm((DEPTH, D, N_EXPERTS), D ** -0.5),
        'b_router': nrm((DEPTH, N_EXPERTS), 0.01),
        'w_exp1': nrm((DEPTH, N_EXPERTS, D, D_EXPERT), D ** -0.5),
        'w_exp3': nrm((DEPTH, N_EXPERTS, D, D_EXPERT), D ** -0.5),
        'w_exp2': nrm((DEPTH, N_EXPERTS, D_EXPERT, D), D_EXPERT ** -0.5),
        'w_sh1': nrm((DEPTH, D, D_SHARED), D ** -0.5),
        'w_sh3': nrm((DEPTH, D, D_SHARED), D ** -0.5),
        'w_sh2': nrm((DEPTH, D_SHARED, D), D_SHARED ** -0.5),
    }

def reference(x_prompt, x_sample, cache_na_k, cache_na_v, cache_df_k, cache_df_v, state_ml_C, state_ml_n,
              state_ml_m, c, c_ctx, w_ada, b_ada, g_norm1, g_norm2, w_in, w_out, na_qn, na_kn, na_rpb,
              df_qn, df_kn, df_lam, df_subln, ml_gate_b, ml_outn, w_router, b_router, w_exp1, w_exp3, w_exp2,
              w_sh1, w_sh3, w_sh2):
    y_p = x_prompt
    y_s = x_sample
    outs = [[] for _ in range(7)]
    for l in range(DEPTH):
        lp = {
            'w_ada': w_ada[l], 'b_ada': b_ada[l], 'g_norm1': g_norm1[l], 'g_norm2': g_norm2[l],
            'w_in': w_in[l], 'w_out': w_out[l], 'na_qn': na_qn[l], 'na_kn': na_kn[l], 'na_rpb': na_rpb[l],
            'df_qn': df_qn[l], 'df_kn': df_kn[l], 'df_lam': df_lam[l], 'df_subln': df_subln[l],
            'ml_gate_b': ml_gate_b[l], 'ml_outn': ml_outn[l], 'w_router': w_router[l], 'b_router': b_router[l],
            'w_exp1': w_exp1[l], 'w_exp3': w_exp3[l], 'w_exp2': w_exp2[l],
            'w_sh1': w_sh1[l], 'w_sh3': w_sh3[l], 'w_sh2': w_sh2[l],
        }
        lam_init = 0.8 - 0.6 * math.exp(-0.3 * l)
        y_p, ctx_l = trunk_layer(y_p, c_ctx[None, :], None, lp, lam_init)
        for i in range(7):
            outs[i].append(ctx_l[i])
        cache_l = (cache_na_k[:, l], cache_na_v[:, l], cache_df_k[:, l], cache_df_v[:, l],
                   state_ml_C[:, l], state_ml_n[:, l], state_ml_m[:, l])
        y_s, _ = trunk_layer(y_s, c, cache_l, lp, lam_init)
    new_na_k = jnp.stack(outs[0], axis=1)
    new_na_v = jnp.stack(outs[1], axis=1)
    new_df_k = jnp.stack(outs[2], axis=1)
    new_df_v = jnp.stack(outs[3], axis=1)
    new_ml_C = jnp.stack(outs[4], axis=1)
    new_ml_n = jnp.stack(outs[5], axis=1)
    new_ml_m = jnp.stack(outs[6], axis=1)
    return (y_p, y_s, new_na_k, new_na_v, new_df_k, new_df_v, new_ml_C, new_ml_n, new_ml_m)


_drawn_inputs = setup_inputs


def setup_inputs(seed=0):
    import zlib

    import numpy as np

    out = dict(_drawn_inputs(seed))
    spreads = {}
    factors = {'na_qn': 2.67, 'na_rpb': 29.405}
    for name, (base, spread) in spreads.items():
        noise = np.random.default_rng([zlib.crc32(name.encode()), seed]).standard_normal(out[name].shape)
        drawn = base * np.exp(spread * noise) if base else spread * noise
        out[name] = __import__('jax').numpy.asarray(drawn.astype(out[name].dtype))
    for name, factor in factors.items():
        out[name] = (out[name] * factor).astype(out[name].dtype)
    return out
```

```python
from contextlib import ExitStack

import concourse.bass as bass
import numpy as np
from concourse import mybir

F32 = mybir.dt.float32
F32R = mybir.dt.float32r
I32 = mybir.dt.int32
U32 = mybir.dt.uint32
HIGH_BITS = 0xFFFFF000
ALU = mybir.AluOpType
ACT = mybir.ActivationFunctionType
AX = mybir.AxisListType

P = 128
DEPTH, D = 2, 1024
DEPTH_RUN = DEPTH
KC = D // P
T = 3
GRID_W = 64
NAH, NAD = 4, 64
DFH, DFD, DFV = 4, 32, 64
MLH, MLD = 4, 128
NA_W, DF_W, ML_W = 256, 256, 512
IN_COLS = 3600
NE, TOPK, DE = 32, 4, 256
ROUTED_SCALE = 2.5
EPS = 1e-6
WIN_C = 16
RPB_R, RPB_C = 15, 31
NEG = -1e30
SLOTS = P
GROUP = 4
SLOTF = 2048

C_ID, C_IOTA, C_TRIU, C_ONES, C_MF, C_MB = 0, 128, 256, 384, 512, 640
C_COL, C_COS, C_SIN, C_LAM, C_SEL, C_SELC, C_N = 768, 832, 896, 960, 964, 1476, 1732
B_NAG, B_DFG, B_SUB, B_OUT, B_GB, B_BR, B_LAM, B_N = 0, 128, 192, 256, 384, 400, 432, 560


def constants():
    c = np.zeros((P, C_N), np.float32)
    p = np.arange(P)
    c[:, C_ID:C_ID + P] = np.eye(P)
    c[:, C_IOTA:C_IOTA + P] = p[None, :]
    c[:, C_TRIU:C_TRIU + P] = p[:, None] < p[None, :]
    c[:, C_ONES:C_ONES + P] = 1.0
    c[:, C_MF:C_MF + P] = np.where(p[:, None] <= p[None, :], 0.0, 1e30)
    c[:, C_MB:C_MB + P] = np.where(p[:, None] >= p[None, :], 0.0, 1e30)
    col = p % GRID_W
    first = np.clip(col - WIN_C // 2, 0, GRID_W - WIN_C)
    k = np.arange(GRID_W)
    c[:, C_COL:C_COL + GRID_W] = np.where((k >= first[:, None]) & (k < first[:, None] + WIN_C), 0.0, NEG)
    nf = DFD // 4
    inv = 1.0 / (10000.0 ** (np.arange(nf, dtype=np.float32) / nf))
    for t in range(2):
        row = (t * P + p) // GRID_W
        for a, pos in enumerate((row, col)):
            ang = pos.astype(np.float32)[:, None] * inv
            at = t * DFD + a * 2 * nf
            c[:, C_COS + at:C_COS + at + nf] = c[:, C_COS + at + nf:C_COS + at + 2 * nf] = np.cos(ang)
            c[:, C_SIN + at:C_SIN + at + nf] = -np.sin(ang)
            c[:, C_SIN + at + nf:C_SIN + at + 2 * nf] = np.sin(ang)
    for layer in range(DEPTH):
        lam_init = 0.8 - 0.6 * np.exp(-0.3 * layer)
        c[:, C_LAM + 2 * layer] = lam_init
        c[:, C_LAM + 2 * layer + 1] = 1.0 - lam_init
    for h in range(MLH):
        c[h, C_SEL + h * P:C_SEL + (h + 1) * P] = 1.0
    for i in range(2):
        c[i, C_SELC + i * P:C_SELC + (i + 1) * P] = 1.0
    return c


def hi(ap):
    return ap.bitcast(F32R)


def round_high(eng, out, in_):
    return eng.tensor_copy(hi(out), in_)


class Chain:

    def __init__(self, eng, sem, base=0):
        self.eng, self.sem, self.n, self.base = eng, sem, 0, base

    def __call__(self, ins):
        self.n += 1
        ins.then_inc(self.sem, 1)
        self.eng.wait_ge(self.sem, self.base + self.n)
        return ins


def program(nc, A, O, debug=None):
    with ExitStack() as top:
        top.enter_context(nc.allow_non_contiguous_dma(reason="a few short vectors are loaded across partitions"))
        def sb(name, shape, dt=F32, ctx=top):
            return ctx.enter_context(nc.sbuf_tensor(name, shape, dt))

        sems = []

        def sem(name):
            s = top.enter_context(nc.semaphore(name))
            sems.append(s)
            return s

        def end_section():
            nc.all_engine_barrier()
            nc.gpsimd.dma_reset(range(sems[0].num, sems[-1].num + 1))
            nc.gpsimd.sem_clear(range(sems[0].num, sems[-1].num + 1))
            nc.all_engine_barrier()

        cst = sb("cst", [P, C_N])
        x = sb("x", [P, T, D])
        prm = sb("prm", [P, B_N])
        mcol = sb("mcol", [P, 64])
        gate = sb("gate", [P, 2, D])
        small = sb("small", [P, 256])
        npass = sb("npass", [P, 1], I32)
        nhalf = small[:, 0:8]
        ssq, rstd = small[:, 32:35], small[:, 36:39]
        PS = top.enter_context(nc.psum_tensor("PS", [P, 8, 512], F32))

        ident = cst[:, C_ID:C_ID + P]
        ones = cst[:, C_ONES:C_ONES + P]

        NRING = 12
        landed = [sem(f"slot_landed{i}") for i in range(NRING)]
        slot_used = sem("slot_used")
        loaded = sem("small_loaded")
        loaded2 = sem("late_loaded")
        stored = sem("stored")
        chain_v = sem("vector_chain")
        chain_s = sem("scalar_chain")
        chain_p = sem("pool_chain")
        chain_t = sem("tensor_chain")
        N = {k: sem(k) for k in (
            "csilu", "mod_row", "mod_tr", "mod_col",
            "ssq_ready", "rstd_ready", "xn_ready", "xn_tr", "hT_s", "hT_v",
            "tail_mm", "proj_mm", "proj_ev", "lf_ready", "rows_tr", "rows_v",
            "cols_mm", "ctx_tr", "ctx_ev", "sq_ready", "ms_ready", "r_ready", "qk_ready",
            "att_tr", "att_ev", "sc_mm", "nm_ready", "ex_ready", "w_ready", "pt_mm", "pt_ev",
            "pv_mm", "pv_ev", "exin", "exout", "mix_df", "mqk_tr", "mqk_ev", "st_mm", "st_ev",
            "mb_mm", "mb_free", "d_ready", "e_ready", "s_ready", "wk_ready", "num_mm", "num_ev", "upd_mm",
            "c_ready", "ml_done", "sig_e", "mix_ready", "mix_tr", "mix_ev", "out_mm", "x_done",
            "rt_mm", "rt_e", "rt_s", "mask_ready", "pos_mm", "back_tr", "back_ev", "total_mm", "route_done",
            "cut_v", "cut_p", "low_v", "low_p", "he_ev", "ga_mm", "gs_mm", "gs_ev", "pb_ready", "silu", "hid_ready",
            "ht_mm", "ht_ev", "hidT_low", "y_high", "y_low", "sc_ev",
            "sh_mm", "sh_silu", "sh_hid", "sh_tr", "sh_trev", "sh_down", "sh_done",
        )}
        S = N

        modd = nc.dram_tensor("mod_rows", [DEPTH, 2, 6 * D], F32, kind="Internal").ap()
        mcold = nc.dram_tensor("mod_cols", [DEPTH, P, 64], F32, kind="Internal").ap()
        biasd = nc.dram_tensor("na_bias", [DEPTH, 2, P, NAH, 256], F32, kind="Internal").ap()

        def bcast(ap, n):
            return bass.AP(tensor=ap.tensor, offset=ap.offset, ap=[[0, P], [1, n]])

        with ExitStack() as sec:
            ring = sb("ring0", [P, NRING, SLOTF], ctx=sec)
            modr = sb("modr", [2, 6 * D], ctx=sec)
            bada = sb("bada", [2, 6 * D], ctx=sec)
            gn = sb("gn", [2, 2, D], ctx=sec)
            ccol = sb("ccol", [P, KC, 2], ctx=sec)
            mstage = sb("mstage", [P, 64], ctx=sec)
            NB = 12

            with nc.Block() as block:
                @block.sync
                def _(sp):
                    sp.dma_start(cst[:, :], A["consts"]).then_inc(loaded, 16)
                    sp.dma_start(ccol[:, :, 0], A["c_ctx"].rearrange("(c p) -> p c", p=P)).then_inc(loaded, 16)
                    sp.dma_start(ccol[:, :, 1], A["c"][0].rearrange("(c p) -> p c", p=P)).then_inc(loaded, 16)
                    sp.dma_start(x[:, 0, :], A["x_prompt"][0]).then_inc(loaded, 16)
                    sp.dma_start(x[:, 1:3, :], A["x_sample"][0].rearrange("(t p) d -> p t d", p=P)).then_inc(loaded, 16)
                    n = 0
                    for l in range(DEPTH):
                        for b in range(NB):
                            for half in range(2):
                                if n >= NRING:
                                    sp.wait_ge(slot_used, n - NRING + 1)
                                src = A["w_ada"][l, half * 512:(half + 1) * 512, b * 512:(b + 1) * 512]
                                sp.dma_start(ring[:, n % NRING, :].rearrange("p (c n) -> p c n", c=4),
                                             src.rearrange("(c p) n -> p c n", p=P)).then_inc(landed[n % NRING], 16)
                                n += 1

                @block.gpsimd
                def _(pool):
                    pool.memset(nhalf, -0.5).then_inc(chain_p, 1)
                    for l in range(DEPTH):
                        for t in range(2):
                            for r2 in range(2):
                                for h in range(NAH):
                                    r = 2 * t + r2
                                    base = A["na_rpb"][l, h]
                                    src = bass.AP(tensor=base.tensor,
                                                  offset=base.offset + (7 - r) * RPB_C + WIN_C - 1,
                                                  ap=[[RPB_C, 4], [-1, 64], [1, 64]])
                                    pool.dma_start(
                                        biasd[l, t, r2 * 64:(r2 + 1) * 64, h].rearrange("q (j k) -> j q k", j=4),
                                        src).then_inc(loaded2, 16)
                    for l in range(DEPTH):
                        pool.wait_ge(S["mod_col"], l + 1)
                        pool.dma_start(mcold[l], mstage[:, :]).then_inc(stored, 16)
                        pool.dma_start(modd[l], modr[:, :]).then_inc(stored, 16)
                        pool.wait_ge(stored, 32 * (l + 1))
                    pool.wait_ge(loaded2, 16 * 32)

                @block.scalar
                def _(act):
                    for l in range(DEPTH):
                        if l:
                            act.wait_ge(stored, 32 * l)
                        for i in range(2):
                            act.dma_start(bada[i:i + 1, :], A["b_ada"][l].rearrange("(o n) -> o n", o=1)).then_inc(S["exin"], 16)
                            act.dma_start(gn[i:i + 1, 0, :], A["g_norm1"][l].rearrange("(o n) -> o n", o=1)).then_inc(S["exin"], 16)
                            act.dma_start(gn[i:i + 1, 1, :], A["g_norm2"][l].rearrange("(o n) -> o n", o=1)).then_inc(S["exin"], 16)
                        if l == 0:
                            act.wait_ge(loaded, 80)
                            act.activation(ccol[:, :, :], ccol[:, :, :], ACT.Silu).then_inc(S["csilu"], 1)

                @block.tensor
                def _(pe):
                    pe.wait_ge(S["csilu"], 1)
                    n = 0
                    for l in range(DEPTH):
                        for b in range(NB):
                            i = l * NB + b
                            if i >= 2:
                                pe.wait_ge(S["mod_row"], i - 1)
                            for half in range(2):
                                pe.wait_ge(landed[n % NRING], 16 * (n // NRING + 1))
                                for c in range(4):
                                    k = half * 4 + c
                                    mm = pe.matmul(PS[0:2, i % 2, :], ccol[:, k, :],
                                                   ring[:, n % NRING, c * 512:(c + 1) * 512],
                                                   start=(k == 0), stop=(k == 7))
                                mm.then_inc(slot_used, 1)
                                n += 1
                        pe.wait_ge(S["exout"], l + 1)
                        for kind, at in enumerate((0, D, 3 * D, 4 * D)):
                            for c in range(KC):
                                o = (kind * KC + c) * 2
                                mm = pe.transpose(PS[:, 2, o:o + 2], modr[:, at + c * P:at + (c + 1) * P], ident[0:2, 0:2])
                        mm.then_inc(S["mod_tr"], 1)

                @block.vector
                def _(dve):
                    v = Chain(dve, chain_v)
                    for l in range(DEPTH):
                        dve.wait_ge(S["exin"], 96 * (l + 1))
                        if l:
                            dve.wait_ge(stored, 32 * l)
                        for b in range(NB):
                            dve.wait_ge(slot_used, 2 * (l * NB + b + 1))
                            dve.tensor_tensor(modr[:, b * 512:(b + 1) * 512], PS[0:2, b % 2, :],
                                              bada[:, b * 512:(b + 1) * 512], ALU.add).then_inc(S["mod_row"], 1)
                        dve.wait_ge(S["mod_row"], NB * (l + 1))
                        for i, at in enumerate((D, 4 * D)):
                            v(dve.scalar_tensor_tensor(modr[:, at:at + D], modr[:, at:at + D], 1.0, gn[:, i, :],
                                                       ALU.add, ALU.mult))
                        dve.sem_inc(S["exout"], 1)
                        dve.wait_ge(S["mod_tr"], l + 1)
                        dve.tensor_copy(mstage[:, :], PS[:, 2, 0:64]).then_inc(S["mod_col"], 1)

            end_section()

        def norm_act(act, which):
            for t in range(T):
                act.activation(tok[:, t, :], x[:, t, :], ACT.Square, accum_out=ssq[:, t:t + 1]).then_inc(S["ssq_ready"], 1)

        def norm_pool(pool, chain):
            pool.wait_ge(S["ssq_ready"], T)
            chain(pool.tensor_scalar(rstd, ssq, 1.0 / D, EPS, ALU.mult, ALU.add))
            pool.tensor_tensor(rstd, rstd, nhalf[:, 0:T], ALU.pow).then_inc(S["rstd_ready"], 1)

        def norm_dve(dve):
            dve.wait_ge(S["rstd_ready"], 1)
            for t in range(T):
                dve.tensor_scalar(tok[:, t, :], x[:, t, :], rstd[:, t:t + 1], None, ALU.mult).then_inc(S["xn_ready"], 1)

        def norm_pe(pe):
            for t in range(T):
                pe.wait_ge(S["xn_ready"], t + 1)
                for half in range(2):
                    i = 2 * t + half
                    if i >= 4:
                        pe.wait_ge(S["hT_s" if half == 0 else "hT_v"], 4 * (t - 1))
                    for c in range(4):
                        k = half * 4 + c
                        mm = pe.transpose(PS[:, i % 4, c * P:(c + 1) * P], tok[:, t, k * P:(k + 1) * P], ident)
                    mm.then_inc(S["xn_tr"], 1)

        def mod_at(kind, k, t):
            o = (kind * KC + k) * 2 + min(t, 1)
            return mcol[:, o:o + 1]

        def norm_ev_act(act, which, hT):
            for t in range(T):
                act.wait_ge(S["xn_tr"], 2 * t + 1)
                for c in range(4):
                    act.activation(hT[:, c, t * P:(t + 1) * P], PS[:, (2 * t) % 4, c * P:(c + 1) * P], ACT.Identity,
                                   bias=mod_at(2 * which, c, t), scale=mod_at(2 * which + 1, c, t)).then_inc(S["hT_s"], 1)

        def norm_ev_dve(dve, which, hT):
            for t in range(T):
                dve.wait_ge(S["xn_tr"], 2 * t + 2)
                for c in range(4):
                    k = 4 + c
                    dve.tensor_scalar(hT[:, k, t * P:(t + 1) * P], PS[:, (2 * t + 1) % 4, c * P:(c + 1) * P],
                                      mod_at(2 * which + 1, k, t), mod_at(2 * which, k, t),
                                      ALU.mult, ALU.add).then_inc(S["hT_v"], 1)


        nm, rs, rr = small[:, 84:88], small[:, 88:92], small[:, 92:96]
        nlam, omli = small[:, 96:97], small[:, 97:98]
        lamt = small[:, 98:102]
        zrow = small[0:4, 128:256]
        NSA = 4
        ML_ORDER = [(0, 0), (0, 1), (1, 0), (2, 1), (2, 0), (1, 1)]
        BATCHES = [(t, kind) for t in range(T) for kind in ("na", "df0", "df1")]
        UNITS = [(g, t) for g in range(3, 7) for t in range(T)]
        LATE = 2

        with nc.Fori(0, DEPTH_RUN) as l:
            with ExitStack() as sec:
                tok = sb("tokA", [P, T, D], ctx=sec)
                ring = sb("ringA", [P, NSA, SLOTF], ctx=sec)
                hT = sb("hT", [P, KC, T * P], ctx=sec)
                p = sb("p", [P, T, 2560], ctx=sec)
                attT = sb("attT", [P, 8, 512], ctx=sec)
                bias = sb("bias", [P, 2, NAH, 256], ctx=sec)
                W1 = sb("W1", [P, 4, 384], ctx=sec)
                W2 = sb("W2", [P, 4, 384], ctx=sec)
                PT = sb("PT", [P, 2, 384], ctx=sec)
                ckv = sb("ckv", [P, 4, 256], ctx=sec)
                vaug = sb("vaug", [P, T, MLH, MLD + 1], ctx=sec)
                Caug = sb("Caug", [P, 8, MLD + 1], ctx=sec)
                Cp = sb("Cp", [P, 8, MLD + 1], ctx=sec)
                ST = sb("ST", [P, T, 512], ctx=sec)
                mlh = sb("mlh", [P, T, 512], ctx=sec)
                num = sb("num", [P, 4, MLD + 1], ctx=sec)
                tmp = sb("tmp", [P, 4, MLD + 1], ctx=sec)
                wk = sb("wk", [P, 512], ctx=sec)
                R = sb("R", [4, T, 2, 2, P], ctx=sec)
                brow = sb("brow", [4, T, 2, P], ctx=sec)
                sm = sb("sm", [P, 512], ctx=sec)
                gt = sm[:, 0:48].rearrange("p (t g) -> p t g", t=T)
                e1 = sm[:, 48:72].rearrange("p (t d h) -> p t d h", t=T, d=2)
                e2 = sm[:, 72:96].rearrange("p (t d h) -> p t d h", t=T, d=2)
                cols = sm[:, 96:168].rearrange("p (q n) -> p q n", q=3)
                bcs = sm[:, 168:216].rearrange("p (n k h) -> p n k h", n=6, k=2)
                arg = sm[:, 216:312].rearrange("p (q n) -> p q n", q=4)
                ms = sm[:, 312:384]
                ms2 = sm[:, 384:396]
                den = sm[:, 396:400]
                scal = sm[0:4, 400:412].rearrange("p (n k) -> p n k", n=6)
                diag = sm[0:4, 412:460].rearrange("p (n h) -> p n h", n=12)
                m0 = sm[0:4, 460:462]
                mout = sm[0:4, 462:464]
                nq = W1[:, :, :].rearrange("p a b -> p (a b)")
                dq = W2[:, :, :].rearrange("p a b -> p (a b)")
                last = lambda d: P - 1 if d == 0 else 0

                def col4(q, td):
                    return cols[:, q, 4 * td:4 * td + 4]

                def arg4(q, td):
                    return arg[:, q, 4 * td:4 * td + 4]

                def keys_of(t):
                    return (0, P) if t == 0 else (P, 512)

                def aps_of(batch):
                    t, kind = batch
                    k0, k1 = keys_of(t)
                    out = []
                    for m in range(4):
                        if kind == "na":
                            i, rows = m // 2, slice(64 * (m % 2), 64 * (m % 2) + 64)
                            j = 2 + i
                        else:
                            hf = int(kind[2])
                            i, rows = 4 + hf, slice(32 * m, 32 * m + 32)
                            j = 6 + hf
                        out.append((attT[rows, i, t * P:(t + 1) * P], attT[rows, j, k0:k1]))
                    return out

                def values_of(batch, m):
                    t, kind = batch
                    at, ck, h = (512, 1, m) if kind == "na" else (1280, 3, 2 * int(kind[2]) + m)
                    if t == 0:
                        return [p[:, 0, at + 64 * h:at + 64 * h + 64]]
                    return [p[:, u, at + 64 * h:at + 64 * h + 64] for u in (1, 2)] + [ckv[:, ck, 64 * h:64 * h + 64]]

                n_maps = lambda batch: 4 if batch[1] == "na" else 2
                first_map = [sum(n_maps(b) for b in BATCHES[:i]) for i in range(len(BATCHES) + 1)]

                with nc.Block() as block:
                    @block.sync
                    def _(sp):
                        for at, n, name in ((B_NAG, 64, "na_qn"), (B_NAG + 64, 64, "na_kn"), (B_DFG, 32, "df_qn"),
                                            (B_DFG + 32, 32, "df_kn"), (B_SUB, 64, "df_subln"), (B_OUT, 128, "ml_outn"),
                                            (B_BR, 32, "b_router")):
                            sp.dma_start(prm[:, at:at + n], bcast(A[name][l], n)).then_inc(loaded, 16)
                        sp.dma_start(prm[:, B_GB:B_GB + 16], bcast(A["ml_gate_b"][l], 16)).then_inc(loaded, 16)
                        sp.dma_start(prm[:, B_LAM:B_LAM + 128], bcast(A["df_lam"][l], 128)).then_inc(loaded, 16)
                        sp.dma_start(mcol[:, :], mcold[l]).then_inc(loaded, 16)
                        sp.dma_start(m0, A["state_ml_m"][0, l].rearrange("r h -> h r")).then_inc(loaded, 16)
                        n = 0

                        def slot_free():
                            if n >= NSA:
                                sp.wait_ge(slot_used, n - NSA + 1)

                        sp.dma_start(ring[:, 0, 0:128].rearrange("p (c n) -> p c n", c=KC),
                                     A["w_in"][l, :, 3584:3600].rearrange("(c p) n -> p c n", p=P)).then_inc(landed[0], 16)
                        n = 1
                        for w, groups in (("w_in", 7), ("w_out", 2)):
                            for gr in range(groups):
                                for half in range(2):
                                    slot_free()
                                    src = A[w][l, half * 512:(half + 1) * 512, gr * 512:(gr + 1) * 512]
                                    sp.dma_start(ring[:, n % NSA, :].rearrange("p (c n) -> p c n", c=4),
                                                 src.rearrange("(c p) n -> p c n", p=P)).then_inc(landed[n % NSA], 16)
                                    n += 1

                    @block.gpsimd
                    def _(pool):
                        c = Chain(pool, chain_p)
                        for i in range(2):
                            pool.dma_start(gate[:, i, :], bcast(modd[l, i, 2 * D:3 * D], D)).then_inc(loaded2, 16)
                        pool.dma_start(ckv[:, 0, :].rearrange("p (h d) -> p h d", h=4),
                                       A["cache_na_k"][0, l].rearrange("h k d -> k h d")).then_inc(loaded2, 16)
                        pool.dma_start(ckv[:, 1, :].rearrange("p (h d) -> p h d", h=4),
                                       A["cache_na_v"][0, l].rearrange("h k d -> k h d")).then_inc(loaded2, 16)
                        pool.dma_start(ckv[:, 2, :].rearrange("p (h d) -> p h d", h=8),
                                       A["cache_df_k"][0, l].rearrange("h a k d -> k (h a) d")).then_inc(loaded2, 16)
                        pool.dma_start(ckv[:, 3, :].rearrange("p (h d) -> p h d", h=4),
                                       A["cache_df_v"][0, l].rearrange("h k d -> k h d")).then_inc(loaded2, 16)
                        for t in range(2):
                            pool.dma_start(bias[:, t, :, :], biasd[l, t]).then_inc(loaded2, 16)
                        pool.dma_start(Caug[:, :, 0:MLD], A["state_ml_C"][0, l].rearrange("r h d e -> d (r h) e")).then_inc(loaded2, 16)
                        pool.dma_start(Caug[:, :, MLD], A["state_ml_n"][0, l].rearrange("r h d -> d (r h)")).then_inc(loaded2, 16)
                        norm_pool(pool, c)
                        pool.wait_ge(S["ms_ready"], 1)
                        pool.tensor_tensor(ms, ms, nhalf[:, 0:1].to_broadcast([P, 72]), ALU.pow).then_inc(S["r_ready"], 1)
                        pool.wait_ge(S["qk_ready"], 1)
                        pool.dma_start(O["new_na_k"][0, l].rearrange("h p d -> p h d"),
                                       p[:, 0, 256:512].rearrange("p (h d) -> p h d", h=4)).then_inc(stored, 16)
                        pool.dma_start(O["new_na_v"][0, l].rearrange("h p d -> p h d"),
                                       p[:, 0, 512:768].rearrange("p (h d) -> p h d", h=4)).then_inc(stored, 16)
                        pool.dma_start(O["new_df_k"][0, l].rearrange("h a p d -> p (h a) d"),
                                       p[:, 0, 1024:1280].rearrange("p (h d) -> p h d", h=8)).then_inc(stored, 16)
                        pool.dma_start(O["new_df_v"][0, l].rearrange("h p d -> p h d"),
                                       p[:, 0, 1280:1536].rearrange("p (h d) -> p h d", h=4)).then_inc(stored, 16)
                        for i in range(2):
                            pool.wait_ge(S["ms_ready"], 2 + i)
                            pool.tensor_tensor(ms2, ms2, nhalf[:, 0:1].to_broadcast([P, 12]), ALU.pow).then_inc(S["r_ready"], 1)
                        pool.wait_ge(S["c_ready"], 2)
                        pool.dma_start(O["new_ml_C"][0, l].rearrange("r h d e -> d (r h) e"), Cp[:, :, 0:MLD]).then_inc(stored, 16)
                        pool.dma_start(O["new_ml_n"][0, l].rearrange("r h d -> d (r h)"), Cp[:, :, MLD]).then_inc(stored, 16)
                        pool.dma_start(O["new_ml_m"][0, l].rearrange("r h -> h r"), mout).then_inc(stored, 16)
                        pool.wait_ge(stored, 16 * 7)

                    @block.scalar
                    def _(act):
                        a = Chain(act, chain_s)
                        norm_act(act, 0)
                        act.wait_ge(loaded, 16 * 11)
                        norm_ev_act(act, 0, hT)
                        act.wait_ge(S["exin"], 1)
                        a(act.activation(e1, e1, ACT.Exp, scale=-1.0))
                        act.activation(e1, e1, ACT.Ln, bias=ones[:, 0:1]).then_inc(S["exout"], 1)

                        def proj_evac(u, g, t):
                            act.wait_ge(S["proj_mm"], u + 1)
                            dst = {3: tok[:, t, 512:1024], 4: p[:, t, 1536:2048], 6: p[:, t, 2048:2560],
                                   5: vaug[:, t, :, 0:MLD]}.get(g)
                            if dst is None:
                                dst = p[:, t, g * 512:(g + 1) * 512]
                            src = PS[:, u % 2, :]
                            if g == 5:
                                src = src.rearrange("p (h d) -> p h d", h=4)
                            act.activation(dst, src, ACT.Copy).then_inc(S["proj_ev"], 1)

                        u = 0
                        for g in range(3):
                            for t in range(T):
                                proj_evac(u, g, t)
                                u += 1
                                if g == 0:
                                    act.wait_ge(S["proj_ev"], u)
                                    act.activation(nq[:, t * 512:(t + 1) * 512], p[:, t, 0:512], ACT.Square).then_inc(S["sq_ready"], 1)
                                if g == 2:
                                    act.wait_ge(S["proj_ev"], u)
                                    act.activation(dq[:, t * 512:(t + 1) * 512], p[:, t, 768:1280], ACT.Square).then_inc(S["sq_ready"], 1)
                            if g == 0:
                                act.wait_ge(S["ctx_tr"], 1)
                                for j, idx in enumerate((2, 3, 6, 7)):
                                    act.activation(attT[:, idx, 384:512], PS[:, 4, j * P:(j + 1) * P], ACT.Copy).then_inc(S["ctx_ev"], 1)
                        act.wait_ge(S["exin"], 2)
                        act.activation(arg, arg, ACT.Exp).then_inc(S["exout"], 1)
                        act.wait_ge(S["exin"], 3)
                        act.activation(lamt[:, 2:4], lamt[:, 0:2], ACT.Exp).then_inc(S["exout"], 1)

                        def exps(i):
                            t, kind = BATCHES[i]
                            nk = keys_of(t)[1] - keys_of(t)[0]
                            act.wait_ge(S["nm_ready"], i + 1)
                            for m in range(4):
                                src = W1[:, m, 0:nk] if kind == "na" else PS[:, 2 + m, 0:nk]
                                act.activation(W2[:, m, 0:nk], src, ACT.Exp, bias=nm[:, m:m + 1],
                                               scale=1.0 if kind == "na" else DFD ** -0.5,
                                               accum_out=rs[:, m:m + 1]).then_inc(S["ex_ready"], 1)

                        def pt_evac(i):
                            t, kind = BATCHES[i]
                            nk = keys_of(t)[1] - keys_of(t)[0]
                            for m in range(first_map[i], first_map[i + 1]):
                                act.wait_ge(S["pt_mm"], m + 1)
                                if m >= 2:
                                    act.wait_ge(S["pv_mm"], m - 1)
                                act.activation(PT[:, m % 2, 0:nk], PS[:, 6 + m % 2, 0:nk], ACT.Copy).then_inc(S["pt_ev"], 1)

                        for i, (g, t) in enumerate(UNITS):
                            proj_evac(u, g, t)
                            u += 1
                            b = i - LATE
                            if b == -1:
                                for t2 in range(T):
                                    act.wait_ge(S["att_tr"], t2 + 1)
                                    for j in range(2):
                                        act.activation(attT[:, 4 * j:4 * j + 4, t2 * P:(t2 + 1) * P],
                                                       PS[:, 2 + 2 * (t2 % 2) + j, :].rearrange("p (c n) -> p c n", c=4),
                                                       ACT.Copy).then_inc(S["att_ev"], 1)
                            if 0 <= b < len(BATCHES):
                                pt_evac(b)
                            if 0 <= b + 1 < len(BATCHES):
                                exps(b + 1)
                        for t in range(T):
                            act.wait_ge(S["mqk_tr"], t + 1)
                            for j in range(2):
                                act.activation(hT[:, 4 * j:4 * j + 4, t * P:(t + 1) * P],
                                               PS[:, 2 + 2 * t + j, :].rearrange("p (c n) -> p c n", c=4),
                                               ACT.Copy, scale=MLD ** -0.5 if j else 1.0).then_inc(S["mqk_ev"], 1)
                        for t in range(T):
                            act.wait_ge(S["st_mm"], t + 1)
                            act.activation(ST[:, t, :], PS[:, t, :], ACT.Copy).then_inc(S["st_ev"], 1)
                        act.activation(dq.rearrange("p (t n) -> p t n", t=T), p[:, :, 2048:2560], ACT.Exp, scale=-1.0).then_inc(S["sig_e"], 1)
                        for i in range(6):
                            act.wait_ge(S["d_ready"], i + 1)
                            act.activation(tmp[:, :, 0:P], tmp[:, :, 0:P], ACT.Exp, scale=-1.0).then_inc(S["e_ready"], 1)
                        act.wait_ge(S["ml_done"], 1)
                        act.activation(nq.rearrange("p (t n) -> p t n", t=T), mlh[:, :, :], ACT.Square).then_inc(S["sq_ready"], 1)
                        for t in range(T):
                            act.wait_ge(S["mix_tr"], 2 * t + 1)
                            act.activation(hT[:, 0:4, t * P:(t + 1) * P],
                                           PS[:, (2 * t) % 4, :].rearrange("p (c n) -> p c n", c=4), ACT.Copy).then_inc(S["hT_s"], 1)

                    @block.tensor
                    def _(pe):
                        n = 0

                        def slot(c, n0, n1):
                            return ring[:, n % NSA, c * 512 + n0:c * 512 + n1]

                        norm_pe(pe)
                        pe.wait_ge(S["hT_s"], 4 * T)
                        pe.wait_ge(S["hT_v"], 4 * T)
                        pe.wait_ge(landed[0], 16)
                        for t in range(T):
                            for k in range(KC):
                                mm = pe.matmul(PS[:, 4, t * 16:(t + 1) * 16], hT[:, k, t * P:(t + 1) * P],
                                               ring[:, 0, k * 16:(k + 1) * 16], start=(k == 0), stop=(k == KC - 1))
                            if t < T - 1:
                                continue
                            mm.then_inc(S["tail_mm"], 1)
                        pe.wait_ge(S["tail_mm"], 1)
                        pe.sem_inc(slot_used, 1)
                        n = 1

                        def project(u, t, last_chunk):
                            nonlocal n
                            if u >= 2:
                                pe.wait_ge(S["proj_ev"], u - 1)
                            for half in range(2):
                                s = (n + half) % NSA
                                pe.wait_ge(landed[s], 16 * ((n + half) // NSA + 1))
                                for c in range(4):
                                    k = half * 4 + c
                                    mm = pe.matmul(PS[:, u % 2, :], hT[:, k, t * P:(t + 1) * P],
                                                   ring[:, s, c * 512:(c + 1) * 512], start=(k == 0), stop=(k == 7))
                                if last_chunk and half == 0:
                                    mm.then_inc(slot_used, 1)
                            mm.then_inc(S["proj_mm"], 1)
                            if last_chunk:
                                pe.wait_ge(S["proj_mm"], u + 1)
                                pe.sem_inc(slot_used, 1)
                                n += 2

                        u = 0
                        for g in range(3):
                            for t in range(T):
                                project(u, t, t == T - 1)
                                u += 1
                            if g == 0:
                                pe.wait_ge(loaded2, 16 * 10)
                                pe.wait_ge(S["exin"], 1)
                                for j, src in enumerate((ckv[:, 0, 0:P], ckv[:, 0, P:256], ckv[:, 2, 0:P], ckv[:, 2, P:256])):
                                    mm = pe.transpose(PS[:, 4, j * P:(j + 1) * P], src, ident)
                                mm.then_inc(S["ctx_tr"], 1)
                                pe.wait_ge(S["lf_ready"], 1)
                                for t in range(T):
                                    for q in range(4):
                                        mm = pe.transpose(PS[0:4, 5 + t, q * P:(q + 1) * P], gt[:, t, 4 * q:4 * q + 4], ident)
                                    mm.then_inc(S["rows_tr"], 1)
                            if g == 1:
                                pe.wait_ge(S["rows_v"], 1)
                                for q in range(3):
                                    for t in range(T):
                                        for d in range(2):
                                            src = (R[:, t, d, 0, :], R[:, t, d, 1, :], brow[:, t, d, :])[q]
                                            o = (q * 6 + 2 * t + d) * 4
                                            pe.transpose(PS[:, 5, o:o + 4], src, ident[0:4, 0:4])
                                pe.matmul(PS[:, 5, 128:176], ones[0:4, :], sm[0:4, 412:460], start=True, stop=True).then_inc(S["cols_mm"], 1)

                        def scores(i):
                            t, kind = BATCHES[i]
                            for m in (3, 2, 1, 0):
                                q, k = aps_of(BATCHES[i])[m]
                                if m == 0 and i:
                                    pe.wait_ge(S["pv_ev"], i)
                                mm = pe.matmul(PS[:, 2 + m, 0:k.shape[1]], q, k, start=True, stop=True)
                            mm.then_inc(S["sc_mm"], 1)

                        def weigh(i):
                            t, kind = BATCHES[i]
                            nc_ = 1 if t == 0 else 3
                            f = first_map[i]
                            nm_ = n_maps(BATCHES[i])

                            def turn(j):
                                m = f + j
                                if m >= 2:
                                    pe.wait_ge(S["pt_ev"], m - 1)
                                if kind == "na":
                                    pe.wait_ge(S["ex_ready"], 4 * i + j + 1)
                                else:
                                    pe.wait_ge(S["w_ready"], 2 * sum(b[1] != "na" for b in BATCHES[:i]) + j + 1)
                                src = (W2 if kind == "na" else W1)[:, j, :]
                                for c in range(nc_):
                                    mm = pe.transpose(PS[:, 6 + m % 2, c * P:(c + 1) * P], src[:, c * P:(c + 1) * P], ident)
                                mm.then_inc(S["pt_mm"], 1)

                            def product(j):
                                m = f + j
                                if j == 0:
                                    pe.wait_ge(S["ex_ready"], 4 * i + 4)
                                pe.wait_ge(S["pt_ev"], m + 1)
                                for c, val in enumerate(values_of(BATCHES[i], j)):
                                    mm = pe.matmul(PS[:, 2, j * 64:(j + 1) * 64], PT[:, m % 2, c * P:(c + 1) * P], val,
                                                   start=(c == 0), stop=(c == nc_ - 1))
                                mm.then_inc(S["pv_mm"], 1)

                            turn(0)
                            for j in range(nm_):
                                if j + 1 < nm_:
                                    turn(j + 1)
                                product(j)

                        for i, (g, t) in enumerate(UNITS):
                            project(u, t, t == T - 1)
                            u += 1
                            b = i - LATE
                            if b == -1:
                                for t2 in range(T):
                                    pe.wait_ge(S["qk_ready"], t2 + 1)
                                    if t2 == 2:
                                        pe.wait_ge(S["att_ev"], 2)
                                    for j in range(2):
                                        for c in range(4):
                                            at = j * 768 + c * P
                                            mm = pe.transpose(PS[:, 2 + 2 * (t2 % 2) + j, c * P:(c + 1) * P], p[:, t2, at:at + P], ident)
                                    mm.then_inc(S["att_tr"], 1)
                                pe.wait_ge(S["att_ev"], 6)
                                pe.wait_ge(S["ctx_ev"], 4)
                            if 0 <= b < len(BATCHES):
                                weigh(b)
                            if 0 <= b + 1 < len(BATCHES):
                                scores(b + 1)
                        pe.wait_ge(S["pv_ev"], len(BATCHES))
                        pe.wait_ge(S["proj_ev"], 21)
                        for t in range(T):
                            for j in range(2):
                                for h in range(MLH):
                                    src = tok[:, t, 512 + h * P:512 + (h + 1) * P] if j == 0 else p[:, t, 1536 + h * P:1536 + (h + 1) * P]
                                    mm = pe.transpose(PS[:, 2 + 2 * t + j, h * P:(h + 1) * P], src, ident)
                            mm.then_inc(S["mqk_tr"], 1)
                        for t in range(T):
                            pe.wait_ge(S["mqk_ev"], 2 * (t + 1))
                            for h in range(MLH):
                                mm = pe.matmul(PS[:, t, h * P:(h + 1) * P], hT[:, 4 + h, t * P:(t + 1) * P],
                                               hT[:, h, t * P:(t + 1) * P], start=True, stop=True)
                            mm.then_inc(S["st_mm"], 1)

                        def spread(i):
                            t, d = ML_ORDER[i]
                            if i >= 2:
                                pe.wait_ge(S["mb_free"], i - 1)
                            for h in range(MLH):
                                mm = pe.matmul(PS[:, 3 + i % 2, h * P:(h + 1) * P], cst[0:4, C_SEL + h * P:C_SEL + (h + 1) * P],
                                               R[:, t, d, 1, :], start=True, stop=True)
                            mm.then_inc(S["mb_mm"], 1)

                        pe.wait_ge(S["st_ev"], T)
                        spread(0)
                        for i, (t, d) in enumerate(ML_ORDER):
                            if i + 1 < 6:
                                spread(i + 1)
                            if i:
                                pe.wait_ge(S["num_ev"], i)
                            if t:
                                if i >= 4:
                                    pe.wait_ge(S["c_ready"], i - 1)
                                for h in range(MLH):
                                    b = (7, 0)[h // 2]
                                    pe.matmul(PS[:, b, (h % 2) * 129:(h % 2) * 129 + 129], hT[:, h, t * P:(t + 1) * P],
                                              Caug[:, 4 * d + h, :], start=True, stop=True)
                            pe.wait_ge(S["s_ready"], i + 1)
                            for h in range(MLH):
                                mm = pe.matmul(PS[:, 5 + h // 2, (h % 2) * 129:(h % 2) * 129 + 129], num[:, h, 0:P],
                                               vaug[:, t, h, :], start=True, stop=True)
                            mm.then_inc(S["num_mm"], 1)
                            if i < 4:
                                if i:
                                    pe.wait_ge(S["c_ready"], i)
                                pe.wait_ge(S["wk_ready"], i + 1)
                                for h in range(MLH):
                                    mm = pe.matmul(PS[:, 1 + h // 2, (h % 2) * 129:(h % 2) * 129 + 129], wk[:, h * P:(h + 1) * P],
                                                   vaug[:, t, h, :], start=True, stop=True)
                                mm.then_inc(S["upd_mm"], 1)
                        for t in range(T):
                            pe.wait_ge(S["mix_ready"], t + 1)
                            for half in range(2):
                                i = 2 * t + half
                                if i >= 4:
                                    pe.wait_ge(S["hT_s" if half == 0 else "hT_v"], 12 + t - 1)
                                for c in range(4):
                                    k = half * 4 + c
                                    mm = pe.transpose(PS[:, i % 4, c * P:(c + 1) * P], tok[:, t, k * P:(k + 1) * P], ident)
                                mm.then_inc(S["mix_tr"], 1)
                        pe.wait_ge(S["hT_s"], 12 + T)
                        pe.wait_ge(S["hT_v"], 12 + T)
                        for j in range(2):
                            for t in range(T):
                                o = 3 * j + t
                                if o >= 2:
                                    pe.wait_ge(S["x_done"], o - 1)
                                for half in range(2):
                                    s = (n + half) % NSA
                                    pe.wait_ge(landed[s], 16 * ((n + half) // NSA + 1))
                                    for c in range(4):
                                        k = half * 4 + c
                                        mm = pe.matmul(PS[:, 4 + o % 2, :], hT[:, k, t * P:(t + 1) * P],
                                                       ring[:, s, c * 512:(c + 1) * 512], start=(k == 0), stop=(k == 7))
                                mm.then_inc(S["out_mm"], 1)
                            n += 2

                    @block.vector
                    def _(dve):
                        v = Chain(dve, chain_v)
                        norm_dve(dve)
                        dve.wait_ge(loaded, 16 * 11)
                        norm_ev_dve(dve, 0, hT)
                        dve.memset(zrow, 0.0).then_inc(chain_v, 1)
                        v.n += 1
                        dve.memset(vaug[:, :, :, MLD], 1.0).then_inc(chain_v, 1)
                        v.n += 1
                        dve.wait_ge(S["tail_mm"], 1)
                        v(dve.tensor_tensor(gt, PS[:, 4, 0:48].rearrange("p (t g) -> p t g", t=T),
                                            prm[:, None, B_GB:B_GB + 16].to_broadcast([P, T, 16]), ALU.add))
                        f = gt.rearrange("p t (d k h) -> p t d k h", d=2, k=2)[:, :, :, 1, :]
                        dve.scalar_tensor_tensor(e1, f, -1.0, f, ALU.mult, ALU.max).then_inc(S["exin"], 1)
                        v(dve.tensor_scalar(e2, f, 0.0, None, ALU.min))
                        dve.wait_ge(S["exout"], 1)
                        dve.tensor_tensor(f, e2, e1, ALU.subtract).then_inc(S["lf_ready"], 1)
                        lam = prm[:, B_LAM:B_LAM + 128].rearrange("p (a b d) -> p a b d", a=2, b=2)
                        v(dve.tensor_tensor(lam[:, :, 0, :], lam[:, :, 0, :], lam[:, :, 1, :], ALU.mult))
                        v(dve.tensor_reduce(lamt[:, 0:2], lam[:, :, 0, :], AX.X, ALU.add))
                        v(dve.tensor_copy(small[:, 102:104], cst[:, bass.ds(C_LAM + 2 * l, 2)]))
                        v(dve.tensor_scalar(prm[:, B_SUB:B_SUB + 64], prm[:, B_SUB:B_SUB + 64], small[:, 103:104], None, ALU.mult))
                        for t in range(T):
                            dve.wait_ge(S["rows_tr"], t + 1)
                            v(dve.tensor_copy(R[:, t].rearrange("p d k n -> p (d k n)"), PS[0:4, 5 + t, :]))
                        v(dve.memset(scal, 0.0))
                        v(dve.tensor_copy(scal[:, 2, 0:1], m0[:, 0:1]))
                        v(dve.tensor_copy(scal[:, 5, 0:1], m0[:, 1:2]))
                        for t, d in ML_ORDER:
                            td, e = 2 * t + d, last(d)
                            way = slice(None, None, -1) if d else slice(None)
                            i_, f_, b_ = R[:, t, d, 0, :], R[:, t, d, 1, :], brow[:, t, d, :]
                            v(dve.tensor_tensor_scan(b_[:, way], ones[0:4, :], f_[:, way], 0.0, ALU.mult, ALU.add))
                            v(dve.tensor_tensor(i_, i_, b_, ALU.subtract))
                            v(dve.tensor_tensor_scan(f_[:, way], zrow, i_[:, way], scal[:, td, 0:1], ALU.add, ALU.max))
                            v(dve.tensor_copy(scal[:, td, 1:2], f_[:, e:e + 1]))
                            follow = {(0, 0): mout[:, 0:1], (0, 1): mout[:, 1:2], (1, 0): scal[:, 4, 0:1],
                                      (2, 1): scal[:, 3, 0:1]}.get((t, d))
                            if follow is not None:
                                v(dve.tensor_tensor(follow, b_[:, e:e + 1], f_[:, e:e + 1], ALU.add))
                        dve.tensor_tensor(diag, sm[0:4, 400:412, None].to_broadcast([4, 12, 4]),
                                          cst[0:4, None, C_ID:C_ID + 4].to_broadcast([4, 12, 4]), ALU.mult).then_inc(S["rows_v"], 1)
                        dve.wait_ge(S["cols_mm"], 1)
                        v(dve.tensor_copy(sm[:, 96:168], PS[:, 5, 0:72]))
                        v(dve.tensor_copy(sm[:, 168:216], PS[:, 5, 128:176]))
                        dve.wait_ge(S["sq_ready"], 6)
                        v(dve.tensor_reduce(ms[:, 0:24], nq.rearrange("p (g d) -> p g d", d=NAD), AX.X, ALU.add))
                        v(dve.tensor_reduce(ms[:, 24:72], dq.rearrange("p (g d) -> p g d", d=DFD), AX.X, ALU.add))
                        v(dve.tensor_scalar(ms[:, 0:24], ms[:, 0:24], 1.0 / NAD, EPS, ALU.mult, ALU.add))
                        dve.tensor_scalar(ms[:, 24:72], ms[:, 24:72], 1.0 / DFD, EPS, ALU.mult, ALU.add).then_inc(S["ms_ready"], 1)
                        bv = bias[:, :, :, :].rearrange("p t h (j k) -> p (t h j) k", k=64)
                        dve.wait_ge(loaded2, 16 * 10)
                        v(dve.tensor_tensor(bv, bv, cst[:, None, C_COL:C_COL + 64].to_broadcast([P, 32, 64]), ALU.add))
                        dve.wait_ge(S["r_ready"], 1)
                        for t in range(T):
                            na = p[:, t, 0:512].rearrange("p (g d) -> p g d", d=NAD)
                            v(dve.tensor_tensor(na, na, ms[:, 8 * t:8 * t + 8, None].to_broadcast([P, 8, NAD]), ALU.mult))
                            na = p[:, t, 0:512].rearrange("p (a h d) -> p a h d", a=2, h=4)
                            gn_ = prm[:, B_NAG:B_NAG + 128].rearrange("p (a d) -> p a d", a=2)
                            v(dve.tensor_tensor(na, na, gn_[:, :, None, :].to_broadcast([P, 2, 4, NAD]), ALU.mult))
                            df = p[:, t, 768:1280].rearrange("p (g d) -> p g d", d=DFD)
                            v(dve.tensor_tensor(df, df, ms[:, 24 + 16 * t:40 + 16 * t, None].to_broadcast([P, 16, DFD]), ALU.mult))
                            df = p[:, t, 768:1280].rearrange("p (a h d) -> p a h d", a=2, h=8)
                            gd = prm[:, B_DFG:B_DFG + 64].rearrange("p (a d) -> p a d", a=2)
                            ins = dve.tensor_tensor(df, df, gd[:, :, None, :].to_broadcast([P, 2, 8, DFD]), ALU.mult)
                            if t == 0:
                                ins.then_inc(S["qk_ready"], 1)
                                continue
                            v(ins)
                            co, si = C_COS + (t - 1) * DFD, C_SIN + (t - 1) * DFD
                            xr = p[:, t, 768:1280].rearrange("p (g r s f) -> p g r s f", r=2, s=2, f=8)
                            yr = wkr = tmp.rearrange("p a b -> p (a b)")[:, 0:512].rearrange("p (g r s f) -> p g r s f", r=2, s=2, f=8)
                            for s_ in range(2):
                                sn = cst[:, si:si + DFD].rearrange("p (r s f) -> p r s f", r=2, s=2)[:, None, :, s_, :]
                                v(dve.tensor_tensor(yr[:, :, :, s_, :], xr[:, :, :, 1 - s_, :], sn.to_broadcast([P, 16, 2, 8]), ALU.mult))
                            df = p[:, t, 768:1280].rearrange("p (g d) -> p g d", d=DFD)
                            v(dve.tensor_tensor(df, df, cst[:, None, co:co + DFD].to_broadcast([P, 16, DFD]), ALU.mult))
                            dve.tensor_tensor(p[:, t, 768:1280], p[:, t, 768:1280], tmp.rearrange("p a b -> p (a b)")[:, 0:512],
                                              ALU.add).then_inc(S["qk_ready"], 1)
                        mprev, mlast = bcs[:, :, 0, :], bcs[:, :, 1, :]
                        c3 = cols.rearrange("p q (n h) -> p q n h", h=4)
                        g3 = arg.rearrange("p q (n h) -> p q n h", h=4)
                        v(dve.scalar_tensor_tensor(arg[:, 0, :], cols[:, 2, :], -1.0, cols[:, 1, :], ALU.mult, ALU.subtract))
                        v(dve.tensor_tensor(g3[:, 1], mprev, c3[:, 1], ALU.subtract))
                        v(dve.tensor_tensor(g3[:, 2], c3[:, 0], mlast, ALU.subtract))
                        dve.tensor_tensor(g3[:, 3], mprev, mlast, ALU.subtract).then_inc(S["exin"], 1)
                        dve.wait_ge(S["exout"], 2)
                        v(dve.tensor_scalar(arg[:, 2, :], arg[:, 2, :], MLD ** -0.5, None, ALU.mult))
                        dve.sem_inc(S["exin"], 1)
                        dve.wait_ge(S["exout"], 3)
                        v(dve.tensor_tensor(lamt[:, 0:1], lamt[:, 3:4], lamt[:, 2:3], ALU.subtract))
                        v(dve.tensor_tensor(nlam, lamt[:, 0:1], small[:, 102:103], ALU.subtract))

                        def reduce_scores(i):
                            t, kind = BATCHES[i]
                            nk = keys_of(t)[1] - keys_of(t)[0]
                            dve.wait_ge(S["sc_mm"], i + 1)
                            if kind == "na":
                                if t:
                                    v(dve.scalar_tensor_tensor(W1[:, :, 0:256], PS[:, 2:6, 0:256], NAD ** -0.5, bias[:, t - 1], ALU.mult, ALU.add))
                                    v(dve.tensor_scalar(W1[:, :, 256:384], PS[:, 2:6, 256:384], NAD ** -0.5, None, ALU.mult))
                                else:
                                    v(dve.tensor_scalar(W1[:, :, 0:P], PS[:, 2:6, 0:P], NAD ** -0.5, None, ALU.mult))
                                dve.tensor_reduce(nm, W1[:, :, 0:nk], AX.X, ALU.max, negate=True).then_inc(S["nm_ready"], 1)
                            else:
                                v(dve.tensor_reduce(nm, PS[:, 2:6, 0:nk], AX.X, ALU.max, negate=True))
                                dve.tensor_scalar(nm, nm, DFD ** -0.5, None, ALU.mult).then_inc(S["nm_ready"], 1)

                        def combine(i):
                            t, kind = BATCHES[i]
                            nk = keys_of(t)[1] - keys_of(t)[0]
                            dve.wait_ge(S["ex_ready"], 4 * i + 4)
                            v(dve.reciprocal(rr, rs))
                            if kind == "na":
                                return
                            odd = rr.rearrange("p (h a) -> p h a", a=2)[:, :, 1]
                            v(dve.tensor_scalar(odd, odd, nlam, None, ALU.mult))
                            for j in range(2):
                                v(dve.tensor_scalar(W2[:, 2 * j + 1, 0:nk], W2[:, 2 * j + 1, 0:nk], rr[:, 2 * j + 1:2 * j + 2], None, ALU.mult))
                                dve.scalar_tensor_tensor(W1[:, j, 0:nk], W2[:, 2 * j, 0:nk], rr[:, 2 * j:2 * j + 1],
                                                         W2[:, 2 * j + 1, 0:nk], ALU.mult, ALU.add).then_inc(S["w_ready"], 1)

                        def outputs(i):
                            t, kind = BATCHES[i]
                            dve.wait_ge(S["pv_mm"], first_map[i + 1])
                            if kind == "na":
                                dve.tensor_tensor(tok[:, t, 0:256].rearrange("p (h d) -> p h d", h=4),
                                                  PS[:, 2, 0:256].rearrange("p (h d) -> p h d", h=4),
                                                  rr[:, :, None].to_broadcast([P, 4, 64]), ALU.mult).then_inc(S["pv_ev"], 1)
                            else:
                                at = 256 + 128 * int(kind[2])
                                dve.tensor_copy(tok[:, t, at:at + 128], PS[:, 2, 0:128]).then_inc(S["pv_ev"], 1)

                        for i in range(len(BATCHES)):
                            reduce_scores(i)
                            combine(i)
                            outputs(i)
                        dve.wait_ge(S["pv_ev"], len(BATCHES))
                        do = tok[:, :, 256:512].rearrange("p t (h d) -> p t h d", h=4)
                        sq = nq[:, 0:768].rearrange("p (t h d) -> p t h d", t=T, h=4)
                        v(dve.tensor_tensor(sq, do, do, ALU.mult))
                        v(dve.tensor_reduce(ms2, nq[:, 0:768].rearrange("p (g d) -> p g d", d=64), AX.X, ALU.add))
                        dve.tensor_scalar(ms2, ms2, 1.0 / DFV, EPS, ALU.mult, ALU.add).then_inc(S["ms_ready"], 1)
                        dve.wait_ge(S["r_ready"], 2)
                        v(dve.tensor_tensor(do, do, ms2.rearrange("p (t h) -> p t h", t=T)[:, :, :, None].to_broadcast([P, T, 4, 64]), ALU.mult))
                        do12 = [tok[:, t, 256:512].rearrange("p (h d) -> p h d", h=4) for t in range(T)]
                        for t in range(T):
                            v(dve.tensor_tensor(do12[t], do12[t], prm[:, None, B_SUB:B_SUB + 64].to_broadcast([P, 4, 64]), ALU.mult))
                        seen = set()
                        two = lambda b0, n=129: PS[:, b0:b0 + 2, 0:258].rearrange("p b (h e) -> p b h e", h=2)
                        n4 = num[:, :, :].rearrange("p (b h) e -> p b h e", b=2)
                        t4 = tmp[:, :, :].rearrange("p (b h) e -> p b h e", b=2)

                        def b4(ap):
                            return ap.rearrange("p (b h) -> p b h", b=2)[:, :, :, None].to_broadcast([P, 2, 2, 129])

                        for i, (t, d) in enumerate(ML_ORDER):
                            td = 2 * t + d
                            dve.wait_ge(S["mb_mm"], i + 1)
                            X = tmp[:, :, 0:P]
                            v(dve.tensor_tensor(X, PS[:, 3 + i % 2, :].rearrange("p (h n) -> p h n", h=4),
                                                col4(0, td)[:, :, None].to_broadcast([P, 4, P]), ALU.subtract))
                            dve.sem_inc(S["mb_free"], 1)
                            mask = C_MF if d == 0 else C_MB
                            dve.tensor_tensor(X, X, cst[:, None, mask:mask + P].to_broadcast([P, 4, P]), ALU.max).then_inc(S["d_ready"], 1)
                            if i < 4:
                                if i:
                                    dve.wait_ge(S["upd_mm"], i)
                                dve.tensor_tensor(wk[:, :].rearrange("p (h n) -> p h n", h=4),
                                                  p[:, t, 1536:2048].rearrange("p (h n) -> p h n", h=4),
                                                  arg4(2, td)[:, :, None].to_broadcast([P, 4, P]), ALU.mult).then_inc(S["wk_ready"], 1)
                            dve.wait_ge(S["e_ready"], i + 1)
                            dve.wait_ge(S["st_ev"], T)
                            dve.tensor_tensor(num[:, :, 0:P], X, ST[:, t, :].rearrange("p (h n) -> p h n", h=4), ALU.mult).then_inc(S["s_ready"], 1)
                            dve.wait_ge(S["num_mm"], i + 1)
                            if t:
                                for b, bank in enumerate((7, 0)):
                                    v(dve.tensor_tensor(t4[:, b], PS[:, bank, 0:258].rearrange("p (h e) -> p h e", h=2),
                                                        arg4(1, td)[:, 2 * b:2 * b + 2, None].to_broadcast([P, 2, 129]), ALU.mult))
                                v(dve.tensor_tensor(n4, two(5), t4, ALU.add))
                            else:
                                v(dve.tensor_copy(n4, two(5)))
                            dve.sem_inc(S["num_ev"], 1)
                            v(dve.scalar_tensor_tensor(den, num[:, :, MLD], -1.0, num[:, :, MLD], ALU.mult, ALU.max))
                            v(dve.tensor_tensor(den, den, arg4(0, td), ALU.max))
                            v(dve.reciprocal(den, den))
                            out = mlh[:, t, :].rearrange("p (h n) -> p h n", h=4)
                            r4 = den[:, :, None].to_broadcast([P, 4, P])
                            if t in seen:
                                v(dve.tensor_tensor(num[:, :, 0:P], num[:, :, 0:P], r4, ALU.mult))
                                ins = v(dve.tensor_tensor(out, out, num[:, :, 0:P], ALU.add))
                            else:
                                v(dve.tensor_tensor(out, num[:, :, 0:P], r4, ALU.mult))
                            seen.add(t)
                            if i < 4:
                                dve.wait_ge(S["upd_mm"], i + 1)
                                if t == 0:
                                    dve.tensor_copy(Cp[:, 4 * d:4 * d + 4, :].rearrange("p (b h) e -> p b h e", b=2), two(1)).then_inc(S["c_ready"], 1)
                                else:
                                    C4 = Caug[:, 4 * d:4 * d + 4, :].rearrange("p (b h) e -> p b h e", b=2)
                                    v(dve.tensor_tensor(C4, C4, b4(arg4(3, td)), ALU.mult))
                                    dve.tensor_tensor(C4, C4, two(1), ALU.add).then_inc(S["c_ready"], 1)
                        dve.sem_inc(S["ml_done"], 1)
                        dve.wait_ge(S["sq_ready"], 7)
                        v(dve.tensor_reduce(ms2, nq.rearrange("p (g d) -> p g d", d=MLD), AX.X, ALU.add))
                        dve.tensor_scalar(ms2, ms2, 1.0 / MLD, EPS, ALU.mult, ALU.add).then_inc(S["ms_ready"], 1)
                        dve.wait_ge(S["sig_e"], 1)
                        v(dve.tensor_scalar(dq, dq, 1.0, None, ALU.add))
                        v(dve.reciprocal(dq, dq))
                        dve.wait_ge(S["r_ready"], 3)
                        for t in range(T):
                            hv = mlh[:, t, :].rearrange("p (h n) -> p h n", h=4)
                            v(dve.tensor_tensor(hv, hv, ms2[:, 4 * t:4 * t + 4, None].to_broadcast([P, 4, P]), ALU.mult))
                            v(dve.tensor_tensor(hv, hv, prm[:, None, B_OUT:B_OUT + P].to_broadcast([P, 4, P]), ALU.mult))
                            dve.tensor_tensor(tok[:, t, 512:1024], mlh[:, t, :], dq[:, t * 512:(t + 1) * 512], ALU.mult).then_inc(S["mix_ready"], 1)
                        for t in range(T):
                            dve.wait_ge(S["mix_tr"], 2 * t + 2)
                            dve.tensor_copy(hT[:, 4:8, t * P:(t + 1) * P],
                                            PS[:, (2 * t + 1) % 4, :].rearrange("p (c n) -> p c n", c=4)).then_inc(S["hT_v"], 1)
                        for j in range(2):
                            for t in range(T):
                                o = 3 * j + t
                                dve.wait_ge(S["out_mm"], o + 1)
                                if o:
                                    dve.wait_ge(S["x_done"], o)
                                v(dve.tensor_tensor(wk[:, :], PS[:, 4 + o % 2, :], gate[:, min(t, 1), j * 512:(j + 1) * 512], ALU.mult))
                                xs = x[:, t, j * 512:(j + 1) * 512]
                                dve.tensor_tensor(xs, xs, wk[:, :], ALU.add).then_inc(S["x_done"], 1)
                        dve.wait_ge(S["x_done"], 6)
                end_section()
            if debug == "mix":
                with nc.Block() as block:
                    @block.sync
                    def _(sp):
                        sp.dma_start(O["dbg"].rearrange("(t p) d -> p t d", p=P), x[:, :, :]).then_inc(stored, 16)
                        sp.wait_ge(stored, 16)
                end_section()
                continue_ = None
            with ExitStack() as layer:
                acc = sb("acc", [P, T, D], ctx=layer)
                tokh = sb("tokh", [P, T, D], ctx=layer)
                tokl = sb("tokl", [P, T, D], ctx=layer)
                posm = sb("posm", [P, T, NE + 2], ctx=layer)
                wts = sb("wts", [P, T, NE + 2], ctx=layer)

                with ExitStack() as sec:
                    tok = sb("tokB", [P, T, D], ctx=sec)
                    ring = sb("ringB", [P, 3, SLOTF], ctx=sec)
                    hT = sb("hTB", [P, KC, T * P], ctx=sec)
                    wr = sb("wr", [P, KC, NE], ctx=sec)
                    sg = sb("sg", [P, 2, DE], ctx=sec)
                    hid = sb("hid", [P, DE], ctx=sec)
                    hidT = sb("hidT", [P, 2, P], ctx=sec)
                    rt = sb("rt", [P, 8, T, NE], ctx=sec)
                    r8 = sb("r8", [P, T, 8], ctx=sec)
                    rem = sb("rem", [P, 8], ctx=sec)
                    s_, sel, gtm, eq, cum, mask = (rt[:, i] for i in range(6))

                    with nc.Block() as block:
                        @block.sync
                        def _(sp):
                            sp.dma_start(wr[:, :, :], A["w_router"][l].rearrange("(c p) n -> p c n", p=P)).then_inc(loaded, 16)
                            for half in range(2):
                                rows = slice(half * 512, (half + 1) * 512)
                                dst = ring[:, half, :].rearrange("p (c w n) -> p c w n", c=4, w=2)
                                for w in range(2):
                                    sp.dma_start(dst[:, :, w, :], A[("w_sh1", "w_sh3")[w]][l, rows, :]
                                                 .rearrange("(c p) n -> p c n", p=P)).then_inc(landed[half], 16)
                            sp.dma_start(ring[:, 2, :].rearrange("p (c n) -> p c n", c=2),
                                         A["w_sh2"][l].rearrange("(c p) n -> p c n", p=P)).then_inc(landed[2], 16)
                            for i in range(2):
                                sp.dma_start(gate[:, i, :], bcast(modd[l, i, 5 * D:6 * D], D)).then_inc(loaded2, 16)
                            sp.wait_ge(loaded2, 32)

                        @block.gpsimd
                        def _(pool):
                            norm_pool(pool, Chain(pool, chain_p))

                        @block.scalar
                        def _(act):
                            norm_act(act, 1)
                            norm_ev_act(act, 1, hT)
                            act.wait_ge(S["rt_mm"], 1)
                            act.activation(s_.rearrange("p t e -> p (t e)"), PS[:, 0, 0:T * NE], ACT.Exp, scale=-1.0).then_inc(S["rt_e"], 1)
                            for t in range(T):
                                act.wait_ge(S["sh_mm"], t + 1)
                                act.activation(sg[:, t % 2, :], PS[:, 2 + t % 2, 0:DE], ACT.Silu).then_inc(S["sh_silu"], 1)
                                act.wait_ge(S["sh_tr"], t + 1)
                                act.activation(hidT[:, :, :].rearrange("p a b -> p (a b)"), PS[:, 4, 0:256], ACT.Copy).then_inc(S["sh_trev"], 1)

                        @block.tensor
                        def _(pe):
                            norm_pe(pe)
                            pe.wait_ge(S["hT_s"], 4 * T)
                            pe.wait_ge(S["hT_v"], 4 * T)
                            pe.wait_ge(loaded, 16)
                            for t in range(T):
                                for k in range(KC):
                                    mm = pe.matmul(PS[:, 0, t * NE:(t + 1) * NE], hT[:, k, t * P:(t + 1) * P], wr[:, k, :],
                                                   start=(k == 0), stop=(k == KC - 1))
                            mm.then_inc(S["rt_mm"], 1)
                            for t in range(T):
                                for half in range(2):
                                    i = 2 * t + half
                                    if i >= 4:
                                        pe.wait_ge(S["back_ev"], i - 3)
                                    for c in range(4):
                                        mm = pe.transpose(PS[:, 4 + i % 4, c * P:(c + 1) * P], hT[:, 4 * half + c, t * P:(t + 1) * P], ident)
                                    mm.then_inc(S["back_tr"], 1)
                            def up(t):
                                if t >= 2:
                                    pe.wait_ge(S["sh_hid"], t - 1)
                                for half in range(2):
                                    pe.wait_ge(landed[half], 32)
                                    for c in range(4):
                                        k = 4 * half + c
                                        mm = pe.matmul(PS[:, 2 + t % 2, :], hT[:, k, t * P:(t + 1) * P], ring[:, half, c * 512:(c + 1) * 512],
                                                       start=(k == 0), stop=(k == 7))
                                mm.then_inc(S["sh_mm"], 1)

                            up(0)
                            pe.wait_ge(S["back_ev"], 2 * T)
                            pe.wait_ge(landed[2], 16)
                            for t in range(T):
                                if t + 1 < T:
                                    up(t + 1)
                                if t == 0:
                                    pe.wait_ge(S["mask_ready"], 1)
                                    for u in range(T):
                                        for w in range(u + 1):
                                            lhs = cst[:, C_TRIU:C_TRIU + P] if w == u else ones
                                            pe.matmul(PS[:, 1, u * NE:(u + 1) * NE], lhs, mask[:, w, :], start=(w == 0), stop=(w == u))
                                    for w in range(T):
                                        mm = pe.matmul(PS[:, 1, T * NE:(T + 1) * NE], ones, mask[:, w, :], start=(w == 0), stop=(w == T - 1))
                                    mm.then_inc(S["pos_mm"], 1)
                                pe.wait_ge(S["sh_hid"], t + 1)
                                for f in range(2):
                                    mm = pe.transpose(PS[:, 4, f * P:(f + 1) * P], hid[:, f * P:(f + 1) * P], ident)
                                mm.then_inc(S["sh_tr"], 1)
                                pe.wait_ge(S["sh_trev"], t + 1)
                                if t:
                                    pe.wait_ge(S["sh_done"], t)
                                for half in range(2):
                                    for f in range(2):
                                        mm = pe.matmul(PS[:, 5 + half, :], hidT[:, f, :], ring[:, 2, f * D + half * 512:f * D + (half + 1) * 512],
                                                       start=(f == 0), stop=(f == 1))
                                mm.then_inc(S["sh_down"], 1)

                        @block.vector
                        def _(dve):
                            v = Chain(dve, chain_v)
                            norm_dve(dve)
                            norm_ev_dve(dve, 1, hT)
                            for t in range(T):
                                for half in range(2):
                                    i = 2 * t + half
                                    at = slice(half * 512, (half + 1) * 512)
                                    dve.wait_ge(S["back_tr"], i + 1)
                                    v(round_high(dve, tokh[:, t, at], PS[:, 4 + i % 4, :]))
                                    dve.tensor_tensor(hi(tokl[:, t, at]), PS[:, 4 + i % 4, :], tokh[:, t, at], ALU.subtract).then_inc(S["back_ev"], 1)
                            dve.wait_ge(S["rt_e"], 1)
                            v(dve.tensor_scalar(s_, s_, 1.0, None, ALU.add))
                            v(dve.reciprocal(s_, s_))
                            v(dve.tensor_tensor(sel, s_, prm[:, None, B_BR:B_BR + NE].to_broadcast([P, T, NE]), ALU.add))
                            for t in range(T):
                                v(dve.max(r8[:, t, :], sel[:, t, :]))
                            thr = r8[:, :, TOPK - 1:TOPK].to_broadcast([P, T, NE])
                            v(dve.tensor_tensor(gtm, sel, thr, ALU.is_gt))
                            v(dve.tensor_tensor(eq, sel, thr, ALU.is_equal))
                            v(dve.tensor_reduce(rem[:, 0:T], gtm, AX.X, ALU.add))
                            v(dve.tensor_scalar(rem[:, 0:T], rem[:, 0:T], -1.0, float(TOPK), ALU.mult, ALU.add))
                            for t in range(T):
                                v(dve.tensor_tensor_scan(cum[:, t, :], ones[:, 0:NE], eq[:, t, :], 0.0, ALU.mult, ALU.add))
                            v(dve.tensor_tensor(cum, cum, rem[:, 0:T, None].to_broadcast([P, T, NE]), ALU.is_le))
                            v(dve.tensor_tensor(eq, eq, cum, ALU.mult))
                            dve.tensor_tensor(mask, gtm, eq, ALU.add).then_inc(S["mask_ready"], 1)
                            dve.wait_ge(S["mask_ready"], 1)
                            v(dve.memset(wts[:, :, :], 0.0))
                            v(dve.memset(posm[:, :, :], -1.0))
                            v(dve.tensor_tensor(s_, s_, mask, ALU.mult))
                            v(dve.tensor_reduce(rem[:, 0:T], s_, AX.X, ALU.add))
                            v(dve.reciprocal(rem[:, 0:T], rem[:, 0:T]))
                            v(dve.tensor_scalar(rem[:, 0:T], rem[:, 0:T], ROUTED_SCALE, None, ALU.mult))
                            v(dve.tensor_tensor(wts[:, :, 0:NE], s_, rem[:, 0:T, None].to_broadcast([P, T, NE]), ALU.mult))

                            def gated(t):
                                dve.wait_ge(S["sh_silu"], t + 1)
                                if t:
                                    dve.wait_ge(S["sh_tr"], t)
                                dve.tensor_tensor(hid[:, :], PS[:, 2 + t % 2, 256:512], sg[:, t % 2, :], ALU.mult).then_inc(S["sh_hid"], 1)

                            for t in range(T):
                                if t == 0:
                                    dve.wait_ge(S["pos_mm"], 1)
                                    pos = PS[:, 1, 0:T * NE].rearrange("p (t e) -> p t e", t=T)
                                    v(dve.scalar_tensor_tensor(posm[:, :, 0:NE], pos, 1.0, mask, ALU.add, ALU.mult))
                                    v(dve.tensor_scalar(posm[:, :, 0:NE], posm[:, :, 0:NE], -1.0, None, ALU.add))
                                    v(dve.tensor_reduce(rem[:, 4:5], PS[:, 1, T * NE:(T + 1) * NE], AX.X, ALU.max))
                                    v(dve.tensor_scalar(rem[:, 5:6], rem[:, 4:5], float(SLOTS), 1.0, ALU.is_gt, ALU.add))
                                    v(dve.tensor_scalar(rem[:, 6:7], rem[:, 4:5], 2.0 * SLOTS, None, ALU.is_gt))
                                    v(dve.tensor_tensor(npass[:, :], rem[:, 5:6], rem[:, 6:7], ALU.add))
                                gated(t)
                                dve.wait_ge(S["sh_down"], t + 1)
                                dve.tensor_copy(acc[:, t, :].rearrange("p (b n) -> p b n", b=2), PS[:, 5:7, :]).then_inc(S["sh_done"], 1)
                            dve.wait_ge(S["sh_done"], T)
                    end_section()

                passes = nc.values_load(npass[0:1, 0:1], min_val=1, max_val=T)
                with ExitStack() as sec:
                    NR = 4
                    ring = sb("ringC", [P, NR, SLOTF], ctx=sec)
                    high = sb("high", [P, 3, SLOTF], ctx=sec)
                    low = sb("low", [P, 3, SLOTF], ctx=sec)
                    Pb = sb("Pb", [P, 2, T, SLOTS], ctx=sec)
                    PTb = sb("PTb", [P, GROUP, T * P], ctx=sec)
                    hTe = sb("hTe", [P, 2, KC, SLOTS], ctx=sec)
                    gs = sb("gs", [P, 2], ctx=sec)
                    sg = sb("sgC", [P, DE], ctx=sec)
                    hid = sb("hidC", [P, DE], ctx=sec)
                    hidT = sb("hidTC", [P, 2, 2, P], ctx=sec)
                    yh = sb("yh", [P, GROUP, D], ctx=sec)
                    yl = sb("yl", [P, GROUP, D], ctx=sec)
                    NG = NE // GROUP
                    GS = 3 * GROUP
                    wcol = lambda c: bass.ds(c, 1)
                    CV, CP = 3, 1
                    loads = lambda s: 16 * sum(2 if i % 3 < 2 else 1 for i in range(s % NR, s + 1, NR))
                    loads_group = lambda s: loads(s % NR + GS - NR)

                    def cut_done(eng, g, s):
                        e, k = GROUP * g + s // 3, s % 3
                        if k == 1:
                            eng.wait_ge(S["low_p"], e + 1 + CP)
                        else:
                            eng.wait_ge(S["low_v"], 2 * e + (1 if k == 0 else 2) + CV)

                    with nc.Fori(0, passes) as _pass:
                        with nc.Block() as block:

                            @block.sync
                            def _(sp):
                                with sp.Fori(0, NG) as g:
                                    for j in range(GROUP):
                                        for k in range(3):
                                            s = 3 * j + k
                                            r = s % NR
                                            cut_done(sp, g, s - NR)
                                            e = GROUP * g + j
                                            if k < 2:
                                                rows = slice(k * 512, (k + 1) * 512)
                                                dst = ring[:, r, :].rearrange("p (c w n) -> p c w n", c=4, w=2)
                                                for w in range(2):
                                                    sp.dma_start(dst[:, :, w, :], A[("w_exp1", "w_exp3")[w]][l, e, rows, :]
                                                                 .rearrange("(c p) n -> p c n", p=P)).then_inc(landed[r], 16)
                                            else:
                                                sp.dma_start(ring[:, r, :].rearrange("p (c n) -> p c n", c=2),
                                                             A["w_exp2"][l, e].rearrange("(c p) n -> p c n", p=P)).then_inc(landed[r], 16)

                            @block.gpsimd
                            def _(pool):
                                def rest(e, s):
                                    pool.wait_ge(S["cut_p"], e + 1)
                                    pool.tensor_tensor(hi(low[:, 1, :]), ring[:, s % NR, :], high[:, 1, :], ALU.subtract).then_inc(S["low_p"], 1)

                                def step(g, last=False):
                                    for j in range(GROUP):
                                        e = GROUP * g + j
                                        if not (last and j == GROUP - 1):
                                            rest(e + 1, 3 * j + 4)

                                pool.sem_inc(S["low_p"], CP)
                                rest(0, 1)
                                with pool.Fori(0, NG - 1) as g:
                                    step(g)
                                step(NG - 1, last=True)

                            @block.scalar
                            def _(act):
                                def take(quad, n):
                                    act.wait_ge(S["ga_mm"], n)
                                    for part in range(2):
                                        act.activation(hi(hTe[:, part, 4 * quad:4 * quad + 4, :].rearrange("p c n -> p (c n)")),
                                                       PS[:, part, :], ACT.Copy).then_inc(S["he_ev"], 1)

                                def step(g, last=False):
                                    for j in range(GROUP):
                                        e = GROUP * g + j
                                        more = not (last and j == GROUP - 1)
                                        act.wait_ge(slot_used, 3 * e + 5)
                                        act.activation(sg[:, :], PS[:, 2, 0:DE], ACT.Silu).then_inc(S["silu"], 1)
                                        if more:
                                            take(0, 2 * e + 3)
                                        act.wait_ge(S["ht_mm"], e + 1)
                                        act.activation(hi(hidT[:, 0, :, :].rearrange("p b n -> p (b n)")), PS[:, 3, 0:DE], ACT.Copy).then_inc(S["ht_ev"], 1)
                                        act.wait_ge(S["pt_mm"], e + 1)
                                        act.activation(hi(PTb[:, j, :]), PS[:, 4, 0:T * P], ACT.Copy).then_inc(S["pt_ev"], 1)
                                        act.wait_ge(slot_used, 3 * e + 6)
                                        act.activation(hi(yh[:, j, :].rearrange("p (b n) -> p b n", b=2)), PS[:, 5:7, :], ACT.Copy).then_inc(S["y_high"], 1)
                                        if more:
                                            take(1, 2 * e + 4)

                                take(0, 1)
                                take(1, 2)
                                with act.Fori(0, NG - 1) as g:
                                    step(g)
                                step(NG - 1, last=True)

                            @block.tensor
                            def _(pe):
                                pe.sem_inc(slot_used, 3)

                                def gather(quad, b):
                                    for part, src in enumerate((tokh, tokl)):
                                        for kk in range(4):
                                            k = 4 * quad + kk
                                            for c in range(T):
                                                mm = pe.matmul(PS[:, part, kk * P:(kk + 1) * P], hi(src[:, c, k * P:(k + 1) * P]),
                                                               hi(Pb[:, b, c, :]), start=(c == 0), stop=(c == T - 1))
                                    mm.then_inc(S["ga_mm"], 1)

                                def slot_weights(b, e):
                                    for c in range(T):
                                        mm = pe.matmul(PS[:, 7, 0:1], Pb[:, b, c, :], wts[:, c, wcol(e)], start=(c == 0), stop=(c == T - 1))
                                    mm.then_inc(S["gs_mm"], 1)

                                def three(out, ah, al, wh, wl, first, last):
                                    pe.matmul(out, hi(ah), hi(wh), start=first, stop=False)
                                    pe.matmul(out, hi(ah), hi(wl), start=False, stop=False)
                                    return pe.matmul(out, hi(al), hi(wh), start=False, stop=last)

                                def step(g, last=False):
                                    for j in range(GROUP):
                                        e = GROUP * g + j
                                        b = j % 2
                                        more = not (last and j == GROUP - 1)
                                        for half in range(2):
                                            pe.wait_ge(S["he_ev"], 4 * e + 2 + 2 * half)
                                            cut_done(pe, g, 3 * j + half)
                                            for c in range(4):
                                                k = 4 * half + c
                                                w = slice(c * 512, (c + 1) * 512)
                                                mm = three(PS[:, 2, :], hTe[:, 0, k, :], hTe[:, 1, k, :], high[:, half, w],
                                                           low[:, half, w], k == 0, k == 7)
                                            mm.then_inc(slot_used, 1)
                                        if more:
                                            pe.wait_ge(S["pb_ready"], e + 2)
                                            gather(0, 1 - b)
                                            if j == 0:
                                                pe.wait_ge(S["sc_ev"], 6 * g + 1)
                                            pe.wait_ge(S["gs_ev"], e + 1)
                                            slot_weights(1 - b, e + 1)
                                        pe.wait_ge(S["hid_ready"], e + 1)
                                        for f in range(2):
                                            mm = pe.transpose(PS[:, 3, f * P:(f + 1) * P], hid[:, f * P:(f + 1) * P], ident)
                                        mm.then_inc(S["ht_mm"], 1)
                                        pe.wait_ge(S["pt_ev"], e + 1)
                                        for c in range(T):
                                            mm = pe.transpose(PS[:, 4, c * P:(c + 1) * P], Pb[:, b, c, :], ident)
                                        mm.then_inc(S["pt_mm"], 1)
                                        pe.wait_ge(S["hidT_low"], e + 1)
                                        pe.wait_ge(S["y_low"], e + 1)
                                        cut_done(pe, g, 3 * j + 2)
                                        for half in range(2):
                                            for f in range(2):
                                                w = slice(f * D + half * 512, f * D + (half + 1) * 512)
                                                mm = three(PS[:, 5 + half, :], hidT[:, 0, f, :], hidT[:, 1, f, :],
                                                           high[:, 2, w], low[:, 2, w], f == 0, f == 1)
                                        mm.then_inc(slot_used, 1)
                                        if more:
                                            pe.wait_ge(S["he_ev"], 4 * e + 6)
                                            gather(1, 1 - b)
                                    if not last:
                                        pe.wait_ge(S["gs_ev"], GROUP * g + GROUP + 1)
                                    for q in range(2 * T):
                                        c, half = q // 2, q % 2
                                        if q >= 2:
                                            pe.wait_ge(S["sc_ev"], 6 * g + q)
                                        for j in range(GROUP):
                                            if q == 0:
                                                pe.wait_ge(S["y_low"], GROUP * g + j + 2)
                                            for yy in (yh, yl):
                                                mm = pe.matmul(PS[:, (7, 3)[q % 2], :], hi(PTb[:, j, c * P:(c + 1) * P]),
                                                               hi(yy[:, j, half * 512:(half + 1) * 512]),
                                                               start=(j == 0 and yy is yh), stop=(j == GROUP - 1 and yy is yl))
                                        mm.then_inc(S["sc_mm"], 1)

                                pe.wait_ge(S["pb_ready"], 1)
                                gather(0, 0)
                                pe.wait_ge(S["he_ev"], 2)
                                gather(1, 0)
                                slot_weights(0, 0)
                                with pe.Fori(0, NG - 1) as g:
                                    step(g)
                                step(NG - 1, last=True)

                            @block.vector
                            def _(dve):
                                for name in ("pt_ev", "y_low", "sc_ev"):
                                    dve.sem_inc(S[name], 1)
                                dve.sem_inc(S["low_v"], CV)

                                def one_hot(b, e):
                                    for c in range(T):
                                        ins = dve.tensor_scalar(hi(Pb[:, b, c, :]), cst[:, C_IOTA:C_IOTA + P], posm[:, c, wcol(e)], None, ALU.is_equal)
                                    ins.then_inc(S["pb_ready"], 1)

                                def weights(b, n):
                                    dve.wait_ge(S["gs_mm"], n)
                                    dve.tensor_copy(gs[:, b:b + 1], PS[:, 7, 0:1]).then_inc(S["gs_ev"], 1)

                                def cut(g, s):
                                    r, k = s % NR, s % 3
                                    dve.wait_ge(landed[r], loads_group(s) * g + loads(s))
                                    dve.wait_ge(slot_used, GS * g + s + 1)
                                    round_high(dve, high[:, k, :], ring[:, r, :]).then_inc(S["cut_p" if k == 1 else "cut_v"], 1)
                                    if k != 1:
                                        dve.wait_ge(S["cut_v"], 2 * GROUP * g + 2 * (s // 3) + (1 if k == 0 else 2))
                                        dve.tensor_tensor(hi(low[:, k, :]), ring[:, r, :], high[:, k, :], ALU.subtract).then_inc(S["low_v"], 1)

                                def step(g, last=False):
                                    for j in range(GROUP):
                                        e = GROUP * g + j
                                        b = j % 2
                                        more = not (last and j == GROUP - 1)
                                        if more:
                                            cut(g, 3 * j + 3)
                                        dve.wait_ge(S["silu"], e + 1)
                                        dve.wait_ge(S["gs_ev"], e + 1)
                                        dve.scalar_tensor_tensor(hid[:, :], PS[:, 2, DE:2 * DE], gs[:, b:b + 1], sg[:, :],
                                                                 ALU.mult, ALU.mult).then_inc(S["hid_ready"], 1)
                                        if more:
                                            weights(1 - b, e + 2)
                                        dve.wait_ge(S["ht_ev"], e + 1)
                                        dve.tensor_tensor(hi(hidT[:, 1, :, :].rearrange("p b n -> p (b n)")), PS[:, 3, 0:DE],
                                                          hidT[:, 0, :, :].rearrange("p b n -> p (b n)"), ALU.subtract).then_inc(S["hidT_low"], 1)
                                        if more:
                                            cut(g, 3 * j + 4)
                                            dve.wait_ge(S["pt_mm"], e + 1)
                                            one_hot(b, e + 2)
                                        dve.wait_ge(S["y_high"], e + 1)
                                        dve.tensor_tensor(hi(yl[:, j, :].rearrange("p (b n) -> p b n", b=2)), PS[:, 5:7, :],
                                                          yh[:, j, :].rearrange("p (b n) -> p b n", b=2), ALU.subtract).then_inc(S["y_low"], 1)
                                        if more:
                                            cut(g, 3 * j + 5)
                                    for q in range(2 * T):
                                        c, half = q // 2, q % 2
                                        dve.wait_ge(S["sc_mm"], 6 * g + q + 1)
                                        at = acc[:, c, half * 512:(half + 1) * 512]
                                        dve.tensor_tensor(at, at, PS[:, (7, 3)[q % 2], :], ALU.add).then_inc(S["sc_ev"], 1)

                                one_hot(0, 0)
                                one_hot(1, 1)
                                cut(0, 0)
                                cut(0, 1)
                                cut(0, 2)
                                weights(0, 1)
                                with dve.Fori(0, NG - 1) as g:
                                    step(g)
                                step(NG - 1, last=True)
                                dve.wait_ge(S["pb_ready"], NE + 1)
                                dve.tensor_scalar(posm[:, :, 0:NE], posm[:, :, 0:NE], -float(SLOTS), None, ALU.add).then_inc(chain_v, 1)
                                dve.wait_ge(chain_v, 1)
                                dve.wait_ge(S["sc_ev"], 6 * NG + 1)
                        end_section()

                with nc.Block() as block:
                    @block.vector
                    def _(dve):
                        v = Chain(dve, chain_v)
                        for t in range(T):
                            dve.tensor_tensor(acc[:, t, :], acc[:, t, :], gate[:, min(t, 1), :], ALU.mult).then_inc(chain_v, 1)
                        v.n = T
                        dve.wait_ge(chain_v, T)
                        for t in range(T):
                            dve.tensor_tensor(x[:, t, :], x[:, t, :], acc[:, t, :], ALU.add).then_inc(chain_v, 1)
                        dve.wait_ge(chain_v, 2 * T)
                end_section()
            if debug == "moe":
                with nc.Block() as block:
                    @block.sync
                    def _(sp):
                        sp.dma_start(O["dbg"].rearrange("(t p) d -> p t d", p=P), x[:, :, :]).then_inc(stored, 16)
                        sp.wait_ge(stored, 16)
                end_section()

        with nc.Block() as block:
            @block.sync
            def _(sp):
                sp.dma_start(O["y_prompt"][0], x[:, 0, :]).then_inc(stored, 16)
                sp.dma_start(O["y_sample"][0].rearrange("(t p) d -> p t d", p=P), x[:, 1:3, :]).then_inc(stored, 16)
                sp.wait_ge(stored, 32)


OUTS = ["y_prompt", "y_sample", "new_na_k", "new_na_v", "new_df_k", "new_df_v", "new_ml_C", "new_ml_n", "new_ml_m"]
INS = ["x_prompt", "x_sample", "cache_na_k", "cache_na_v", "cache_df_k", "cache_df_v", "state_ml_C", "state_ml_n",
       "state_ml_m", "c", "c_ctx", "w_ada", "b_ada", "g_norm1", "g_norm2", "w_in", "w_out", "na_qn", "na_kn", "na_rpb",
       "df_qn", "df_kn", "df_lam", "df_subln", "ml_gate_b", "ml_outn", "w_router", "b_router", "w_exp1", "w_exp3",
       "w_exp2", "w_sh1", "w_sh3", "w_sh2"]
SHAPES = [(1, P, D), (1, 2 * P, D), (1, DEPTH, NAH, P, NAD), (1, DEPTH, NAH, P, NAD), (1, DEPTH, DFH, 2, P, DFD),
          (1, DEPTH, DFH, P, DFV), (1, DEPTH, 2, MLH, MLD, MLD), (1, DEPTH, 2, MLH, MLD), (1, DEPTH, 2, MLH)]


def kernel(**inputs):
    import concourse.bacc as bacc
    from concourse.bass_utils import run_bass_kernel_spmd

    nc = bacc.Bacc("TRN2", target_bir_lowering=False, num_devices=1)
    arrays = {f"in_{n}": np.ascontiguousarray(inputs[n]) for n in INS}
    arrays["in_consts"] = constants()
    A = {n[3:]: nc.dram_tensor(n, a.shape, mybir.dt.from_np(a.dtype), kind="ExternalInput").ap() for n, a in arrays.items()}
    O = {n: nc.dram_tensor(f"out_{n}", s, F32, kind="ExternalOutput").ap() for n, s in zip(OUTS, SHAPES)}
    program(nc, A, O)
    r = run_bass_kernel_spmd(nc, [arrays], core_ids=[0])
    return tuple(r.results[0][f"out_{n}"] for n in OUTS)
```

```python
from contextlib import ExitStack

import concourse.bass as bass
import numpy as np
from concourse import mybir

F32 = mybir.dt.float32
F32R = mybir.dt.float32r
I32 = mybir.dt.int32
U32 = mybir.dt.uint32
HIGH_BITS = 0xFFFFF000
ALU = mybir.AluOpType
ACT = mybir.ActivationFunctionType
AX = mybir.AxisListType

P = 128
DEPTH, D = 2, 1024
DEPTH_RUN = DEPTH
KC = D // P
T = 3
GRID_W = 64
NAH, NAD = 4, 64
DFH, DFD, DFV = 4, 32, 64
MLH, MLD = 4, 128
NA_W, DF_W, ML_W = 256, 256, 512
IN_COLS = 3600
NE, TOPK, DE = 32, 4, 256
ROUTED_SCALE = 2.5
EPS = 1e-6
WIN_C = 16
RPB_R, RPB_C = 15, 31
NEG = -1e30
SLOTS = P
GROUP = 4
SLOTF = 2048

C_ID, C_IOTA, C_TRIU, C_ONES, C_TAB = 0, 128, 256, 384, 512
T_MF, T_MB, T_COL, T_COS, T_SIN, T_LAM, T_SEL, T_N = 0, 128, 256, 320, 384, 448, 452, 964
B_NAG, B_DFG, B_SUB, B_OUT, B_GB, B_LAM, B_N = 0, 128, 192, 256, 384, 400, 528


def constants():
    c = np.zeros((P, C_TAB + T_N), np.float32)
    tab = c[:, C_TAB:]
    p = np.arange(P)
    c[:, C_ID:C_ID + P] = np.eye(P)
    c[:, C_IOTA:C_IOTA + P] = p[None, :]
    c[:, C_TRIU:C_TRIU + P] = p[:, None] < p[None, :]
    c[:, C_ONES:C_ONES + P] = 1.0
    tab[:, T_MF:T_MF + P] = np.where(p[:, None] <= p[None, :], 0.0, 1e30)
    tab[:, T_MB:T_MB + P] = np.where(p[:, None] >= p[None, :], 0.0, 1e30)
    col = p % GRID_W
    first = np.clip(col - WIN_C // 2, 0, GRID_W - WIN_C)
    k = np.arange(GRID_W)
    tab[:, T_COL:T_COL + GRID_W] = np.where((k >= first[:, None]) & (k < first[:, None] + WIN_C), 0.0, NEG)
    nf = DFD // 4
    inv = 1.0 / (10000.0 ** (np.arange(nf, dtype=np.float32) / nf))
    for t in range(2):
        row = (t * P + p) // GRID_W
        for a, pos in enumerate((row, col)):
            ang = pos.astype(np.float32)[:, None] * inv
            at = t * DFD + a * 2 * nf
            tab[:, T_COS + at:T_COS + at + nf] = tab[:, T_COS + at + nf:T_COS + at + 2 * nf] = np.cos(ang)
            tab[:, T_SIN + at:T_SIN + at + nf] = -np.sin(ang)
            tab[:, T_SIN + at + nf:T_SIN + at + 2 * nf] = np.sin(ang)
    for layer in range(DEPTH):
        lam_init = 0.8 - 0.6 * np.exp(-0.3 * layer)
        tab[:, T_LAM + 2 * layer] = lam_init
        tab[:, T_LAM + 2 * layer + 1] = 1.0 - lam_init
    for h in range(MLH):
        tab[h, T_SEL + h * P:T_SEL + (h + 1) * P] = 1.0
    return c


def hi(ap):
    return ap.bitcast(F32R)


def round_high(eng, out, in_):
    return eng.tensor_copy(hi(out), in_)


class Chain:

    def __init__(self, eng, sem, base=0):
        self.eng, self.sem, self.n, self.base = eng, sem, 0, base

    def __call__(self, ins):
        self.n += 1
        ins.then_inc(self.sem, 1)
        self.eng.wait_ge(self.sem, self.base + self.n)
        return ins


def program(nc, A, O, debug=None):
    with ExitStack() as top:
        top.enter_context(nc.allow_non_contiguous_dma(reason="a few short vectors are loaded across partitions"))
        def sb(name, shape, dt=F32, ctx=top):
            return ctx.enter_context(nc.sbuf_tensor(name, shape, dt))

        sems = []

        def sem(name):
            s = top.enter_context(nc.semaphore(name))
            sems.append(s)
            return s

        def end_section():
            nc.all_engine_barrier()
            nc.gpsimd.dma_reset(range(sems[0].num, sems[-1].num + 1))
            nc.gpsimd.sem_clear(range(sems[0].num, sems[-1].num + 1))
            nc.all_engine_barrier()

        cst = sb("cst", [P, C_TAB])
        x = sb("x", [P, T, D])
        mcol = sb("mcol", [P, 64])
        gate = sb("gate", [P, 2, D])
        small = sb("small", [P, 256])
        npass = sb("npass", [P, 1], I32)
        nhalf = small[:, 0:8]
        ssq, rstd = small[:, 32:35], small[:, 36:39]
        PS = top.enter_context(nc.psum_tensor("PS", [P, 8, 512], F32))

        ident = cst[:, C_ID:C_ID + P]
        ones = cst[:, C_ONES:C_ONES + P]

        NRING = 12
        landed = [sem(f"slot_landed{i}") for i in range(NRING)]
        slot_used = sem("slot_used")
        loaded = sem("small_loaded")
        loaded2 = sem("late_loaded")
        stored = sem("stored")
        chain_v = sem("vector_chain")
        chain_s = sem("scalar_chain")
        chain_p = sem("pool_chain")
        chain_t = sem("tensor_chain")
        N = {k: sem(k) for k in (
            "csilu", "mod_row", "mod_tr", "mod_col",
            "ssq_ready", "rstd_ready", "xn_ready", "xn_tr", "hT_s", "hT_v",
            "tail_mm", "proj_mm", "proj_ev", "lf_ready", "rows_tr", "rows_v",
            "cols_mm", "ctx_tr", "ctx_ev", "sq_ready", "ms_ready", "r_ready", "qk_ready",
            "att_tr", "att_ev", "sc_mm", "nm_ready", "ex_ready", "w_ready", "pt_mm", "pt_ev",
            "pv_mm", "pv_ev", "exin", "exout", "mix_df", "mqk_tr", "mqk_ev", "st_mm", "st_ev",
            "mb_mm", "mb_free", "d_ready", "e_ready", "s_ready", "wk_ready", "num_mm", "num_ev", "upd_mm",
            "c_ready", "decayed", "gate_ready", "sq_part", "mixT", "ml_done", "sig_e", "mix_ready", "mix_tr", "mix_ev", "out_mm", "x_done",
            "rt_mm", "rt_e", "rt_s", "mask_ready", "pos_mm", "back_tr", "back_ev", "total_mm", "route_done",
            "cut_v", "cut_p", "cut_s", "low_v", "low_p", "idw_ready", "id_part", "ga_mm", "ga_ev", "gs_ev", "pb_ready", "silu", "hid_ready",
            "ht_mm", "ht_ev", "hidT_low", "y_high", "y_low", "sc_ev",
            "sh_mm", "sh_silu", "sh_hid", "sh_tr", "sh_trev", "sh_down", "sh_done",
        )}
        S = N

        modd = nc.dram_tensor("mod_rows", [DEPTH, 2, 6 * D], F32, kind="Internal").ap()
        mcold = nc.dram_tensor("mod_cols", [DEPTH, P, 64], F32, kind="Internal").ap()
        biasd = nc.dram_tensor("na_bias", [DEPTH, 2, P, NAH, 256], F32, kind="Internal").ap()

        def bcast(ap, n):
            return bass.AP(tensor=ap.tensor, offset=ap.offset, ap=[[0, P], [1, n]])

        with ExitStack() as sec:
            NR, NC_ = 5, 3
            raw = sb("raw0", [P, NR, SLOTF], ctx=sec)
            high = sb("high0", [P, NC_, SLOTF], ctx=sec)
            low = sb("low0", [P, NC_, SLOTF], ctx=sec)
            modr = sb("modr", [2, 6 * D], ctx=sec)
            bada = sb("bada", [2, DEPTH, 6 * D], ctx=sec)
            gn = sb("gn", [2, DEPTH, 2, D], ctx=sec)
            ccol = sb("ccol", [P, KC, 2], ctx=sec)
            chigh = sb("chigh", [P, KC, 2], ctx=sec)
            clow = sb("clow", [P, KC, 2], ctx=sec)
            mstage = sb("mstage", [P, 64], ctx=sec)
            NB = 12
            SLOTS0 = DEPTH * NB * 2

            with nc.Block() as block:
                @block.sync
                def _(sp):
                    sp.dma_start(cst[:, :], A["consts"][:, 0:C_TAB]).then_inc(loaded, 16)
                    sp.dma_start(ccol[:, :, 0], A["c_ctx"].rearrange("(c p) -> p c", p=P)).then_inc(loaded, 16)
                    sp.dma_start(ccol[:, :, 1], A["c"][0].rearrange("(c p) -> p c", p=P)).then_inc(loaded, 16)
                    sp.dma_start(x[:, 0, :], A["x_prompt"][0]).then_inc(loaded, 16)
                    sp.dma_start(x[:, 1:3, :], A["x_sample"][0].rearrange("(t p) d -> p t d", p=P)).then_inc(loaded, 16)
                    n = 0
                    for l in range(DEPTH):
                        for b in range(NB):
                            for half in range(2):
                                if n >= NR:
                                    sp.wait_ge(S["low_v"], n - NR + 1)
                                src = A["w_ada"][l, half * 512:(half + 1) * 512, b * 512:(b + 1) * 512]
                                sp.dma_start(raw[:, n % NR, :].rearrange("p (c n) -> p c n", c=4),
                                             src.rearrange("(c p) n -> p c n", p=P)).then_inc(landed[n % NR], 16)
                                n += 1

                @block.gpsimd
                def _(pool):
                    pool.memset(nhalf, -0.5).then_inc(chain_p, 1)
                    for l in range(DEPTH):
                        for t in range(2):
                            for r2 in range(2):
                                for h in range(NAH):
                                    r = 2 * t + r2
                                    base = A["na_rpb"][l, h]
                                    src = bass.AP(tensor=base.tensor,
                                                  offset=base.offset + (7 - r) * RPB_C + WIN_C - 1,
                                                  ap=[[RPB_C, 4], [-1, 64], [1, 64]])
                                    pool.dma_start(
                                        biasd[l, t, r2 * 64:(r2 + 1) * 64, h].rearrange("q (j k) -> j q k", j=4),
                                        src).then_inc(loaded2, 16)
                    for l in range(DEPTH):
                        pool.wait_ge(S["mod_col"], l + 1)
                        pool.dma_start(mcold[l], mstage[:, :]).then_inc(stored, 16)
                        pool.dma_start(modd[l], modr[:, :]).then_inc(stored, 16)
                        pool.wait_ge(stored, 32 * (l + 1))
                    pool.wait_ge(loaded2, 16 * 32)

                @block.scalar
                def _(act):
                    for l in range(DEPTH):
                        for i in range(2):
                            act.dma_start(bada[i:i + 1, l, :], A["b_ada"][l].rearrange("(o n) -> o n", o=1)).then_inc(S["exin"], 16)
                            act.dma_start(gn[i:i + 1, l, 0, :], A["g_norm1"][l].rearrange("(o n) -> o n", o=1)).then_inc(S["exin"], 16)
                            act.dma_start(gn[i:i + 1, l, 1, :], A["g_norm2"][l].rearrange("(o n) -> o n", o=1)).then_inc(S["exin"], 16)
                    act.wait_ge(loaded, 80)
                    act.activation(ccol[:, :, :], ccol[:, :, :], ACT.Silu).then_inc(S["silu"], 1)
                    for n in range(SLOTS0):
                        act.wait_ge(landed[n % NR], 16 * (n // NR + 1))
                        if n >= NC_:
                            act.wait_ge(slot_used, n - NC_ + 1)
                        act.activation(hi(high[:, n % NC_, :]), raw[:, n % NR, :], ACT.Copy).then_inc(S["cut_s"], 1)

                @block.tensor
                def _(pe):
                    pe.wait_ge(S["csilu"], 2)
                    n = 0
                    for l in range(DEPTH):
                        for b in range(NB):
                            i = l * NB + b
                            if i >= 4:
                                pe.wait_ge(S["mod_row"], i - 3)
                            for half in range(2):
                                pe.wait_ge(S["low_v"], n + 1)
                                for c in range(4):
                                    k = half * 4 + c
                                    w = slice(c * 512, (c + 1) * 512)
                                    out = PS[0:2, i % 4, :]
                                    pe.matmul(out, hi(chigh[:, k, :]), hi(high[:, n % NC_, w]), start=(k == 0), stop=False)
                                    pe.matmul(out, hi(chigh[:, k, :]), hi(low[:, n % NC_, w]), start=False, stop=False)
                                    mm = pe.matmul(out, hi(clow[:, k, :]), hi(high[:, n % NC_, w]), start=False, stop=(k == 7))
                                mm.then_inc(slot_used, 1)
                                n += 1
                        pe.wait_ge(S["exout"], l + 1)
                        for kind, at in enumerate((0, D, 3 * D, 4 * D)):
                            for c in range(KC):
                                o = (kind * KC + c) * 2
                                mm = pe.transpose(PS[:, 4, o:o + 2], modr[:, at + c * P:at + (c + 1) * P], ident[0:2, 0:2])
                        mm.then_inc(S["mod_tr"], 1)

                @block.vector
                def _(dve):
                    v = Chain(dve, chain_v)
                    dve.wait_ge(S["silu"], 1)
                    round_high(dve, chigh[:, :, :], ccol[:, :, :]).then_inc(S["csilu"], 1)
                    dve.wait_ge(S["csilu"], 1)
                    dve.tensor_tensor(hi(clow[:, :, :]), ccol[:, :, :], chigh[:, :, :], ALU.subtract).then_inc(S["csilu"], 1)

                    def cut_low(n):
                        dve.wait_ge(S["cut_s"], n + 1)
                        dve.tensor_tensor(hi(low[:, n % NC_, :]), raw[:, n % NR, :], high[:, n % NC_, :], ALU.subtract).then_inc(S["low_v"], 1)

                    def rows(l, b):
                        i = l * NB + b
                        dve.wait_ge(slot_used, 2 * (i + 1))
                        dve.tensor_tensor(modr[:, b * 512:(b + 1) * 512], PS[0:2, i % 4, :],
                                          bada[:, l, b * 512:(b + 1) * 512], ALU.add).then_inc(S["mod_row"], 1)

                    cut_low(0)
                    cut_low(1)
                    dve.wait_ge(S["exin"], 96 * DEPTH)
                    for l in range(DEPTH):
                        for b in range(NB):
                            for n in (2 * (l * NB + b) + 2, 2 * (l * NB + b) + 3):
                                if n < SLOTS0:
                                    cut_low(n)
                            if l and b == 0:
                                dve.wait_ge(stored, 32 * l)
                            rows(l, b)
                        dve.wait_ge(S["mod_row"], NB * (l + 1))
                        for i, at in enumerate((D, 4 * D)):
                            v(dve.scalar_tensor_tensor(modr[:, at:at + D], modr[:, at:at + D], 1.0, gn[:, l, i, :],
                                                       ALU.add, ALU.mult))
                        dve.sem_inc(S["exout"], 1)
                        dve.wait_ge(S["mod_tr"], l + 1)
                        dve.tensor_copy(mstage[:, :], PS[:, 4, 0:64]).then_inc(S["mod_col"], 1)

            end_section()

        def norm_act(act, which):
            for t in range(T):
                act.activation(tok[:, t, :], x[:, t, :], ACT.Square, accum_out=ssq[:, t:t + 1]).then_inc(S["ssq_ready"], 1)

        def norm_pool(pool, chain):
            pool.wait_ge(S["ssq_ready"], T)
            chain(pool.tensor_scalar(rstd, ssq, 1.0 / D, EPS, ALU.mult, ALU.add))
            pool.tensor_tensor(rstd, rstd, nhalf[:, 0:T], ALU.pow).then_inc(S["rstd_ready"], 1)

        def norm_dve(dve):
            dve.wait_ge(S["rstd_ready"], 1)
            for t in range(T):
                dve.tensor_scalar(tok[:, t, :], x[:, t, :], rstd[:, t:t + 1], None, ALU.mult).then_inc(S["xn_ready"], 1)

        def norm_pe(pe):
            for t in range(T):
                pe.wait_ge(S["xn_ready"], t + 1)
                for half in range(2):
                    i = 2 * t + half
                    if i >= 4:
                        pe.wait_ge(S["hT_s" if half == 0 else "hT_v"], 4 * (t - 1))
                    for c in range(4):
                        k = half * 4 + c
                        mm = pe.transpose(PS[:, i % 4, c * P:(c + 1) * P], tok[:, t, k * P:(k + 1) * P], ident)
                    mm.then_inc(S["xn_tr"], 1)

        def mod_at(kind, k, t):
            o = (kind * KC + k) * 2 + min(t, 1)
            return mcol[:, o:o + 1]

        def norm_ev_act(act, which, hT):
            for t in range(T):
                act.wait_ge(S["xn_tr"], 2 * t + 1)
                for c in range(4):
                    act.activation(hT[:, c, t * P:(t + 1) * P], PS[:, (2 * t) % 4, c * P:(c + 1) * P], ACT.Identity,
                                   bias=mod_at(2 * which, c, t), scale=mod_at(2 * which + 1, c, t)).then_inc(S["hT_s"], 1)

        def norm_ev_dve(dve, which, hT):
            for t in range(T):
                dve.wait_ge(S["xn_tr"], 2 * t + 2)
                for c in range(4):
                    k = 4 + c
                    dve.tensor_scalar(hT[:, k, t * P:(t + 1) * P], PS[:, (2 * t + 1) % 4, c * P:(c + 1) * P],
                                      mod_at(2 * which + 1, k, t), mod_at(2 * which, k, t),
                                      ALU.mult, ALU.add).then_inc(S["hT_v"], 1)


        nm, rs, rr = small[:, 84:88], small[:, 88:92], small[:, 92:96]
        nlam, omli = small[:, 96:97], small[:, 97:98]
        lamt = small[:, 98:102]
        zrow = small[0:4, 128:256]
        NSA = 4
        ML_ORDER = [(0, 0), (0, 1), (1, 0), (2, 1), (2, 0), (1, 1)]
        FINISHED = {0: 1, 2: 4, 1: 5}
        OUT_ORDER = (0, 2, 1)
        BATCHES = [(t, kind) for t in range(T) for kind in ("na", "df0", "df1")]
        UNITS = [(g, t) for g in range(3, 7) for t in range(T)]
        LATE = 3

        with nc.Fori(0, DEPTH_RUN) as l:
            with ExitStack() as sec:
                tok = sb("tokA", [P, T, D], ctx=sec)
                prm = sb("prm", [P, B_N], ctx=sec)
                tab = sb("tab", [P, T_N], ctx=sec)
                ring = sb("ringA", [P, NSA, SLOTF], ctx=sec)
                hT = sb("hT", [P, KC, T * P], ctx=sec)
                p = sb("p", [P, T, 2560], ctx=sec)
                attT = sb("attT", [P, 8, 512], ctx=sec)
                bias = sb("bias", [P, 2, NAH, 256], ctx=sec)
                W1 = sb("W1", [P, 4, 384], ctx=sec)
                W2 = sb("W2", [P, 4, 384], ctx=sec)
                PT = sb("PT", [P, 2, 384], ctx=sec)
                ckv = sb("ckv", [P, 4, 256], ctx=sec)
                vaug = sb("vaug", [P, T, MLH, MLD + 1], ctx=sec)
                Caug = sb("Caug", [P, 8, MLD + 1], ctx=sec)
                Cp = sb("Cp", [P, 8, MLD + 1], ctx=sec)
                ST = sb("ST", [P, T, 512], ctx=sec)
                mlh = sb("mlh", [P, T, 512], ctx=sec)
                num = sb("num", [P, 4, MLD + 1], ctx=sec)
                tmp = sb("tmp", [P, 4, MLD + 1], ctx=sec)
                wk = sb("wk", [P, 512], ctx=sec)
                R = sb("R", [4, T, 2, 2, P], ctx=sec)
                brow = sb("brow", [4, T, 2, P], ctx=sec)
                sm = sb("sm", [P, 512], ctx=sec)
                gt = sm[:, 0:48].rearrange("p (t g) -> p t g", t=T)
                e1 = sm[:, 48:72].rearrange("p (t d h) -> p t d h", t=T, d=2)
                e2 = sm[:, 72:96].rearrange("p (t d h) -> p t d h", t=T, d=2)
                cols = sm[:, 96:168].rearrange("p (q n) -> p q n", q=3)
                bcs = sm[:, 168:216].rearrange("p (n k h) -> p n k h", n=6, k=2)
                arg = sm[:, 216:312].rearrange("p (q n) -> p q n", q=4)
                ms = sm[:, 312:384]
                ms2 = sm[:, 384:396]
                den = sm[:, 396:400]
                scal = sm[0:4, 400:412].rearrange("p (n k) -> p n k", n=6)
                diag = sm[0:4, 412:460].rearrange("p (n h) -> p n h", n=12)
                m0 = sm[0:4, 460:462]
                mout = sm[0:4, 462:464]
                nq = W1[:, :, :].rearrange("p a b -> p (a b)")
                dq = W2[:, :, :].rearrange("p a b -> p (a b)")
                last = lambda d: P - 1 if d == 0 else 0
                X = [dq[:, i * 512:(i + 1) * 512].rearrange("p (h n) -> p h n", h=4) for i in range(2)]
                wks = [wk[:, :], dq[:, 1024:1536]]

                def col4(q, td):
                    return cols[:, q, 4 * td:4 * td + 4]

                def arg4(q, td):
                    return arg[:, q, 4 * td:4 * td + 4]

                def keys_of(t):
                    return (0, P) if t == 0 else (P, 512)

                def aps_of(batch):
                    t, kind = batch
                    k0, k1 = keys_of(t)
                    out = []
                    for m in range(4):
                        if kind == "na":
                            i, rows = m // 2, slice(64 * (m % 2), 64 * (m % 2) + 64)
                            j = 2 + i
                        else:
                            hf = int(kind[2])
                            i, rows = 4 + hf, slice(32 * m, 32 * m + 32)
                            j = 6 + hf
                        out.append((attT[rows, i, t * P:(t + 1) * P], attT[rows, j, k0:k1]))
                    return out

                def values_of(batch, m):
                    t, kind = batch
                    at, ck, h = (512, 1, m) if kind == "na" else (1280, 3, 2 * int(kind[2]) + m)
                    if t == 0:
                        return [p[:, 0, at + 64 * h:at + 64 * h + 64]]
                    return [p[:, u, at + 64 * h:at + 64 * h + 64] for u in (1, 2)] + [ckv[:, ck, 64 * h:64 * h + 64]]

                n_maps = lambda batch: 4 if batch[1] == "na" else 2
                first_map = [sum(n_maps(b) for b in BATCHES[:i]) for i in range(len(BATCHES) + 1)]

                with nc.Block() as block:
                    @block.sync
                    def _(sp):
                        for at, n, name in ((B_NAG, 64, "na_qn"), (B_NAG + 64, 64, "na_kn"), (B_DFG, 32, "df_qn"),
                                            (B_DFG + 32, 32, "df_kn"), (B_SUB, 64, "df_subln"), (B_OUT, 128, "ml_outn")):
                            sp.dma_start(prm[:, at:at + n], bcast(A[name][l], n)).then_inc(loaded, 16)
                        sp.dma_start(prm[:, B_GB:B_GB + 16], bcast(A["ml_gate_b"][l], 16)).then_inc(loaded, 16)
                        sp.dma_start(prm[:, B_LAM:B_LAM + 128], bcast(A["df_lam"][l], 128)).then_inc(loaded, 16)
                        sp.dma_start(mcol[:, :], mcold[l]).then_inc(loaded, 16)
                        sp.dma_start(m0, A["state_ml_m"][0, l].rearrange("r h -> h r")).then_inc(loaded, 16)
                        sp.dma_start(tab[:, :], A["consts"][:, C_TAB:C_TAB + T_N]).then_inc(loaded, 16)
                        n = 0

                        def slot_free():
                            if n >= NSA:
                                sp.wait_ge(slot_used, n - NSA + 1)

                        sp.dma_start(ring[:, 0, 0:128].rearrange("p (c n) -> p c n", c=KC),
                                     A["w_in"][l, :, 3584:3600].rearrange("(c p) n -> p c n", p=P)).then_inc(landed[0], 16)
                        n = 1
                        for w, groups in (("w_in", 7), ("w_out", 2)):
                            for gr in range(groups):
                                for half in range(2):
                                    slot_free()
                                    src = A[w][l, half * 512:(half + 1) * 512, gr * 512:(gr + 1) * 512]
                                    sp.dma_start(ring[:, n % NSA, :].rearrange("p (c n) -> p c n", c=4),
                                                 src.rearrange("(c p) n -> p c n", p=P)).then_inc(landed[n % NSA], 16)
                                    n += 1

                    @block.gpsimd
                    def _(pool):
                        norm_pool(pool, Chain(pool, chain_p))
                        for i in range(2):
                            pool.dma_start(gate[:, i, :], bcast(modd[l, i, 2 * D:3 * D], D)).then_inc(loaded2, 16)
                        pool.dma_start(ckv[:, 0, :].rearrange("p (h d) -> p h d", h=4),
                                       A["cache_na_k"][0, l].rearrange("h k d -> k h d")).then_inc(loaded2, 16)
                        pool.dma_start(ckv[:, 1, :].rearrange("p (h d) -> p h d", h=4),
                                       A["cache_na_v"][0, l].rearrange("h k d -> k h d")).then_inc(loaded2, 16)
                        pool.dma_start(ckv[:, 2, :].rearrange("p (h d) -> p h d", h=8),
                                       A["cache_df_k"][0, l].rearrange("h a k d -> k (h a) d")).then_inc(loaded2, 16)
                        pool.dma_start(ckv[:, 3, :].rearrange("p (h d) -> p h d", h=4),
                                       A["cache_df_v"][0, l].rearrange("h k d -> k h d")).then_inc(loaded2, 16)
                        for t in range(2):
                            pool.dma_start(bias[:, t, :, :], biasd[l, t]).then_inc(loaded2, 16)
                        pool.dma_start(Caug[:, :, 0:MLD], A["state_ml_C"][0, l].rearrange("r h d e -> d (r h) e")).then_inc(loaded2, 16)
                        pool.dma_start(Caug[:, :, MLD], A["state_ml_n"][0, l].rearrange("r h d -> d (r h)")).then_inc(loaded2, 16)
                        for i, (n0, n1) in enumerate(((0, 24), (24, 72))):
                            pool.wait_ge(S["ms_ready"], i + 1)
                            pool.tensor_tensor(ms[:, n0:n1], ms[:, n0:n1], nhalf[:, 0:1].to_broadcast([P, n1 - n0]), ALU.pow).then_inc(S["r_ready"], 1)
                        pool.wait_ge(S["qk_ready"], 1)
                        pool.dma_start(O["new_na_k"][0, l].rearrange("h p d -> p h d"),
                                       p[:, 0, 256:512].rearrange("p (h d) -> p h d", h=4)).then_inc(stored, 16)
                        pool.dma_start(O["new_na_v"][0, l].rearrange("h p d -> p h d"),
                                       p[:, 0, 512:768].rearrange("p (h d) -> p h d", h=4)).then_inc(stored, 16)
                        pool.dma_start(O["new_df_k"][0, l].rearrange("h a p d -> p (h a) d"),
                                       p[:, 0, 1024:1280].rearrange("p (h d) -> p h d", h=8)).then_inc(stored, 16)
                        pool.dma_start(O["new_df_v"][0, l].rearrange("h p d -> p h d"),
                                       p[:, 0, 1280:1536].rearrange("p (h d) -> p h d", h=4)).then_inc(stored, 16)
                        pool.wait_ge(S["ms_ready"], 3)
                        pool.tensor_tensor(ms2, ms2, nhalf[:, 0:1].to_broadcast([P, 12]), ALU.pow).then_inc(S["r_ready"], 1)
                        c = Chain(pool, chain_p, 1)
                        pool.wait_ge(S["exin"], 3)
                        pool.wait_ge(S["pv_ev"], len(BATCHES))

                        def weigh_keys(i):
                            if i >= 2:
                                pool.wait_ge(S["upd_mm"], i - 1)
                            t, d = ML_ORDER[i]
                            pool.tensor_tensor(wks[i % 2].rearrange("p (h n) -> p h n", h=4),
                                               p[:, t, 1536:2048].rearrange("p (h n) -> p h n", h=4),
                                               arg4(2, 2 * t + d)[:, :, None].to_broadcast([P, 4, P]), ALU.mult).then_inc(S["wk_ready"], 1)

                        def decay(i):
                            t, d = ML_ORDER[i]
                            pool.wait_ge(S["num_mm"], i + 1)
                            C4 = Caug[:, 4 * d:4 * d + 4, :]
                            pool.tensor_tensor(C4, C4, arg4(3, 2 * t + d)[:, :, None].to_broadcast([P, 4, MLD + 1]), ALU.mult).then_inc(S["decayed"], 1)

                        def head_rsqrt(o):
                            m4 = ms2[:, 4 * o:4 * o + 4]
                            pool.wait_ge(S["sq_ready"], 7 + o)
                            c(pool.tensor_scalar(m4, m4, 1.0 / MLD, EPS, ALU.mult, ALU.add))
                            pool.tensor_tensor(m4, m4, nhalf[:, 0:4], ALU.pow).then_inc(S["r_ready"], 1)

                        weigh_keys(0)
                        weigh_keys(1)
                        pool.wait_ge(S["sig_e"], 1)
                        for t in OUT_ORDER:
                            mo = p[:, t, 2048:2560].rearrange("p (h n) -> p h n", h=4)
                            pool.tensor_tensor(mo, mo, prm[:, None, B_OUT:B_OUT + P].to_broadcast([P, 4, P]), ALU.mult).then_inc(S["gate_ready"], 1)
                        weigh_keys(2)
                        head_rsqrt(0)
                        decay(2)
                        weigh_keys(3)
                        decay(3)
                        pool.dma_start(O["new_ml_C"][0, l].rearrange("r h d e -> d (r h) e"), Cp[:, :, 0:MLD]).then_inc(stored, 16)
                        pool.dma_start(O["new_ml_n"][0, l].rearrange("r h d -> d (r h)"), Cp[:, :, MLD]).then_inc(stored, 16)
                        pool.dma_start(O["new_ml_m"][0, l].rearrange("r h -> h r"), mout).then_inc(stored, 16)
                        head_rsqrt(1)
                        head_rsqrt(2)
                        pool.wait_ge(stored, 16 * 7)

                    @block.scalar
                    def _(act):
                        a = Chain(act, chain_s)
                        norm_act(act, 0)
                        act.wait_ge(loaded, 16 * 11)
                        norm_ev_act(act, 0, hT)
                        act.wait_ge(S["exin"], 1)
                        a(act.activation(e1, e1, ACT.Exp, scale=-1.0))
                        act.activation(e1, e1, ACT.Ln, bias=ones[:, 0:1]).then_inc(S["exout"], 1)

                        def proj_evac(u, g, t):
                            act.wait_ge(S["proj_mm"], u + 1)
                            dst = {3: tok[:, t, 512:1024], 4: p[:, t, 1536:2048], 6: p[:, t, 2048:2560],
                                   5: vaug[:, t, :, 0:MLD]}.get(g)
                            if dst is None:
                                dst = p[:, t, g * 512:(g + 1) * 512]
                            src = PS[:, u % 2, :]
                            if g == 5:
                                src = src.rearrange("p (h d) -> p h d", h=4)
                            act.activation(dst, src, ACT.Copy).then_inc(S["proj_ev"], 1)

                        u = 0
                        for g in range(3):
                            for t in range(T):
                                proj_evac(u, g, t)
                                u += 1
                                if g == 0:
                                    act.wait_ge(S["proj_ev"], u)
                                    act.activation(nq[:, t * 512:(t + 1) * 512], p[:, t, 0:512], ACT.Square).then_inc(S["sq_ready"], 1)
                                if g == 2:
                                    act.wait_ge(S["proj_ev"], u)
                                    act.activation(dq[:, t * 512:(t + 1) * 512], p[:, t, 768:1280], ACT.Square).then_inc(S["sq_ready"], 1)
                            if g == 0:
                                act.wait_ge(S["ctx_tr"], 1)
                                for j, idx in enumerate((2, 3, 6, 7)):
                                    act.activation(attT[:, idx, 384:512], PS[:, 4, j * P:(j + 1) * P], ACT.Copy).then_inc(S["ctx_ev"], 1)

                        def exps(i):
                            t, kind = BATCHES[i]
                            nk = keys_of(t)[1] - keys_of(t)[0]
                            act.wait_ge(S["nm_ready"], i + 1)
                            for m in range(4):
                                src = W1[:, m, 0:nk] if kind == "na" else PS[:, 2 + m, 0:nk]
                                act.activation(W2[:, m, 0:nk], src, ACT.Exp, bias=nm[:, m:m + 1],
                                               scale=1.0 if kind == "na" else DFD ** -0.5,
                                               accum_out=rs[:, m:m + 1]).then_inc(S["ex_ready"], 1)

                        def pt_evac(i):
                            t, kind = BATCHES[i]
                            nk = keys_of(t)[1] - keys_of(t)[0]
                            for m in range(first_map[i], first_map[i + 1]):
                                act.wait_ge(S["pt_mm"], m + 1)
                                if m >= 2:
                                    act.wait_ge(S["pv_mm"], m - 1)
                                act.activation(PT[:, m % 2, 0:nk], PS[:, 6 + m % 2, 0:nk], ACT.Copy).then_inc(S["pt_ev"], 1)

                        for i, (g, t) in enumerate(UNITS):
                            proj_evac(u, g, t)
                            u += 1
                            b = i - LATE
                            if b == -1:
                                act.wait_ge(S["exin"], 2)
                                act.activation(arg, arg, ACT.Exp).then_inc(S["exout"], 1)
                                act.wait_ge(S["exin"], 3)
                                act.activation(lamt[:, 2:4], lamt[:, 0:2], ACT.Exp).then_inc(S["exout"], 1)
                                for t2 in range(T):
                                    act.wait_ge(S["att_tr"], t2 + 1)
                                    for j in range(2):
                                        act.activation(attT[:, 4 * j:4 * j + 4, t2 * P:(t2 + 1) * P],
                                                       PS[:, 2 + 2 * (t2 % 2) + j, :].rearrange("p (c n) -> p c n", c=4),
                                                       ACT.Copy).then_inc(S["att_ev"], 1)
                            if 0 <= b < len(BATCHES):
                                pt_evac(b)
                            if 0 <= b + 1 < len(BATCHES):
                                exps(b + 1)
                        for t in range(T):
                            act.wait_ge(S["mqk_tr"], t + 1)
                            for j in range(2):
                                act.activation(hT[:, 4 * j:4 * j + 4, t * P:(t + 1) * P],
                                               PS[:, 2 + 2 * t + j, :].rearrange("p (c n) -> p c n", c=4),
                                               ACT.Copy, scale=MLD ** -0.5 if j else 1.0).then_inc(S["mqk_ev"], 1)
                        for t in range(T):
                            act.wait_ge(S["st_mm"], t + 1)
                            act.activation(ST[:, t, :], PS[:, t, :], ACT.Copy).then_inc(S["st_ev"], 1)
                        mo = p[:, :, 2048:2560]
                        act.activation(mo, mo, ACT.Sigmoid).then_inc(S["sig_e"], 1)

                        def squares(o):
                            t = OUT_ORDER[o]
                            act.wait_ge(S["ml_done"], o + 1)
                            for h in range(MLH):
                                ins = act.activation(nq[:, o * 512 + h * P:o * 512 + (h + 1) * P], mlh[:, t, h * P:(h + 1) * P], ACT.Square,
                                                     accum_out=ms2[:, 4 * o + h:4 * o + h + 1])
                                if h < MLH - 1:
                                    ins.then_inc(S["sq_part"], 1)
                            ins.then_inc(S["sq_ready"], 1)

                        def mixed(o):
                            t = OUT_ORDER[o]
                            act.wait_ge(S["mix_tr"], o + 1)
                            for half in range(2):
                                act.activation(hT[:, 4 * half:4 * half + 4, t * P:(t + 1) * P],
                                               PS[:, 1 + half, :].rearrange("p (c n) -> p c n", c=4), ACT.Copy).then_inc(S["mixT"], 1)

                        for i in range(6):
                            act.wait_ge(S["d_ready"], i + 1)
                            act.activation(X[i % 2], X[i % 2], ACT.Exp, scale=-1.0).then_inc(S["e_ready"], 1)
                            if i == 2:
                                squares(0)
                        mixed(0)
                        squares(1)
                        squares(2)
                        mixed(1)
                        mixed(2)

                    @block.tensor
                    def _(pe):
                        n = 0

                        def slot(c, n0, n1):
                            return ring[:, n % NSA, c * 512 + n0:c * 512 + n1]

                        norm_pe(pe)
                        pe.wait_ge(S["hT_s"], 4 * T)
                        pe.wait_ge(S["hT_v"], 4 * T)
                        pe.wait_ge(landed[0], 16)
                        for t in range(T):
                            for k in range(KC):
                                mm = pe.matmul(PS[:, 4, t * 16:(t + 1) * 16], hT[:, k, t * P:(t + 1) * P],
                                               ring[:, 0, k * 16:(k + 1) * 16], start=(k == 0), stop=(k == KC - 1))
                            if t < T - 1:
                                continue
                            mm.then_inc(S["tail_mm"], 1)
                        pe.wait_ge(S["tail_mm"], 1)
                        pe.sem_inc(slot_used, 1)
                        n = 1

                        def project(u, t, last_chunk):
                            nonlocal n
                            if u >= 2:
                                pe.wait_ge(S["proj_ev"], u - 1)
                            for half in range(2):
                                s = (n + half) % NSA
                                pe.wait_ge(landed[s], 16 * ((n + half) // NSA + 1))
                                for c in range(4):
                                    k = half * 4 + c
                                    mm = pe.matmul(PS[:, u % 2, :], hT[:, k, t * P:(t + 1) * P],
                                                   ring[:, s, c * 512:(c + 1) * 512], start=(k == 0), stop=(k == 7))
                                if last_chunk and half == 0:
                                    mm.then_inc(slot_used, 1)
                            mm.then_inc(S["proj_mm"], 1)
                            if last_chunk:
                                pe.wait_ge(S["proj_mm"], u + 1)
                                pe.sem_inc(slot_used, 1)
                                n += 2

                        u = 0
                        for g in range(3):
                            for t in range(T):
                                project(u, t, t == T - 1)
                                u += 1
                            if g == 0:
                                pe.wait_ge(loaded2, 16 * 10)
                                pe.wait_ge(S["exin"], 1)
                                for j, src in enumerate((ckv[:, 0, 0:P], ckv[:, 0, P:256], ckv[:, 2, 0:P], ckv[:, 2, P:256])):
                                    mm = pe.transpose(PS[:, 4, j * P:(j + 1) * P], src, ident)
                                mm.then_inc(S["ctx_tr"], 1)
                                pe.wait_ge(S["lf_ready"], 1)
                                for t in range(T):
                                    for q in range(4):
                                        mm = pe.transpose(PS[0:4, 5 + t, q * P:(q + 1) * P], gt[:, t, 4 * q:4 * q + 4], ident)
                                    mm.then_inc(S["rows_tr"], 1)
                            if g == 1:
                                pe.wait_ge(S["rows_v"], 1)
                                for q in range(3):
                                    for t in range(T):
                                        for d in range(2):
                                            src = (R[:, t, d, 0, :], R[:, t, d, 1, :], brow[:, t, d, :])[q]
                                            o = (q * 6 + 2 * t + d) * 4
                                            pe.transpose(PS[:, 5, o:o + 4], src, ident[0:4, 0:4])
                                pe.matmul(PS[:, 5, 128:176], ones[0:4, :], sm[0:4, 412:460], start=True, stop=True).then_inc(S["cols_mm"], 1)

                        def scores(i):
                            t, kind = BATCHES[i]
                            for m in (3, 2, 1, 0):
                                q, k = aps_of(BATCHES[i])[m]
                                if m == 0 and i:
                                    pe.wait_ge(S["pv_ev"], i)
                                mm = pe.matmul(PS[:, 2 + m, 0:k.shape[1]], q, k, start=True, stop=True)
                            mm.then_inc(S["sc_mm"], 1)

                        def weigh(i):
                            t, kind = BATCHES[i]
                            nc_ = 1 if t == 0 else 3
                            f = first_map[i]
                            nm_ = n_maps(BATCHES[i])

                            def turn(j):
                                m = f + j
                                if m >= 2:
                                    pe.wait_ge(S["pt_ev"], m - 1)
                                if kind == "na":
                                    pe.wait_ge(S["ex_ready"], 4 * i + j + 1)
                                else:
                                    pe.wait_ge(S["w_ready"], 2 * sum(b[1] != "na" for b in BATCHES[:i]) + j + 1)
                                src = (W2 if kind == "na" else W1)[:, j, :]
                                for c in range(nc_):
                                    mm = pe.transpose(PS[:, 6 + m % 2, c * P:(c + 1) * P], src[:, c * P:(c + 1) * P], ident)
                                mm.then_inc(S["pt_mm"], 1)

                            def product(j):
                                m = f + j
                                if j == 0:
                                    pe.wait_ge(S["ex_ready"], 4 * i + 4)
                                pe.wait_ge(S["pt_ev"], m + 1)
                                for c, val in enumerate(values_of(BATCHES[i], j)):
                                    mm = pe.matmul(PS[:, 2, j * 64:(j + 1) * 64], PT[:, m % 2, c * P:(c + 1) * P], val,
                                                   start=(c == 0), stop=(c == nc_ - 1))
                                mm.then_inc(S["pv_mm"], 1)

                            turn(0)
                            for j in range(nm_):
                                if j + 1 < nm_:
                                    turn(j + 1)
                                product(j)

                        for i, (g, t) in enumerate(UNITS):
                            project(u, t, t == T - 1)
                            u += 1
                            b = i - LATE
                            if b == -1:
                                for t2 in range(T):
                                    pe.wait_ge(S["qk_ready"], t2 + 1)
                                    if t2 == 2:
                                        pe.wait_ge(S["att_ev"], 2)
                                    for j in range(2):
                                        for c in range(4):
                                            at = j * 768 + c * P
                                            mm = pe.transpose(PS[:, 2 + 2 * (t2 % 2) + j, c * P:(c + 1) * P], p[:, t2, at:at + P], ident)
                                    mm.then_inc(S["att_tr"], 1)
                                pe.wait_ge(S["att_ev"], 6)
                                pe.wait_ge(S["ctx_ev"], 4)
                            if 0 <= b < len(BATCHES):
                                weigh(b)
                            if 0 <= b + 1 < len(BATCHES):
                                scores(b + 1)
                        pe.wait_ge(S["pv_ev"], len(BATCHES))
                        pe.wait_ge(S["proj_ev"], 21)
                        for t in range(T):
                            for j in range(2):
                                for h in range(MLH):
                                    src = tok[:, t, 512 + h * P:512 + (h + 1) * P] if j == 0 else p[:, t, 1536 + h * P:1536 + (h + 1) * P]
                                    mm = pe.transpose(PS[:, 2 + 2 * t + j, h * P:(h + 1) * P], src, ident)
                            mm.then_inc(S["mqk_tr"], 1)
                        for t in range(T):
                            pe.wait_ge(S["mqk_ev"], 2 * (t + 1))
                            for h in range(MLH):
                                mm = pe.matmul(PS[:, t, h * P:(h + 1) * P], hT[:, 4 + h, t * P:(t + 1) * P],
                                               hT[:, h, t * P:(t + 1) * P], start=True, stop=True)
                            mm.then_inc(S["st_mm"], 1)

                        def spread(i):
                            t, d = ML_ORDER[i]
                            if i >= 2:
                                pe.wait_ge(S["mb_free"], i - 1)
                            for h in range(MLH):
                                mm = pe.matmul(PS[:, 3 + i % 2, h * P:(h + 1) * P], tab[0:4, T_SEL + h * P:T_SEL + (h + 1) * P],
                                               R[:, t, d, 1, :], start=True, stop=True)
                            mm.then_inc(S["mb_mm"], 1)

                        def turn_mixed(o):
                            t = OUT_ORDER[o]
                            pe.wait_ge(S["mix_ready"], o + 1)
                            if o:
                                pe.wait_ge(S["mixT"], 2 * o)
                            else:
                                pe.wait_ge(S["c_ready"], 4)
                            for k in range(KC):
                                mm = pe.transpose(PS[:, 1 + k // 4, (k % 4) * P:(k % 4 + 1) * P], tok[:, t, k * P:(k + 1) * P], ident)
                            mm.then_inc(S["mix_tr"], 1)

                        def project_out(o, j):
                            t = OUT_ORDER[o]
                            pe.wait_ge(S["mixT"], 2 * (o + 1))
                            if o:
                                pe.wait_ge(S["x_done"], 2 * (o - 1) + j + 1)
                            else:
                                pe.wait_ge(S["mb_free"], 5 + j)
                            for half in range(2):
                                m = n + 2 * j + half
                                pe.wait_ge(landed[m % NSA], 16 * (m // NSA + 1))
                                for c in range(4):
                                    k = half * 4 + c
                                    mm = pe.matmul(PS[:, 3 + j, :], hT[:, k, t * P:(t + 1) * P],
                                                   ring[:, m % NSA, c * 512:(c + 1) * 512], start=(k == 0), stop=(k == 7))
                            mm.then_inc(S["out_mm"], 1)

                        pe.wait_ge(S["st_ev"], T)
                        spread(0)
                        for i, (t, d) in enumerate(ML_ORDER):
                            if i + 1 < 6:
                                spread(i + 1)
                            if i:
                                pe.wait_ge(S["num_ev"], i)
                            if t:
                                if i >= 4:
                                    pe.wait_ge(S["c_ready"], i - 1)
                                for h in range(MLH):
                                    b = (7, 0)[h // 2]
                                    pe.matmul(PS[:, b, (h % 2) * 129:(h % 2) * 129 + 129], hT[:, h, t * P:(t + 1) * P],
                                              Caug[:, 4 * d + h, :], start=True, stop=True)
                            pe.wait_ge(S["s_ready"], i + 1)
                            for h in range(MLH):
                                mm = pe.matmul(PS[:, 5 + h // 2, (h % 2) * 129:(h % 2) * 129 + 129], num[:, h, 0:P],
                                               vaug[:, t, h, :], start=True, stop=True)
                            mm.then_inc(S["num_mm"], 1)
                            if i < 4:
                                if i:
                                    pe.wait_ge(S["c_ready"], i)
                                pe.wait_ge(S["wk_ready"], i + 1)
                                for h in range(MLH):
                                    mm = pe.matmul(PS[:, 1 + h // 2, (h % 2) * 129:(h % 2) * 129 + 129], wks[i % 2][:, h * P:(h + 1) * P],
                                                   vaug[:, t, h, :], start=True, stop=True)
                                mm.then_inc(S["upd_mm"], 1)
                            if i == 4:
                                turn_mixed(0)
                                project_out(0, 0)
                        project_out(0, 1)
                        for o in (1, 2):
                            turn_mixed(o)
                            for j in range(2):
                                project_out(o, j)

                    @block.vector
                    def _(dve):
                        v = Chain(dve, chain_v)
                        norm_dve(dve)
                        dve.wait_ge(loaded, 16 * 11)
                        norm_ev_dve(dve, 0, hT)
                        dve.memset(zrow, 0.0).then_inc(chain_v, 1)
                        v.n += 1
                        dve.memset(vaug[:, :, :, MLD], 1.0).then_inc(chain_v, 1)
                        v.n += 1
                        dve.wait_ge(S["tail_mm"], 1)
                        v(dve.tensor_tensor(gt, PS[:, 4, 0:48].rearrange("p (t g) -> p t g", t=T),
                                            prm[:, None, B_GB:B_GB + 16].to_broadcast([P, T, 16]), ALU.add))
                        f = gt.rearrange("p t (d k h) -> p t d k h", d=2, k=2)[:, :, :, 1, :]
                        dve.scalar_tensor_tensor(e1, f, -1.0, f, ALU.mult, ALU.max).then_inc(S["exin"], 1)
                        v(dve.tensor_scalar(e2, f, 0.0, None, ALU.min))
                        dve.wait_ge(S["exout"], 1)
                        dve.tensor_tensor(f, e2, e1, ALU.subtract).then_inc(S["lf_ready"], 1)
                        lam = prm[:, B_LAM:B_LAM + 128].rearrange("p (a b d) -> p a b d", a=2, b=2)
                        v(dve.tensor_tensor(lam[:, :, 0, :], lam[:, :, 0, :], lam[:, :, 1, :], ALU.mult))
                        v(dve.tensor_reduce(lamt[:, 0:2], lam[:, :, 0, :], AX.X, ALU.add))
                        v(dve.tensor_copy(small[:, 102:104], tab[:, bass.ds(T_LAM + 2 * l, 2)]))
                        v(dve.tensor_scalar(prm[:, B_SUB:B_SUB + 64], prm[:, B_SUB:B_SUB + 64], small[:, 103:104], None, ALU.mult))
                        for t in range(T):
                            dve.wait_ge(S["rows_tr"], t + 1)
                            v(dve.tensor_copy(R[:, t].rearrange("p d k n -> p (d k n)"), PS[0:4, 5 + t, :]))
                        v(dve.memset(scal, 0.0))
                        v(dve.tensor_copy(scal[:, 2, 0:1], m0[:, 0:1]))
                        v(dve.tensor_copy(scal[:, 5, 0:1], m0[:, 1:2]))
                        for t, d in ML_ORDER:
                            td, e = 2 * t + d, last(d)
                            way = slice(None, None, -1) if d else slice(None)
                            i_, f_, b_ = R[:, t, d, 0, :], R[:, t, d, 1, :], brow[:, t, d, :]
                            v(dve.tensor_tensor_scan(b_[:, way], ones[0:4, :], f_[:, way], 0.0, ALU.mult, ALU.add))
                            v(dve.tensor_tensor(i_, i_, b_, ALU.subtract))
                            v(dve.tensor_tensor_scan(f_[:, way], zrow, i_[:, way], scal[:, td, 0:1], ALU.add, ALU.max))
                            v(dve.tensor_copy(scal[:, td, 1:2], f_[:, e:e + 1]))
                            follow = {(0, 0): mout[:, 0:1], (0, 1): mout[:, 1:2], (1, 0): scal[:, 4, 0:1],
                                      (2, 1): scal[:, 3, 0:1]}.get((t, d))
                            if follow is not None:
                                v(dve.tensor_tensor(follow, b_[:, e:e + 1], f_[:, e:e + 1], ALU.add))
                        dve.tensor_tensor(diag, sm[0:4, 400:412, None].to_broadcast([4, 12, 4]),
                                          cst[0:4, None, C_ID:C_ID + 4].to_broadcast([4, 12, 4]), ALU.mult).then_inc(S["rows_v"], 1)
                        dve.wait_ge(S["cols_mm"], 1)
                        v(dve.tensor_copy(sm[:, 96:168], PS[:, 5, 0:72]))
                        v(dve.tensor_copy(sm[:, 168:216], PS[:, 5, 128:176]))
                        dve.wait_ge(S["sq_ready"], 3)
                        v(dve.tensor_reduce(ms[:, 0:24], nq.rearrange("p (g d) -> p g d", d=NAD), AX.X, ALU.add))
                        dve.tensor_scalar(ms[:, 0:24], ms[:, 0:24], 1.0 / NAD, EPS, ALU.mult, ALU.add).then_inc(S["ms_ready"], 1)
                        bv = bias[:, :, :, :].rearrange("p t h (j k) -> p (t h j) k", k=64)
                        dve.wait_ge(loaded2, 16 * 10)
                        v(dve.tensor_tensor(bv, bv, tab[:, None, T_COL:T_COL + 64].to_broadcast([P, 32, 64]), ALU.add))
                        dve.wait_ge(S["r_ready"], 1)
                        for t in range(T):
                            na = p[:, t, 0:512].rearrange("p (g d) -> p g d", d=NAD)
                            v(dve.tensor_tensor(na, na, ms[:, 8 * t:8 * t + 8, None].to_broadcast([P, 8, NAD]), ALU.mult))
                            na = p[:, t, 0:512].rearrange("p (a h d) -> p a h d", a=2, h=4)
                            gn_ = prm[:, B_NAG:B_NAG + 128].rearrange("p (a d) -> p a d", a=2)
                            v(dve.tensor_tensor(na, na, gn_[:, :, None, :].to_broadcast([P, 2, 4, NAD]), ALU.mult))
                        dve.wait_ge(S["sq_ready"], 6)
                        v(dve.tensor_reduce(ms[:, 24:72], dq.rearrange("p (g d) -> p g d", d=DFD), AX.X, ALU.add))
                        dve.tensor_scalar(ms[:, 24:72], ms[:, 24:72], 1.0 / DFD, EPS, ALU.mult, ALU.add).then_inc(S["ms_ready"], 1)
                        dve.wait_ge(S["r_ready"], 2)
                        for t in range(T):
                            df = p[:, t, 768:1280].rearrange("p (g d) -> p g d", d=DFD)
                            v(dve.tensor_tensor(df, df, ms[:, 24 + 16 * t:40 + 16 * t, None].to_broadcast([P, 16, DFD]), ALU.mult))
                            df = p[:, t, 768:1280].rearrange("p (a h d) -> p a h d", a=2, h=8)
                            gd = prm[:, B_DFG:B_DFG + 64].rearrange("p (a d) -> p a d", a=2)
                            ins = dve.tensor_tensor(df, df, gd[:, :, None, :].to_broadcast([P, 2, 8, DFD]), ALU.mult)
                            if t == 0:
                                ins.then_inc(S["qk_ready"], 1)
                                continue
                            v(ins)
                            co, si = T_COS + (t - 1) * DFD, T_SIN + (t - 1) * DFD
                            xr = p[:, t, 768:1280].rearrange("p (g r s f) -> p g r s f", r=2, s=2, f=8)
                            yr = wkr = tmp.rearrange("p a b -> p (a b)")[:, 0:512].rearrange("p (g r s f) -> p g r s f", r=2, s=2, f=8)
                            for s_ in range(2):
                                sn = tab[:, si:si + DFD].rearrange("p (r s f) -> p r s f", r=2, s=2)[:, None, :, s_, :]
                                v(dve.tensor_tensor(yr[:, :, :, s_, :], xr[:, :, :, 1 - s_, :], sn.to_broadcast([P, 16, 2, 8]), ALU.mult))
                            df = p[:, t, 768:1280].rearrange("p (g d) -> p g d", d=DFD)
                            v(dve.tensor_tensor(df, df, tab[:, None, co:co + DFD].to_broadcast([P, 16, DFD]), ALU.mult))
                            dve.tensor_tensor(p[:, t, 768:1280], p[:, t, 768:1280], tmp.rearrange("p a b -> p (a b)")[:, 0:512],
                                              ALU.add).then_inc(S["qk_ready"], 1)
                        mprev, mlast = bcs[:, :, 0, :], bcs[:, :, 1, :]
                        c3 = cols.rearrange("p q (n h) -> p q n h", h=4)
                        g3 = arg.rearrange("p q (n h) -> p q n h", h=4)
                        v(dve.scalar_tensor_tensor(arg[:, 0, :], cols[:, 2, :], -1.0, cols[:, 1, :], ALU.mult, ALU.subtract))
                        v(dve.tensor_tensor(g3[:, 1], mprev, c3[:, 1], ALU.subtract))
                        v(dve.tensor_tensor(g3[:, 2], c3[:, 0], mlast, ALU.subtract))
                        dve.tensor_tensor(g3[:, 3], mprev, mlast, ALU.subtract).then_inc(S["exin"], 1)
                        dve.wait_ge(S["exout"], 2)
                        v(dve.tensor_scalar(arg[:, 2, :], arg[:, 2, :], MLD ** -0.5, None, ALU.mult))
                        dve.sem_inc(S["exin"], 1)
                        dve.wait_ge(S["exout"], 3)
                        v(dve.tensor_tensor(lamt[:, 0:1], lamt[:, 3:4], lamt[:, 2:3], ALU.subtract))
                        v(dve.tensor_tensor(nlam, lamt[:, 0:1], small[:, 102:103], ALU.subtract))

                        def reduce_scores(i):
                            t, kind = BATCHES[i]
                            nk = keys_of(t)[1] - keys_of(t)[0]
                            dve.wait_ge(S["sc_mm"], i + 1)
                            if kind == "na":
                                if t:
                                    v(dve.scalar_tensor_tensor(W1[:, :, 0:256], PS[:, 2:6, 0:256], NAD ** -0.5, bias[:, t - 1], ALU.mult, ALU.add))
                                    v(dve.tensor_scalar(W1[:, :, 256:384], PS[:, 2:6, 256:384], NAD ** -0.5, None, ALU.mult))
                                else:
                                    v(dve.tensor_scalar(W1[:, :, 0:P], PS[:, 2:6, 0:P], NAD ** -0.5, None, ALU.mult))
                                dve.tensor_reduce(nm, W1[:, :, 0:nk], AX.X, ALU.max, negate=True).then_inc(S["nm_ready"], 1)
                            else:
                                v(dve.tensor_reduce(nm, PS[:, 2:6, 0:nk], AX.X, ALU.max, negate=True))
                                dve.tensor_scalar(nm, nm, DFD ** -0.5, None, ALU.mult).then_inc(S["nm_ready"], 1)

                        def combine(i):
                            t, kind = BATCHES[i]
                            nk = keys_of(t)[1] - keys_of(t)[0]
                            dve.wait_ge(S["ex_ready"], 4 * i + 4)
                            v(dve.reciprocal(rr, rs))
                            if kind == "na":
                                return
                            odd = rr.rearrange("p (h a) -> p h a", a=2)[:, :, 1]
                            v(dve.tensor_scalar(odd, odd, nlam, None, ALU.mult))
                            for j in range(2):
                                v(dve.tensor_scalar(W2[:, 2 * j + 1, 0:nk], W2[:, 2 * j + 1, 0:nk], rr[:, 2 * j + 1:2 * j + 2], None, ALU.mult))
                                dve.scalar_tensor_tensor(W1[:, j, 0:nk], W2[:, 2 * j, 0:nk], rr[:, 2 * j:2 * j + 1],
                                                         W2[:, 2 * j + 1, 0:nk], ALU.mult, ALU.add).then_inc(S["w_ready"], 1)

                        def outputs(i):
                            t, kind = BATCHES[i]
                            dve.wait_ge(S["pv_mm"], first_map[i + 1])
                            if kind == "na":
                                dve.tensor_tensor(tok[:, t, 0:256].rearrange("p (h d) -> p h d", h=4),
                                                  PS[:, 2, 0:256].rearrange("p (h d) -> p h d", h=4),
                                                  rr[:, :, None].to_broadcast([P, 4, 64]), ALU.mult).then_inc(S["pv_ev"], 1)
                            else:
                                at = 256 + 128 * int(kind[2])
                                dve.tensor_copy(tok[:, t, at:at + 128], PS[:, 2, 0:128]).then_inc(S["pv_ev"], 1)

                        for i in range(len(BATCHES)):
                            reduce_scores(i)
                            combine(i)
                            outputs(i)
                        dve.wait_ge(S["pv_ev"], len(BATCHES))
                        do = tok[:, :, 256:512].rearrange("p t (h d) -> p t h d", h=4)
                        sq = nq[:, 0:768].rearrange("p (t h d) -> p t h d", t=T, h=4)
                        v(dve.tensor_tensor(sq, do, do, ALU.mult))
                        v(dve.tensor_reduce(ms2, nq[:, 0:768].rearrange("p (g d) -> p g d", d=64), AX.X, ALU.add))
                        dve.tensor_scalar(ms2, ms2, 1.0 / DFV, EPS, ALU.mult, ALU.add).then_inc(S["ms_ready"], 1)
                        dve.wait_ge(S["r_ready"], 3)
                        v(dve.tensor_tensor(do, do, ms2.rearrange("p (t h) -> p t h", t=T)[:, :, :, None].to_broadcast([P, T, 4, 64]), ALU.mult))
                        do12 = [tok[:, t, 256:512].rearrange("p (h d) -> p h d", h=4) for t in range(T)]
                        for t in range(T):
                            v(dve.tensor_tensor(do12[t], do12[t], prm[:, None, B_SUB:B_SUB + 64].to_broadcast([P, 4, 64]), ALU.mult))
                        seen = set()
                        two = lambda b0, n=129: PS[:, b0:b0 + 2, 0:258].rearrange("p b (h e) -> p b h e", h=2)
                        n4 = num[:, :, :].rearrange("p (b h) e -> p b h e", b=2)
                        t4 = tmp[:, :, :].rearrange("p (b h) e -> p b h e", b=2)

                        def b4(ap):
                            return ap.rearrange("p (b h) -> p b h", b=2)[:, :, :, None].to_broadcast([P, 2, 2, 129])

                        def exponents(i):
                            t, d = ML_ORDER[i]
                            dve.wait_ge(S["mb_mm"], i + 1)
                            v(dve.tensor_tensor(X[i % 2], PS[:, 3 + i % 2, :].rearrange("p (h n) -> p h n", h=4),
                                                col4(0, 2 * t + d)[:, :, None].to_broadcast([P, 4, P]), ALU.subtract))
                            dve.sem_inc(S["mb_free"], 1)
                            mask = T_MF if d == 0 else T_MB
                            dve.tensor_tensor(X[i % 2], X[i % 2], tab[:, None, mask:mask + P].to_broadcast([P, 4, P]), ALU.max).then_inc(S["d_ready"], 1)

                        def finish(o):
                            t = OUT_ORDER[o]
                            dve.wait_ge(S["r_ready"], 4 + o)
                            dve.wait_ge(S["gate_ready"], o + 1)
                            for h in range(MLH):
                                at = slice(h * P, (h + 1) * P)
                                ins = dve.scalar_tensor_tensor(tok[:, t, 512 + h * P:512 + (h + 1) * P], mlh[:, t, at],
                                                               ms2[:, 4 * o + h:4 * o + h + 1], p[:, t, 2048 + h * P:2048 + (h + 1) * P],
                                                               ALU.mult, ALU.mult)
                            ins.then_inc(S["mix_ready"], 1)

                        def add_out(o, j):
                            t = OUT_ORDER[o]
                            n = 2 * o + j
                            dve.wait_ge(S["out_mm"], n + 1)
                            if n:
                                dve.wait_ge(S["x_done"], n)
                            v(dve.tensor_tensor(wk[:, :], PS[:, 3 + j, :], gate[:, min(t, 1), j * 512:(j + 1) * 512], ALU.mult))
                            xs = x[:, t, j * 512:(j + 1) * 512]
                            dve.tensor_tensor(xs, xs, wk[:, :], ALU.add).then_inc(S["x_done"], 1)

                        exponents(0)
                        for i, (t, d) in enumerate(ML_ORDER):
                            td = 2 * t + d
                            dve.wait_ge(S["e_ready"], i + 1)
                            dve.wait_ge(S["st_ev"], T)
                            dve.tensor_tensor(num[:, :, 0:P], X[i % 2], ST[:, t, :].rearrange("p (h n) -> p h n", h=4), ALU.mult).then_inc(S["s_ready"], 1)
                            if i + 1 < 6:
                                exponents(i + 1)
                            dve.wait_ge(S["num_mm"], i + 1)
                            if t:
                                for b, bank in enumerate((7, 0)):
                                    v(dve.tensor_tensor(t4[:, b], PS[:, bank, 0:258].rearrange("p (h e) -> p h e", h=2),
                                                        arg4(1, td)[:, 2 * b:2 * b + 2, None].to_broadcast([P, 2, 129]), ALU.mult))
                                v(dve.tensor_tensor(n4, two(5), t4, ALU.add))
                            else:
                                v(dve.tensor_copy(n4, two(5)))
                            dve.sem_inc(S["num_ev"], 1)
                            v(dve.scalar_tensor_tensor(den, num[:, :, MLD], -1.0, num[:, :, MLD], ALU.mult, ALU.max))
                            v(dve.tensor_tensor(den, den, arg4(0, td), ALU.max))
                            v(dve.reciprocal(den, den))
                            out = mlh[:, t, :].rearrange("p (h n) -> p h n", h=4)
                            r4 = den[:, :, None].to_broadcast([P, 4, P])
                            if t in seen:
                                v(dve.tensor_tensor(num[:, :, 0:P], num[:, :, 0:P], r4, ALU.mult))
                                v(dve.tensor_tensor(out, out, num[:, :, 0:P], ALU.add))
                            else:
                                v(dve.tensor_tensor(out, num[:, :, 0:P], r4, ALU.mult))
                            seen.add(t)
                            if i == FINISHED[t]:
                                dve.sem_inc(S["ml_done"], 1)
                            if i < 4:
                                dve.wait_ge(S["upd_mm"], i + 1)
                                if t == 0:
                                    dve.tensor_copy(Cp[:, 4 * d:4 * d + 4, :].rearrange("p (b h) e -> p b h e", b=2), two(1)).then_inc(S["c_ready"], 1)
                                else:
                                    C4 = Caug[:, 4 * d:4 * d + 4, :].rearrange("p (b h) e -> p b h e", b=2)
                                    dve.wait_ge(S["decayed"], i - 1)
                                    dve.tensor_tensor(C4, C4, two(1), ALU.add).then_inc(S["c_ready"], 1)
                            if i == 2:
                                finish(0)
                        finish(1)
                        add_out(0, 0)
                        add_out(0, 1)
                        finish(2)
                        for o in (1, 2):
                            for j in range(2):
                                add_out(o, j)
                        dve.wait_ge(S["x_done"], 6)
                end_section()
            if debug == "mix":
                with nc.Block() as block:
                    @block.sync
                    def _(sp):
                        sp.dma_start(O["dbg"].rearrange("(t p) d -> p t d", p=P), x[:, :, :]).then_inc(stored, 16)
                        sp.wait_ge(stored, 16)
                end_section()
                continue_ = None
            with ExitStack() as layer:
                acc = sb("acc", [P, T, D], ctx=layer)
                tokh = sb("tokh", [P, T, D], ctx=layer)
                tokl = sb("tokl", [P, T, D], ctx=layer)
                posm = sb("posm", [P, T, NE + 2], ctx=layer)
                wts = sb("wts", [P, T, NE + 2, 2], ctx=layer)

                with ExitStack() as sec:
                    tok = sb("tokB", [P, T, D], ctx=sec)
                    ring = sb("ringB", [P, 3, SLOTF], ctx=sec)
                    hT = sb("hTB", [P, KC, T * P], ctx=sec)
                    wr = sb("wr", [P, KC, NE], ctx=sec)
                    sg = sb("sg", [P, 2, DE], ctx=sec)
                    hid = sb("hid", [P, DE], ctx=sec)
                    hidT = sb("hidT", [P, 2, P], ctx=sec)
                    rt = sb("rt", [P, 8, T, NE], ctx=sec)
                    r8 = sb("r8", [P, T, 8], ctx=sec)
                    rem = sb("rem", [P, 8], ctx=sec)
                    br = sb("br", [P, NE], ctx=sec)
                    wfull = sb("wfull", [P, T, NE + 2], ctx=sec)
                    s_, sel, gtm, eq, cum, mask = (rt[:, i] for i in range(6))

                    with nc.Block() as block:
                        @block.sync
                        def _(sp):
                            sp.dma_start(wr[:, :, :], A["w_router"][l].rearrange("(c p) n -> p c n", p=P)).then_inc(loaded, 16)
                            for half in range(2):
                                rows = slice(half * 512, (half + 1) * 512)
                                dst = ring[:, half, :].rearrange("p (c w n) -> p c w n", c=4, w=2)
                                for w in range(2):
                                    sp.dma_start(dst[:, :, w, :], A[("w_sh1", "w_sh3")[w]][l, rows, :]
                                                 .rearrange("(c p) n -> p c n", p=P)).then_inc(landed[half], 16)
                            sp.dma_start(ring[:, 2, :].rearrange("p (c n) -> p c n", c=2),
                                         A["w_sh2"][l].rearrange("(c p) n -> p c n", p=P)).then_inc(landed[2], 16)
                            sp.dma_start(br[:, :], bcast(A["b_router"][l], NE)).then_inc(landed[3], 16)
                            for i in range(2):
                                sp.dma_start(gate[:, i, :], bcast(modd[l, i, 5 * D:6 * D], D)).then_inc(loaded2, 16)
                            sp.wait_ge(loaded2, 32)

                        @block.gpsimd
                        def _(pool):
                            norm_pool(pool, Chain(pool, chain_p))

                        @block.scalar
                        def _(act):
                            norm_act(act, 1)
                            norm_ev_act(act, 1, hT)
                            act.wait_ge(S["rt_mm"], 1)
                            act.activation(s_.rearrange("p t e -> p (t e)"), PS[:, 0, 0:T * NE], ACT.Exp, scale=-1.0).then_inc(S["rt_e"], 1)
                            for t in range(T):
                                act.wait_ge(S["sh_mm"], t + 1)
                                act.activation(sg[:, t % 2, :], PS[:, 2 + t % 2, 0:DE], ACT.Silu).then_inc(S["sh_silu"], 1)
                                act.wait_ge(S["sh_tr"], t + 1)
                                act.activation(hidT[:, :, :].rearrange("p a b -> p (a b)"), PS[:, 4, 0:256], ACT.Copy).then_inc(S["sh_trev"], 1)

                        @block.tensor
                        def _(pe):
                            norm_pe(pe)
                            pe.wait_ge(S["hT_s"], 4 * T)
                            pe.wait_ge(S["hT_v"], 4 * T)
                            pe.wait_ge(loaded, 16)
                            for t in range(T):
                                for k in range(KC):
                                    mm = pe.matmul(PS[:, 0, t * NE:(t + 1) * NE], hT[:, k, t * P:(t + 1) * P], wr[:, k, :],
                                                   start=(k == 0), stop=(k == KC - 1))
                            mm.then_inc(S["rt_mm"], 1)
                            for t in range(T):
                                for half in range(2):
                                    i = 2 * t + half
                                    if i >= 4:
                                        pe.wait_ge(S["back_ev"], i - 3)
                                    for c in range(4):
                                        mm = pe.transpose(PS[:, 4 + i % 4, c * P:(c + 1) * P], hT[:, 4 * half + c, t * P:(t + 1) * P], ident)
                                    mm.then_inc(S["back_tr"], 1)
                            def up(t):
                                if t >= 2:
                                    pe.wait_ge(S["sh_hid"], t - 1)
                                for half in range(2):
                                    pe.wait_ge(landed[half], 32)
                                    for c in range(4):
                                        k = 4 * half + c
                                        mm = pe.matmul(PS[:, 2 + t % 2, :], hT[:, k, t * P:(t + 1) * P], ring[:, half, c * 512:(c + 1) * 512],
                                                       start=(k == 0), stop=(k == 7))
                                mm.then_inc(S["sh_mm"], 1)

                            up(0)
                            pe.wait_ge(S["back_ev"], 2 * T)
                            pe.wait_ge(landed[2], 16)
                            for t in range(T):
                                if t + 1 < T:
                                    up(t + 1)
                                if t == 0:
                                    pe.wait_ge(S["mask_ready"], 1)
                                    for u in range(T):
                                        for w in range(u + 1):
                                            lhs = cst[:, C_TRIU:C_TRIU + P] if w == u else ones
                                            pe.matmul(PS[:, 1, u * NE:(u + 1) * NE], lhs, mask[:, w, :], start=(w == 0), stop=(w == u))
                                    for w in range(T):
                                        mm = pe.matmul(PS[:, 1, T * NE:(T + 1) * NE], ones, mask[:, w, :], start=(w == 0), stop=(w == T - 1))
                                    mm.then_inc(S["pos_mm"], 1)
                                pe.wait_ge(S["sh_hid"], t + 1)
                                for f in range(2):
                                    mm = pe.transpose(PS[:, 4, f * P:(f + 1) * P], hid[:, f * P:(f + 1) * P], ident)
                                mm.then_inc(S["sh_tr"], 1)
                                pe.wait_ge(S["sh_trev"], t + 1)
                                if t:
                                    pe.wait_ge(S["sh_done"], t)
                                for half in range(2):
                                    for f in range(2):
                                        mm = pe.matmul(PS[:, 5 + half, :], hidT[:, f, :], ring[:, 2, f * D + half * 512:f * D + (half + 1) * 512],
                                                       start=(f == 0), stop=(f == 1))
                                mm.then_inc(S["sh_down"], 1)

                        @block.vector
                        def _(dve):
                            v = Chain(dve, chain_v)
                            norm_dve(dve)
                            norm_ev_dve(dve, 1, hT)
                            for t in range(T):
                                for half in range(2):
                                    i = 2 * t + half
                                    at = slice(half * 512, (half + 1) * 512)
                                    dve.wait_ge(S["back_tr"], i + 1)
                                    v(round_high(dve, tokh[:, t, at], PS[:, 4 + i % 4, :]))
                                    dve.tensor_tensor(hi(tokl[:, t, at]), PS[:, 4 + i % 4, :], tokh[:, t, at], ALU.subtract).then_inc(S["back_ev"], 1)
                            dve.wait_ge(S["rt_e"], 1)
                            v(dve.tensor_scalar(s_, s_, 1.0, None, ALU.add))
                            v(dve.reciprocal(s_, s_))
                            dve.wait_ge(landed[3], 16)
                            v(dve.tensor_tensor(sel, s_, br[:, None, :].to_broadcast([P, T, NE]), ALU.add))
                            for t in range(T):
                                v(dve.max(r8[:, t, :], sel[:, t, :]))
                            thr = r8[:, :, TOPK - 1:TOPK].to_broadcast([P, T, NE])
                            v(dve.tensor_tensor(gtm, sel, thr, ALU.is_gt))
                            v(dve.tensor_tensor(eq, sel, thr, ALU.is_equal))
                            v(dve.tensor_reduce(rem[:, 0:T], gtm, AX.X, ALU.add))
                            v(dve.tensor_scalar(rem[:, 0:T], rem[:, 0:T], -1.0, float(TOPK), ALU.mult, ALU.add))
                            for t in range(T):
                                v(dve.tensor_tensor_scan(cum[:, t, :], ones[:, 0:NE], eq[:, t, :], 0.0, ALU.mult, ALU.add))
                            v(dve.tensor_tensor(cum, cum, rem[:, 0:T, None].to_broadcast([P, T, NE]), ALU.is_le))
                            v(dve.tensor_tensor(eq, eq, cum, ALU.mult))
                            dve.tensor_tensor(mask, gtm, eq, ALU.add).then_inc(S["mask_ready"], 1)
                            dve.wait_ge(S["mask_ready"], 1)
                            v(dve.memset(wfull[:, :, :], 0.0))
                            v(dve.memset(posm[:, :, :], -1.0))
                            v(dve.tensor_tensor(s_, s_, mask, ALU.mult))
                            v(dve.tensor_reduce(rem[:, 0:T], s_, AX.X, ALU.add))
                            v(dve.reciprocal(rem[:, 0:T], rem[:, 0:T]))
                            v(dve.tensor_scalar(rem[:, 0:T], rem[:, 0:T], ROUTED_SCALE, None, ALU.mult))
                            v(dve.tensor_tensor(wfull[:, :, 0:NE], s_, rem[:, 0:T, None].to_broadcast([P, T, NE]), ALU.mult))
                            v(round_high(dve, wts[:, :, :, 0], wfull[:, :, :]))
                            v(dve.tensor_tensor(hi(wts[:, :, :, 1]), wfull[:, :, :], wts[:, :, :, 0], ALU.subtract))

                            def gated(t):
                                dve.wait_ge(S["sh_silu"], t + 1)
                                if t:
                                    dve.wait_ge(S["sh_tr"], t)
                                dve.tensor_tensor(hid[:, :], PS[:, 2 + t % 2, 256:512], sg[:, t % 2, :], ALU.mult).then_inc(S["sh_hid"], 1)

                            for t in range(T):
                                if t == 0:
                                    dve.wait_ge(S["pos_mm"], 1)
                                    pos = PS[:, 1, 0:T * NE].rearrange("p (t e) -> p t e", t=T)
                                    v(dve.scalar_tensor_tensor(posm[:, :, 0:NE], pos, 1.0, mask, ALU.add, ALU.mult))
                                    v(dve.tensor_scalar(posm[:, :, 0:NE], posm[:, :, 0:NE], -1.0, None, ALU.add))
                                    v(dve.tensor_reduce(rem[:, 4:5], PS[:, 1, T * NE:(T + 1) * NE], AX.X, ALU.max))
                                    v(dve.tensor_scalar(rem[:, 5:6], rem[:, 4:5], float(SLOTS), 1.0, ALU.is_gt, ALU.add))
                                    v(dve.tensor_scalar(rem[:, 6:7], rem[:, 4:5], 2.0 * SLOTS, None, ALU.is_gt))
                                    v(dve.tensor_tensor(npass[:, :], rem[:, 5:6], rem[:, 6:7], ALU.add))
                                gated(t)
                                dve.wait_ge(S["sh_down"], t + 1)
                                dve.tensor_copy(acc[:, t, :].rearrange("p (b n) -> p b n", b=2), PS[:, 5:7, :]).then_inc(S["sh_done"], 1)
                            dve.wait_ge(S["sh_done"], T)
                    end_section()

                passes = nc.values_load(npass[0:1, 0:1], min_val=1, max_val=T)
                with ExitStack() as sec:
                    raw = sb("raw", [P, 3, SLOTF], ctx=sec)
                    high = sb("high", [P, 3, SLOTF], ctx=sec)
                    low = sb("low", [P, 3, SLOTF], ctx=sec)
                    Pb = sb("Pb", [P, 2, T, 2 * SLOTS], ctx=sec)
                    PTb = sb("PTb", [P, GROUP, T * P], ctx=sec)
                    hTe = sb("hTe", [P, 12, 2, 2 * SLOTS], ctx=sec)
                    idw = sb("idw", [P, 2, T, P + 2], ctx=sec)
                    gs = sb("gs", [P, 2], ctx=sec)
                    gparts = sb("gparts", [P, T, 2], ctx=sec)
                    sg = sb("sgC", [P, DE], ctx=sec)
                    hid = sb("hidC", [P, DE], ctx=sec)
                    hidT = sb("hidTC", [P, 2, 2, P], ctx=sec)
                    yh = sb("yh", [P, GROUP, D], ctx=sec)
                    yl = sb("yl", [P, GROUP, D], ctx=sec)
                    NG = NE // GROUP
                    LOADS = (32, 32, 16)
                    CV, CP = 3, 1

                    wcol = lambda c: bass.ds(c, 1)

                    SPREAD = ((1, 2, 1),) * (GROUP - 1) + ((2, 2, 0),)

                    def chunks(j, when):
                        first = sum(SPREAD[j][:when])
                        return range(first, first + SPREAD[j][when])

                    def block_of(pair, k):
                        return 4 * (pair % 2) + k if k < 4 else 4 + k

                    def cut_done(eng, e, k):
                        if k == 1:
                            eng.wait_ge(S["low_p"], e + 1 + CP)
                        else:
                            eng.wait_ge(S["low_v"], 2 * e + (1 if k == 0 else 2) + CV)

                    def products_done(eng, e, k):
                        eng.wait_ge(slot_used, 3 * e + k + 4)

                    with nc.Fori(0, passes) as _pass:
                        with nc.Block() as block:

                            @block.sync
                            def _(sp):
                                with sp.Fori(0, NG) as g:
                                    for j in range(GROUP):
                                        e = GROUP * g + j
                                        for k in range(3):
                                            cut_done(sp, e - 1, k)
                                            if k < 2:
                                                rows = slice(k * 512, (k + 1) * 512)
                                                dst = raw[:, k, :].rearrange("p (c w n) -> p c w n", c=4, w=2)
                                                for w in range(2):
                                                    sp.dma_start(dst[:, :, w, :], A[("w_exp1", "w_exp3")[w]][l, e, rows, :]
                                                                 .rearrange("(c p) n -> p c n", p=P)).then_inc(landed[k], 16)
                                            else:
                                                sp.dma_start(raw[:, k, :].rearrange("p (c n) -> p c n", c=2),
                                                             A["w_exp2"][l, e].rearrange("(c p) n -> p c n", p=P)).then_inc(landed[k], 16)

                            @block.gpsimd
                            def _(pool):
                                def rest(e):
                                    pool.wait_ge(S["cut_p"], e + 1)
                                    pool.tensor_tensor(hi(low[:, 1, :]), raw[:, 1, :], high[:, 1, :], ALU.subtract).then_inc(S["low_p"], 1)

                                pool.sem_inc(S["low_p"], CP)

                                def token_weights(b, e):
                                    if not isinstance(e, int):
                                        pool.wait_ge(S["pt_mm"], e - 1)
                                    pool.tensor_copy(hi(idw[:, b, :, P:P + 2]), wts[:, :, wcol(e), :].rearrange("p t o w -> p t (o w)")).then_inc(S["idw_ready"], 1)

                                for b in range(2):
                                    for c in range(T):
                                        ins = pool.tensor_copy(hi(idw[:, b, c, 0:P]), ident)
                                        if c < T - 1:
                                            ins.then_inc(S["id_part"], 1)
                                    ins.then_inc(S["id_part"], 1)
                                for b in range(2):
                                    if b == 0:
                                        pool.wait_ge(S["id_part"], 2 * T)
                                    token_weights(b, b)
                                rest(0)
                                rest(1)
                                with pool.Fori(1, NE // 2) as h:
                                    for b in range(2):
                                        e = 2 * h + b
                                        token_weights(b, e)
                                        rest(e)

                            @block.scalar
                            def _(act):
                                def take(pair, k, n):
                                    act.wait_ge(S["ga_mm"], n + 1)
                                    act.activation(hi(hTe[:, block_of(pair, k)].rearrange("p a n -> p (a n)")), PS[:, k % 2, :],
                                                   ACT.Copy).then_inc(S["ga_ev"], 1)

                                def turned(j, n):
                                    act.wait_ge(S["pt_mm"], n)
                                    got = PS[:, 4, 0:T * (P + 2)].rearrange("p (c n) -> p c n", c=T)
                                    act.activation(gparts[:, :, :], got[:, :, P:P + 2], ACT.Copy, accum_out=gs[:, j % 2:j % 2 + 1]).then_inc(S["gs_ev"], 1)
                                    act.activation(hi(PTb[:, j, :].rearrange("p (c n) -> p c n", c=T)), got[:, :, 0:P], ACT.Copy).then_inc(S["pt_ev"], 1)

                                def cut_down(e):
                                    act.wait_ge(landed[2], LOADS[2] * (e + 1))
                                    products_done(act, e - 1, 2)
                                    act.activation(hi(high[:, 2, :]), raw[:, 2, :], ACT.Copy).then_inc(S["cut_s"], 1)

                                def step(g, last=False):
                                    for j in range(GROUP):
                                        e = GROUP * g + j
                                        more = not (last and j == GROUP - 1)
                                        pair = j // 2 + 1
                                        k0 = 4 * (j % 2)
                                        n0 = 16 * g + 8 * pair + k0
                                        gathering = not (last and pair == 2)
                                        products_done(act, e, 1)
                                        act.activation(sg[:, :], PS[:, 2, 0:DE], ACT.Silu).then_inc(S["silu"], 1)
                                        if gathering:
                                            for i in chunks(j, 0):
                                                take(pair, k0 + i, n0 + i)
                                        if j < GROUP - 1:
                                            turned(j + 1, e + 2)
                                        act.wait_ge(S["ht_mm"], e + 1)
                                        act.activation(hi(hidT[:, 0, :, :].rearrange("p b n -> p (b n)")), PS[:, 3, 0:DE], ACT.Copy).then_inc(S["ht_ev"], 1)
                                        if gathering:
                                            for i in chunks(j, 1):
                                                take(pair, k0 + i, n0 + i)
                                        products_done(act, e, 2)
                                        act.activation(hi(yh[:, j, :].rearrange("p (b n) -> p b n", b=2)), PS[:, 5:7, :], ACT.Copy).then_inc(S["y_high"], 1)
                                        if gathering:
                                            for i in chunks(j, 2):
                                                take(pair, k0 + i, n0 + i)
                                        if more:
                                            cut_down(e + 1)
                                        if more and j == GROUP - 1:
                                            act.wait_ge(S["sc_mm"], 6 * g + 6)
                                            turned(0, e + 2)

                                for k in range(KC):
                                    take(0, k, k)
                                turned(0, 1)
                                act.wait_ge(landed[2], LOADS[2])
                                act.activation(hi(high[:, 2, :]), raw[:, 2, :], ACT.Copy).then_inc(S["cut_s"], 1)
                                with act.Fori(0, NG - 1) as g:
                                    step(g)
                                step(NG - 1, last=True)

                            @block.tensor
                            def _(pe):
                                pe.sem_inc(slot_used, 3)

                                def gather(pair, k, n):
                                    if isinstance(n, int) and n < 2:
                                        pass
                                    else:
                                        pe.wait_ge(S["ga_ev"], n - 1)
                                    for part, src in enumerate((tokh, tokl)):
                                        for c in range(T):
                                            mm = pe.matmul(PS[:, k % 2, part * 256:(part + 1) * 256], hi(src[:, c, k * P:(k + 1) * P]),
                                                           hi(Pb[:, pair % 2, c, :]), start=(c == 0), stop=(c == T - 1))
                                    mm.then_inc(S["ga_mm"], 1)

                                def turn(j, e):
                                    pe.wait_ge(S["pt_ev"], e + 1)
                                    pe.wait_ge(S["gs_ev"], e + 1)
                                    at = slice((j % 2) * SLOTS, (j % 2 + 1) * SLOTS)
                                    pe.wait_ge(S["idw_ready"], e + 1)
                                    for c in range(T):
                                        mm = pe.matmul(PS[:, 4, c * (P + 2):(c + 1) * (P + 2)], hi(Pb[:, j // 2, c, at]),
                                                       hi(idw[:, j % 2, c, :]), start=True, stop=True)
                                    mm.then_inc(S["pt_mm"], 1)

                                def three(out, ah, al, wh, wl, first, last):
                                    pe.matmul(out, hi(ah), hi(wh), start=first, stop=False)
                                    pe.matmul(out, hi(ah), hi(wl), start=False, stop=False)
                                    return pe.matmul(out, hi(al), hi(wh), start=False, stop=last)

                                def step(g, last=False):
                                    for j in range(GROUP):
                                        e = GROUP * g + j
                                        own = j // 2
                                        pair, k0 = own + 1, 4 * (j % 2)
                                        gathering = not (last and pair == 2)
                                        n0 = 16 * g + 8 * pair + k0
                                        at = slice((j % 2) * SLOTS, (j % 2 + 1) * SLOTS)
                                        for half in range(2):
                                            pe.wait_ge(S["ga_ev"], 16 * g + 8 * own + 4 * half + 4)
                                            cut_done(pe, e, half)
                                            for c in range(4):
                                                k = 4 * half + c
                                                w = slice(c * 512, (c + 1) * 512)
                                                h = hTe[:, block_of(own, k)]
                                                mm = three(PS[:, 2, :], h[:, 0, at], h[:, 1, at], high[:, half, w], low[:, half, w], k == 0, k == 7)
                                            mm.then_inc(slot_used, 1)
                                        if gathering:
                                            if j % 2 == 0:
                                                pe.wait_ge(S["pb_ready"], 2 * g + pair + 1)
                                            for i in chunks(j, 0):
                                                gather(pair, k0 + i, n0 + i)
                                        if j < GROUP - 1:
                                            turn(j + 1, e + 1)
                                        pe.wait_ge(S["hid_ready"], e + 1)
                                        if j == 0:
                                            pe.wait_ge(S["sc_ev"], 6 * g + 1)
                                        for f in range(2):
                                            mm = pe.transpose(PS[:, 3, f * P:(f + 1) * P], hid[:, f * P:(f + 1) * P], ident)
                                        mm.then_inc(S["ht_mm"], 1)
                                        if gathering:
                                            for i in chunks(j, 1):
                                                gather(pair, k0 + i, n0 + i)
                                        pe.wait_ge(S["hidT_low"], e + 1)
                                        pe.wait_ge(S["y_low"], e + 1)
                                        cut_done(pe, e, 2)
                                        for half in range(2):
                                            for f in range(2):
                                                w = slice(f * D + half * 512, f * D + (half + 1) * 512)
                                                mm = three(PS[:, 5 + half, :], hidT[:, 0, f, :], hidT[:, 1, f, :],
                                                           high[:, 2, w], low[:, 2, w], f == 0, f == 1)
                                        mm.then_inc(slot_used, 1)
                                        if gathering:
                                            for i in chunks(j, 2):
                                                gather(pair, k0 + i, n0 + i)
                                    def scatter(q, js):
                                        c, half = q // 2, q % 2
                                        for j in js:
                                            for yy in (yh, yl):
                                                mm = pe.matmul(PS[:, (7, 3)[q % 2], :], hi(PTb[:, j, c * P:(c + 1) * P]),
                                                               hi(yy[:, j, half * 512:(half + 1) * 512]),
                                                               start=(j == 0 and yy is yh), stop=(j == GROUP - 1 and yy is yl))
                                        if j == GROUP - 1:
                                            mm.then_inc(S["sc_mm"], 1)

                                    pe.wait_ge(S["pt_ev"], GROUP * g + GROUP + 1)
                                    pe.wait_ge(S["y_low"], GROUP * g + GROUP)
                                    for q in range(2):
                                        scatter(q, range(GROUP - 1))
                                    pe.wait_ge(S["y_low"], GROUP * g + GROUP + 1)
                                    for q in range(2):
                                        scatter(q, (GROUP - 1,))
                                    for q in range(2, 2 * T):
                                        pe.wait_ge(S["sc_ev"], 6 * g + q)
                                        scatter(q, range(GROUP))
                                    if not last:
                                        turn(0, GROUP * g + GROUP)

                                pe.wait_ge(S["pb_ready"], 1)
                                for k in range(KC):
                                    gather(0, k, k)
                                turn(0, 0)
                                with pe.Fori(0, NG - 1) as g:
                                    step(g)
                                step(NG - 1, last=True)

                            @block.vector
                            def _(dve):
                                for name in ("pt_ev", "gs_ev", "y_low", "sc_ev"):
                                    dve.sem_inc(S[name], 1)
                                dve.sem_inc(S["low_v"], CV)

                                def one_hots(b, e):
                                    for c in range(T):
                                        for i in range(2):
                                            ins = dve.tensor_scalar(hi(Pb[:, b, c, i * SLOTS:(i + 1) * SLOTS]), cst[:, C_IOTA:C_IOTA + P],
                                                                    posm[:, c, wcol(e + i)], None, ALU.is_equal)
                                    ins.then_inc(S["pb_ready"], 1)

                                def cut_high(e, k, first=False):
                                    dve.wait_ge(landed[k], LOADS[k] * (e + 1))
                                    if not first:
                                        products_done(dve, e - 1, k)
                                    round_high(dve, high[:, k, :], raw[:, k, :]).then_inc(S["cut_p" if k else "cut_v"], 1)

                                def cut_low(e, k):
                                    dve.wait_ge(S["cut_s" if k else "cut_v"], e + 1)
                                    dve.tensor_tensor(hi(low[:, k, :]), raw[:, k, :], high[:, k, :], ALU.subtract).then_inc(S["low_v"], 1)

                                def step(g, last=False):
                                    for j in range(GROUP):
                                        e = GROUP * g + j
                                        b = j % 2
                                        more = not (last and j == GROUP - 1)
                                        dve.wait_ge(S["silu"], e + 1)
                                        dve.wait_ge(S["gs_ev"], e + 2)
                                        dve.scalar_tensor_tensor(hid[:, :], PS[:, 2, DE:2 * DE], gs[:, b:b + 1], sg[:, :],
                                                                 ALU.mult, ALU.mult).then_inc(S["hid_ready"], 1)
                                        if more:
                                            cut_high(e + 1, 0)
                                        dve.wait_ge(S["ht_ev"], e + 1)
                                        dve.tensor_tensor(hi(hidT[:, 1, :, :].rearrange("p b n -> p (b n)")), PS[:, 3, 0:DE],
                                                          hidT[:, 0, :, :].rearrange("p b n -> p (b n)"), ALU.subtract).then_inc(S["hidT_low"], 1)
                                        if more:
                                            cut_high(e + 1, 1)
                                            cut_low(e + 1, 0)
                                        dve.wait_ge(S["y_high"], e + 1)
                                        dve.tensor_tensor(hi(yl[:, j, :].rearrange("p (b n) -> p b n", b=2)), PS[:, 5:7, :],
                                                          yh[:, j, :].rearrange("p (b n) -> p b n", b=2), ALU.subtract).then_inc(S["y_low"], 1)
                                        if j % 2 and not last:
                                            dve.wait_ge(S["pt_mm"], e + 1)
                                            one_hots(j // 2, e + 3)
                                        if j < GROUP - 1:
                                            cut_low(e + 1, 2)
                                    for q in range(2 * T):
                                        c, half = q // 2, q % 2
                                        dve.wait_ge(S["sc_mm"], 6 * g + q + 1)
                                        at = acc[:, c, half * 512:(half + 1) * 512]
                                        dve.tensor_tensor(at, at, PS[:, (7, 3)[q % 2], :], ALU.add).then_inc(S["sc_ev"], 1)
                                    if not last:
                                        cut_low(GROUP * g + GROUP, 2)

                                one_hots(0, 0)
                                one_hots(1, 2)
                                for k in range(2):
                                    cut_high(0, k, first=True)
                                cut_low(0, 0)
                                cut_low(0, 2)
                                with dve.Fori(0, NG - 1) as g:
                                    step(g)
                                step(NG - 1, last=True)
                                dve.wait_ge(S["pb_ready"], NE // 2)
                                dve.tensor_scalar(posm[:, :, 0:NE], posm[:, :, 0:NE], -float(SLOTS), None, ALU.add).then_inc(chain_v, 1)
                                dve.wait_ge(chain_v, 1)
                                dve.wait_ge(S["sc_ev"], 6 * NG + 1)
                        end_section()

                with nc.Block() as block:
                    @block.vector
                    def _(dve):
                        v = Chain(dve, chain_v)
                        for t in range(T):
                            dve.tensor_tensor(acc[:, t, :], acc[:, t, :], gate[:, min(t, 1), :], ALU.mult).then_inc(chain_v, 1)
                        v.n = T
                        dve.wait_ge(chain_v, T)
                        for t in range(T):
                            dve.tensor_tensor(x[:, t, :], x[:, t, :], acc[:, t, :], ALU.add).then_inc(chain_v, 1)
                        dve.wait_ge(chain_v, 2 * T)
                end_section()
            if debug == "moe":
                with nc.Block() as block:
                    @block.sync
                    def _(sp):
                        sp.dma_start(O["dbg"].rearrange("(t p) d -> p t d", p=P), x[:, :, :]).then_inc(stored, 16)
                        sp.wait_ge(stored, 16)
                end_section()

        with nc.Block() as block:
            @block.sync
            def _(sp):
                sp.dma_start(O["y_prompt"][0], x[:, 0, :]).then_inc(stored, 16)
                sp.dma_start(O["y_sample"][0].rearrange("(t p) d -> p t d", p=P), x[:, 1:3, :]).then_inc(stored, 16)
                sp.wait_ge(stored, 32)


OUTS = ["y_prompt", "y_sample", "new_na_k", "new_na_v", "new_df_k", "new_df_v", "new_ml_C", "new_ml_n", "new_ml_m"]
INS = ["x_prompt", "x_sample", "cache_na_k", "cache_na_v", "cache_df_k", "cache_df_v", "state_ml_C", "state_ml_n",
       "state_ml_m", "c", "c_ctx", "w_ada", "b_ada", "g_norm1", "g_norm2", "w_in", "w_out", "na_qn", "na_kn", "na_rpb",
       "df_qn", "df_kn", "df_lam", "df_subln", "ml_gate_b", "ml_outn", "w_router", "b_router", "w_exp1", "w_exp3",
       "w_exp2", "w_sh1", "w_sh3", "w_sh2"]
SHAPES = [(1, P, D), (1, 2 * P, D), (1, DEPTH, NAH, P, NAD), (1, DEPTH, NAH, P, NAD), (1, DEPTH, DFH, 2, P, DFD),
          (1, DEPTH, DFH, P, DFV), (1, DEPTH, 2, MLH, MLD, MLD), (1, DEPTH, 2, MLH, MLD), (1, DEPTH, 2, MLH)]


def kernel(**inputs):
    import concourse.bacc as bacc
    from concourse.bass_utils import run_bass_kernel_spmd

    nc = bacc.Bacc("TRN2", target_bir_lowering=False, num_devices=1)
    arrays = {f"in_{n}": np.ascontiguousarray(inputs[n]) for n in INS}
    arrays["in_consts"] = constants()
    A = {n[3:]: nc.dram_tensor(n, a.shape, mybir.dt.from_np(a.dtype), kind="ExternalInput").ap() for n, a in arrays.items()}
    O = {n: nc.dram_tensor(f"out_{n}", s, F32, kind="ExternalOutput").ap() for n, s in zip(OUTS, SHAPES)}
    program(nc, A, O)
    r = run_bass_kernel_spmd(nc, [arrays], core_ids=[0])
    return tuple(r.results[0][f"out_{n}"] for n in OUTS)
```

```python
from contextlib import ExitStack

import concourse.bass as bass
import numpy as np
from concourse import mybir

F32 = mybir.dt.float32
F32R = mybir.dt.float32r
I32 = mybir.dt.int32
ALU = mybir.AluOpType
ACT = mybir.ActivationFunctionType
AX = mybir.AxisListType

P = 128
DEPTH, D = 2, 1024
KC = D // P
T = 3
GRID_W = 64
NAH, NAD = 4, 64
DFH, DFD, DFV = 4, 32, 64
MLH, MLD = 4, 128
NA_W, DF_W, ML_W = 256, 256, 512
IN_COLS = 3600
NE, TOPK, DE = 32, 4, 256
ROUTED_SCALE = 2.5
EPS = 1e-6
WIN_C = 16
RPB_R, RPB_C = 15, 31
NEG = -1e30
SLOTS = P
GROUP = 4
SLOTF = 2048

C_ID, C_IOTA, C_TRIU, C_ONES, C_TAB = 0, 128, 256, 384, 512
T_MF, T_MB, T_COL, T_COS, T_SIN, T_LAM, T_SEL, T_N = 0, 128, 256, 320, 384, 448, 452, 964
B_NAG, B_DFG, B_SUB, B_OUT, B_GB, B_LAM, B_N = 0, 128, 192, 256, 384, 400, 528


def constants():
    c = np.zeros((P, C_TAB + T_N), np.float32)
    tab = c[:, C_TAB:]
    p = np.arange(P)
    c[:, C_ID:C_ID + P] = np.eye(P)
    c[:, C_IOTA:C_IOTA + P] = p[None, :]
    c[:, C_TRIU:C_TRIU + P] = p[:, None] < p[None, :]
    c[:, C_ONES:C_ONES + P] = 1.0
    tab[:, T_MF:T_MF + P] = np.where(p[:, None] <= p[None, :], 0.0, 1e30)
    tab[:, T_MB:T_MB + P] = np.where(p[:, None] >= p[None, :], 0.0, 1e30)
    col = p % GRID_W
    first = np.clip(col - WIN_C // 2, 0, GRID_W - WIN_C)
    k = np.arange(GRID_W)
    tab[:, T_COL:T_COL + GRID_W] = np.where((k >= first[:, None]) & (k < first[:, None] + WIN_C), 0.0, NEG)
    nf = DFD // 4
    inv = 1.0 / (10000.0 ** (np.arange(nf, dtype=np.float32) / nf))
    for t in range(2):
        row = (t * P + p) // GRID_W
        for a, pos in enumerate((row, col)):
            ang = pos.astype(np.float32)[:, None] * inv
            at = t * DFD + a * 2 * nf
            tab[:, T_COS + at:T_COS + at + nf] = tab[:, T_COS + at + nf:T_COS + at + 2 * nf] = np.cos(ang)
            tab[:, T_SIN + at:T_SIN + at + nf] = -np.sin(ang)
            tab[:, T_SIN + at + nf:T_SIN + at + 2 * nf] = np.sin(ang)
    for layer in range(DEPTH):
        lam_init = 0.8 - 0.6 * np.exp(-0.3 * layer)
        tab[:, T_LAM + 2 * layer] = lam_init
        tab[:, T_LAM + 2 * layer + 1] = 1.0 - lam_init
    for h in range(MLH):
        tab[h, T_SEL + h * P:T_SEL + (h + 1) * P] = 1.0
    return c


def hi(ap):
    return ap.bitcast(F32R)


def round_high(eng, out, in_):
    return eng.tensor_copy(hi(out), in_)


class Chain:

    def __init__(self, eng, sem, base=0):
        self.eng, self.sem, self.n, self.base = eng, sem, 0, base

    def __call__(self, ins):
        self.n += 1
        ins.then_inc(self.sem, 1)
        self.eng.wait_ge(self.sem, self.base + self.n)
        return ins


def program(nc, A, O):
    with ExitStack() as top:
        top.enter_context(nc.allow_non_contiguous_dma(reason="a few short vectors are loaded across partitions"))
        def sb(name, shape, dt=F32, ctx=top):
            return ctx.enter_context(nc.sbuf_tensor(name, shape, dt))

        sems = []

        def sem(name):
            s = top.enter_context(nc.semaphore(name))
            sems.append(s)
            return s

        def end_section():
            nc.all_engine_barrier()
            nc.gpsimd.dma_reset(range(sems[0].num, sems[-1].num + 1))
            nc.gpsimd.sem_clear(range(sems[0].num, sems[-1].num + 1))
            nc.all_engine_barrier()

        cst = sb("cst", [P, C_TAB])
        x = sb("x", [P, T, D])
        mcol = sb("mcol", [P, 64])
        gate = sb("gate", [P, 2, D])
        small = sb("small", [P, 256])
        npass = sb("npass", [P, 1], I32)
        nhalf = small[:, 0:8]
        ssq, rstd = small[:, 32:35], small[:, 36:39]
        PS = top.enter_context(nc.psum_tensor("PS", [P, 8, 512], F32))

        ident = cst[:, C_ID:C_ID + P]
        ones = cst[:, C_ONES:C_ONES + P]

        NRING = 5
        landed = [sem(f"slot_landed{i}") for i in range(NRING)]
        slot_used = sem("slot_used")
        loaded = sem("small_loaded")
        loaded2 = sem("late_loaded")
        stored = sem("stored")
        chain_v = sem("vector_chain")
        chain_s = sem("scalar_chain")
        chain_p = sem("pool_chain")
        S = {name: sem(name) for name in (
            "csilu", "mod_row", "mod_tr", "mod_col",
            "ssq_ready", "rstd_ready", "xn_ready", "xn_tr", "hT_s", "hT_v",
            "tail_mm", "proj_mm", "proj_ev",
            "lf_ready", "rows_tr", "rows_v", "cols_mm",
            "exp_in", "exp_out",
            "sq_ready", "sq_part", "ms_ready", "r_ready", "qk_ready",
            "ctx_tr", "ctx_ev", "att_tr", "att_ev", "sc_mm", "nm_ready", "ex_ready", "w_ready",
            "pt_mm", "pt_ev", "pv_mm", "pv_ev",
            "mqk_tr", "mqk_ev", "st_mm", "st_ev", "mb_mm", "mb_free", "d_ready", "e_ready", "s_ready", "wk_ready",
            "num_mm", "num_ev", "upd_mm", "decayed", "c_ready", "ml_done",
            "sig_e", "gate_ready", "mix_ready", "mix_tr", "mixT", "out_mm", "x_done",
            "rt_mm", "rt_e", "mask_ready", "pos_mm", "back_tr", "back_high", "back_ev",
            "sh_mm", "sh_silu", "sh_hid", "sh_tr", "sh_trev", "sh_low", "sh_down", "sh_done",
            "cut_v", "cut_p", "cut_s", "low_v", "low_p",
            "pb_ready", "ga_mm", "ga_ev", "gs_ev", "idw_ready", "id_part",
            "silu", "hid_ready", "ht_mm", "ht_ev", "hidT_low", "y_high", "y_low", "sc_ev",
        )}

        modd = nc.dram_tensor("mod_rows", [DEPTH, 2, 6 * D], F32, kind="Internal").ap()
        mcold = nc.dram_tensor("mod_cols", [DEPTH, P, 64], F32, kind="Internal").ap()
        biasd = nc.dram_tensor("na_bias", [DEPTH, 2, P, NAH, 256], F32, kind="Internal").ap()

        def bcast(ap, n):
            return bass.AP(tensor=ap.tensor, offset=ap.offset, ap=[[0, P], [1, n]])

        with ExitStack() as sec:
            NR, NC_ = 5, 3
            raw = sb("raw0", [P, NR, SLOTF], ctx=sec)
            high = sb("high0", [P, NC_, SLOTF], ctx=sec)
            low = sb("low0", [P, NC_, SLOTF], ctx=sec)
            modr = sb("modr", [2, 6 * D], ctx=sec)
            bada = sb("bada", [2, DEPTH, 6 * D], ctx=sec)
            gn = sb("gn", [2, DEPTH, 2, D], ctx=sec)
            ccol = sb("ccol", [P, KC, 2], ctx=sec)
            chigh = sb("chigh", [P, KC, 2], ctx=sec)
            clow = sb("clow", [P, KC, 2], ctx=sec)
            mstage = sb("mstage", [P, 64], ctx=sec)
            NB = 12
            SLOTS0 = DEPTH * NB * 2

            with nc.Block() as block:
                @block.sync
                def _(sp):
                    sp.dma_start(cst[:, :], A["consts"][:, 0:C_TAB]).then_inc(loaded, 16)
                    sp.dma_start(ccol[:, :, 0], A["c_ctx"].rearrange("(c p) -> p c", p=P)).then_inc(loaded, 16)
                    sp.dma_start(ccol[:, :, 1], A["c"][0].rearrange("(c p) -> p c", p=P)).then_inc(loaded, 16)
                    sp.dma_start(x[:, 0, :], A["x_prompt"][0]).then_inc(loaded, 16)
                    sp.dma_start(x[:, 1:3, :], A["x_sample"][0].rearrange("(t p) d -> p t d", p=P)).then_inc(loaded, 16)
                    n = 0
                    for l in range(DEPTH):
                        for b in range(NB):
                            for half in range(2):
                                if n >= NR:
                                    sp.wait_ge(S["low_v"], n - NR + 1)
                                src = A["w_ada"][l, half * 512:(half + 1) * 512, b * 512:(b + 1) * 512]
                                sp.dma_start(raw[:, n % NR, :].rearrange("p (c n) -> p c n", c=4),
                                             src.rearrange("(c p) n -> p c n", p=P)).then_inc(landed[n % NR], 16)
                                n += 1

                @block.gpsimd
                def _(pool):
                    pool.memset(nhalf, -0.5).then_inc(chain_p, 1)
                    for l in range(DEPTH):
                        for t in range(2):
                            for r2 in range(2):
                                for h in range(NAH):
                                    r = 2 * t + r2
                                    base = A["na_rpb"][l, h]
                                    src = bass.AP(tensor=base.tensor,
                                                  offset=base.offset + (7 - r) * RPB_C + WIN_C - 1,
                                                  ap=[[RPB_C, 4], [-1, 64], [1, 64]])
                                    pool.dma_start(
                                        biasd[l, t, r2 * 64:(r2 + 1) * 64, h].rearrange("q (j k) -> j q k", j=4),
                                        src).then_inc(loaded2, 16)
                    for l in range(DEPTH):
                        pool.wait_ge(S["mod_row"], NB * (l + 1))
                        pool.wait_ge(S["exp_out"], l + 1)
                        pool.dma_start(modd[l], modr[:, :]).then_inc(stored, 16)
                        pool.wait_ge(S["mod_col"], l + 1)
                        pool.dma_start(mcold[l], mstage[:, :]).then_inc(stored, 16)
                        pool.wait_ge(stored, 32 * (l + 1))
                    pool.wait_ge(loaded2, 16 * 32)

                @block.scalar
                def _(act):
                    for l in range(DEPTH):
                        for i in range(2):
                            act.dma_start(bada[i:i + 1, l, :], A["b_ada"][l].rearrange("(o n) -> o n", o=1)).then_inc(S["exp_in"], 16)
                            act.dma_start(gn[i:i + 1, l, 0, :], A["g_norm1"][l].rearrange("(o n) -> o n", o=1)).then_inc(S["exp_in"], 16)
                            act.dma_start(gn[i:i + 1, l, 1, :], A["g_norm2"][l].rearrange("(o n) -> o n", o=1)).then_inc(S["exp_in"], 16)
                    act.wait_ge(loaded, 80)
                    act.activation(ccol[:, :, :], ccol[:, :, :], ACT.Silu).then_inc(S["silu"], 1)
                    for n in range(SLOTS0):
                        act.wait_ge(landed[n % NR], 16 * (n // NR + 1))
                        if n >= NC_:
                            act.wait_ge(slot_used, n - NC_ + 1)
                        act.activation(hi(high[:, n % NC_, :]), raw[:, n % NR, :], ACT.Copy).then_inc(S["cut_s"], 1)

                @block.tensor
                def _(pe):
                    pe.wait_ge(S["csilu"], 2)
                    n = 0
                    for l in range(DEPTH):
                        for b in range(NB):
                            i = l * NB + b
                            if i >= 4:
                                pe.wait_ge(S["mod_row"], i - 3)
                            for half in range(2):
                                pe.wait_ge(S["low_v"], n + 1)
                                for c in range(4):
                                    k = half * 4 + c
                                    w = slice(c * 512, (c + 1) * 512)
                                    out = PS[0:2, i % 4, :]
                                    pe.matmul(out, hi(chigh[:, k, :]), hi(high[:, n % NC_, w]), start=(k == 0), stop=False)
                                    pe.matmul(out, hi(chigh[:, k, :]), hi(low[:, n % NC_, w]), start=False, stop=False)
                                    mm = pe.matmul(out, hi(clow[:, k, :]), hi(high[:, n % NC_, w]), start=False, stop=(k == 7))
                                mm.then_inc(slot_used, 1)
                                n += 1
                        pe.wait_ge(S["exp_out"], l + 1)
                        for kind, at in enumerate((0, D, 3 * D, 4 * D)):
                            for c in range(KC):
                                o = (kind * KC + c) * 2
                                mm = pe.transpose(PS[:, 4, o:o + 2], modr[:, at + c * P:at + (c + 1) * P], ident[0:2, 0:2])
                        mm.then_inc(S["mod_tr"], 1)

                @block.vector
                def _(dve):
                    v = Chain(dve, chain_v)
                    dve.wait_ge(S["silu"], 1)
                    round_high(dve, chigh[:, :, :], ccol[:, :, :]).then_inc(S["csilu"], 1)
                    dve.wait_ge(S["csilu"], 1)
                    dve.tensor_tensor(hi(clow[:, :, :]), ccol[:, :, :], chigh[:, :, :], ALU.subtract).then_inc(S["csilu"], 1)

                    def cut_low(n):
                        dve.wait_ge(S["cut_s"], n + 1)
                        dve.tensor_tensor(hi(low[:, n % NC_, :]), raw[:, n % NR, :], high[:, n % NC_, :], ALU.subtract).then_inc(S["low_v"], 1)

                    def rows(l, b):
                        i = l * NB + b
                        dve.wait_ge(slot_used, 2 * (i + 1))
                        dve.tensor_tensor(modr[:, b * 512:(b + 1) * 512], PS[0:2, i % 4, :],
                                          bada[:, l, b * 512:(b + 1) * 512], ALU.add).then_inc(S["mod_row"], 1)

                    AHEAD = 4
                    for n in range(AHEAD):
                        cut_low(n)
                    dve.wait_ge(S["exp_in"], 96 * DEPTH)
                    for l in range(DEPTH):
                        for b in range(NB):
                            n = 2 * (l * NB + b) + AHEAD
                            for ahead in range(n, min(n + 2, SLOTS0)):
                                cut_low(ahead)
                            if l and b == 0:
                                dve.wait_ge(stored, 32 * l)
                            rows(l, b)
                            if b == 9:
                                dve.wait_ge(S["mod_row"], l * NB + b + 1)
                                for i, at in enumerate((D, 4 * D)):
                                    v(dve.scalar_tensor_tensor(modr[:, at:at + D], modr[:, at:at + D], 1.0, gn[:, l, i, :],
                                                               ALU.add, ALU.mult))
                                dve.sem_inc(S["exp_out"], 1)
                        dve.wait_ge(S["mod_tr"], l + 1)
                        dve.tensor_copy(mstage[:, :], PS[:, 4, 0:64]).then_inc(S["mod_col"], 1)

            end_section()

        def norm_act(act, which):
            for t in range(T):
                act.activation(tok[:, t, :], x[:, t, :], ACT.Square, accum_out=ssq[:, t:t + 1]).then_inc(S["ssq_ready"], 1)

        def norm_pool(pool, chain):
            for t in range(T):
                pool.wait_ge(S["ssq_ready"], t + 1)
                chain(pool.tensor_scalar(rstd[:, t:t + 1], ssq[:, t:t + 1], 1.0 / D, EPS, ALU.mult, ALU.add))
                pool.tensor_tensor(rstd[:, t:t + 1], rstd[:, t:t + 1], nhalf[:, 0:1], ALU.pow).then_inc(S["rstd_ready"], 1)

        def norm_dve(dve):
            for t in range(T):
                dve.wait_ge(S["rstd_ready"], t + 1)
                dve.tensor_scalar(tok[:, t, :], x[:, t, :], rstd[:, t:t + 1], None, ALU.mult).then_inc(S["xn_ready"], 1)

        def norm_pe(pe):
            for t in range(T):
                pe.wait_ge(S["xn_ready"], t + 1)
                for half in range(2):
                    for c in range(4):
                        k = half * 4 + c
                        mm = pe.transpose(PS[:, 2 * t + half, c * P:(c + 1) * P], tok[:, t, k * P:(k + 1) * P], ident)
                    mm.then_inc(S["xn_tr"], 1)

        def mod_at(kind, k, t):
            o = (kind * KC + k) * 2 + min(t, 1)
            return mcol[:, o:o + 1]

        def norm_ev_act(act, which, hT):
            for t in range(T):
                act.wait_ge(S["xn_tr"], 2 * t + 1)
                for c in range(4):
                    act.activation(hT[:, c, t * P:(t + 1) * P], PS[:, 2 * t, c * P:(c + 1) * P], ACT.Identity,
                                   bias=mod_at(2 * which, c, t), scale=mod_at(2 * which + 1, c, t)).then_inc(S["hT_s"], 1)

        def norm_ev_dve(dve, which, hT):
            for t in range(T):
                dve.wait_ge(S["xn_tr"], 2 * t + 2)
                for c in range(4):
                    k = 4 + c
                    dve.tensor_scalar(hT[:, k, t * P:(t + 1) * P], PS[:, 2 * t + 1, c * P:(c + 1) * P],
                                      mod_at(2 * which + 1, k, t), mod_at(2 * which, k, t),
                                      ALU.mult, ALU.add).then_inc(S["hT_v"], 1)


        nm, rs, rr = small[:, 84:88], small[:, 88:92], small[:, 92:96]
        nlam, omli = small[:, 96:97], small[:, 97:98]
        lamt = small[:, 98:102]
        zrow = small[0:4, 128:256]
        NSA = 4
        ML_ORDER = [(0, 0), (0, 1), (1, 0), (2, 1), (2, 0), (1, 1)]
        FINISHED = {0: 1, 2: 4, 1: 5}
        OUT_ORDER = (0, 2, 1)
        BATCHES = [(t, kind) for t in range(T) for kind in ("na", "df0", "df1")]
        UNITS = [(g, t) for g in range(3, 7) for t in range(T)]
        LATE = 3

        with nc.Fori(0, DEPTH) as l:
            with ExitStack() as sec:
                tok = sb("tokA", [P, T, D], ctx=sec)
                prm = sb("prm", [P, B_N], ctx=sec)
                tab = sb("tab", [P, T_N], ctx=sec)
                ring = sb("ringA", [P, NSA, SLOTF], ctx=sec)
                hT = sb("hT", [P, KC, T * P], ctx=sec)
                p = sb("p", [P, T, 2560], ctx=sec)
                attT = sb("attT", [P, 8, 512], ctx=sec)
                bias = sb("bias", [P, 2, NAH, 256], ctx=sec)
                W1 = sb("W1", [P, 4, 384], ctx=sec)
                W2 = sb("W2", [P, 4, 384], ctx=sec)
                PT = sb("PT", [P, 2, 384], ctx=sec)
                ckv = sb("ckv", [P, 4, 256], ctx=sec)
                vaug = sb("vaug", [P, T, MLH, MLD + 1], ctx=sec)
                Caug = sb("Caug", [P, 8, MLD + 1], ctx=sec)
                Cp = sb("Cp", [P, 8, MLD + 1], ctx=sec)
                ST = sb("ST", [P, T, 512], ctx=sec)
                mlh = sb("mlh", [P, T, 512], ctx=sec)
                num = sb("num", [P, 4, MLD + 1], ctx=sec)
                tmp = sb("tmp", [P, 4, MLD + 1], ctx=sec)
                wk = sb("wk", [P, 512], ctx=sec)
                R = sb("R", [4, T, 2, 2, P], ctx=sec)
                brow = sb("brow", [4, T, 2, P], ctx=sec)
                sm = sb("sm", [P, 512], ctx=sec)
                gt = sm[:, 0:48].rearrange("p (t g) -> p t g", t=T)
                e1 = sm[:, 48:72].rearrange("p (t d h) -> p t d h", t=T, d=2)
                e2 = sm[:, 72:96].rearrange("p (t d h) -> p t d h", t=T, d=2)
                cols = sm[:, 96:168].rearrange("p (q n) -> p q n", q=3)
                bcs = sm[:, 168:216].rearrange("p (n k h) -> p n k h", n=6, k=2)
                arg = sm[:, 216:312].rearrange("p (q n) -> p q n", q=4)
                ms = sm[:, 312:384]
                ms2 = sm[:, 384:396]
                den = sm[:, 396:400]
                scal = sm[0:4, 400:412].rearrange("p (n k) -> p n k", n=6)
                diag = sm[0:4, 412:460].rearrange("p (n h) -> p n h", n=12)
                m0 = sm[0:4, 460:462]
                mout = sm[0:4, 462:464]
                nq = W1[:, :, :].rearrange("p a b -> p (a b)")
                dq = W2[:, :, :].rearrange("p a b -> p (a b)")
                last = lambda d: P - 1 if d == 0 else 0
                X = [dq[:, i * 512:(i + 1) * 512].rearrange("p (h n) -> p h n", h=4) for i in range(2)]
                wks = [wk[:, :], dq[:, 1024:1536]]

                def col4(q, td):
                    return cols[:, q, 4 * td:4 * td + 4]

                def arg4(q, td):
                    return arg[:, q, 4 * td:4 * td + 4]

                def keys_of(t):
                    return (0, P) if t == 0 else (P, 512)

                def aps_of(batch):
                    t, kind = batch
                    k0, k1 = keys_of(t)
                    out = []
                    for m in range(4):
                        if kind == "na":
                            i, rows = m // 2, slice(64 * (m % 2), 64 * (m % 2) + 64)
                            j = 2 + i
                        else:
                            hf = int(kind[2])
                            i, rows = 4 + hf, slice(32 * m, 32 * m + 32)
                            j = 6 + hf
                        out.append((attT[rows, i, t * P:(t + 1) * P], attT[rows, j, k0:k1]))
                    return out

                def values_of(batch, m):
                    t, kind = batch
                    at, ck, h = (512, 1, m) if kind == "na" else (1280, 3, 2 * int(kind[2]) + m)
                    if t == 0:
                        return [p[:, 0, at + 64 * h:at + 64 * h + 64]]
                    return [p[:, u, at + 64 * h:at + 64 * h + 64] for u in (1, 2)] + [ckv[:, ck, 64 * h:64 * h + 64]]

                n_maps = lambda batch: 4 if batch[1] == "na" else 2
                first_map = [sum(n_maps(b) for b in BATCHES[:i]) for i in range(len(BATCHES) + 1)]

                with nc.Block() as block:
                    @block.sync
                    def _(sp):
                        for at, n, name in ((B_NAG, 64, "na_qn"), (B_NAG + 64, 64, "na_kn"), (B_DFG, 32, "df_qn"),
                                            (B_DFG + 32, 32, "df_kn"), (B_SUB, 64, "df_subln"), (B_OUT, 128, "ml_outn")):
                            sp.dma_start(prm[:, at:at + n], bcast(A[name][l], n)).then_inc(loaded, 16)
                        sp.dma_start(prm[:, B_GB:B_GB + 16], bcast(A["ml_gate_b"][l], 16)).then_inc(loaded, 16)
                        sp.dma_start(prm[:, B_LAM:B_LAM + 128], bcast(A["df_lam"][l], 128)).then_inc(loaded, 16)
                        sp.dma_start(mcol[:, :], mcold[l]).then_inc(loaded, 16)
                        sp.dma_start(m0, A["state_ml_m"][0, l].rearrange("r h -> h r")).then_inc(loaded, 16)
                        sp.dma_start(tab[:, :], A["consts"][:, C_TAB:C_TAB + T_N]).then_inc(loaded, 16)
                        n = 0

                        def slot_free():
                            if n >= NSA:
                                sp.wait_ge(slot_used, n - NSA + 1)

                        sp.dma_start(ring[:, 0, 0:128].rearrange("p (c n) -> p c n", c=KC),
                                     A["w_in"][l, :, 3584:3600].rearrange("(c p) n -> p c n", p=P)).then_inc(landed[0], 16)
                        n = 1
                        for w, groups in (("w_in", 7), ("w_out", 2)):
                            for gr in range(groups):
                                for half in range(2):
                                    slot_free()
                                    src = A[w][l, half * 512:(half + 1) * 512, gr * 512:(gr + 1) * 512]
                                    sp.dma_start(ring[:, n % NSA, :].rearrange("p (c n) -> p c n", c=4),
                                                 src.rearrange("(c p) n -> p c n", p=P)).then_inc(landed[n % NSA], 16)
                                    n += 1

                    @block.gpsimd
                    def _(pool):
                        norm_pool(pool, Chain(pool, chain_p))
                        for i in range(2):
                            pool.dma_start(gate[:, i, :], bcast(modd[l, i, 2 * D:3 * D], D)).then_inc(loaded2, 16)
                        pool.dma_start(ckv[:, 0, :].rearrange("p (h d) -> p h d", h=4),
                                       A["cache_na_k"][0, l].rearrange("h k d -> k h d")).then_inc(loaded2, 16)
                        pool.dma_start(ckv[:, 1, :].rearrange("p (h d) -> p h d", h=4),
                                       A["cache_na_v"][0, l].rearrange("h k d -> k h d")).then_inc(loaded2, 16)
                        pool.dma_start(ckv[:, 2, :].rearrange("p (h d) -> p h d", h=8),
                                       A["cache_df_k"][0, l].rearrange("h a k d -> k (h a) d")).then_inc(loaded2, 16)
                        pool.dma_start(ckv[:, 3, :].rearrange("p (h d) -> p h d", h=4),
                                       A["cache_df_v"][0, l].rearrange("h k d -> k h d")).then_inc(loaded2, 16)
                        for t in range(2):
                            pool.dma_start(bias[:, t, :, :], biasd[l, t]).then_inc(loaded2, 16)
                        pool.dma_start(Caug[:, :, 0:MLD], A["state_ml_C"][0, l].rearrange("r h d e -> d (r h) e")).then_inc(loaded2, 16)
                        pool.dma_start(Caug[:, :, MLD], A["state_ml_n"][0, l].rearrange("r h d -> d (r h)")).then_inc(loaded2, 16)
                        for i, (n0, n1) in enumerate(((0, 24), (24, 72))):
                            pool.wait_ge(S["ms_ready"], i + 1)
                            pool.tensor_tensor(ms[:, n0:n1], ms[:, n0:n1], nhalf[:, 0:1].to_broadcast([P, n1 - n0]), ALU.pow).then_inc(S["r_ready"], 1)
                        pool.wait_ge(S["qk_ready"], 1)
                        pool.dma_start(O["new_na_k"][0, l].rearrange("h p d -> p h d"),
                                       p[:, 0, 256:512].rearrange("p (h d) -> p h d", h=4)).then_inc(stored, 16)
                        pool.dma_start(O["new_na_v"][0, l].rearrange("h p d -> p h d"),
                                       p[:, 0, 512:768].rearrange("p (h d) -> p h d", h=4)).then_inc(stored, 16)
                        pool.dma_start(O["new_df_k"][0, l].rearrange("h a p d -> p (h a) d"),
                                       p[:, 0, 1024:1280].rearrange("p (h d) -> p h d", h=8)).then_inc(stored, 16)
                        pool.dma_start(O["new_df_v"][0, l].rearrange("h p d -> p h d"),
                                       p[:, 0, 1280:1536].rearrange("p (h d) -> p h d", h=4)).then_inc(stored, 16)
                        pool.wait_ge(S["ms_ready"], 3)
                        pool.tensor_tensor(ms2, ms2, nhalf[:, 0:1].to_broadcast([P, 12]), ALU.pow).then_inc(S["r_ready"], 1)
                        c = Chain(pool, chain_p, T)
                        pool.wait_ge(S["exp_in"], 3)
                        pool.wait_ge(S["pv_ev"], len(BATCHES))

                        def weigh_keys(i):
                            if i >= 2:
                                pool.wait_ge(S["upd_mm"], i - 1)
                            t, d = ML_ORDER[i]
                            pool.tensor_tensor(wks[i % 2].rearrange("p (h n) -> p h n", h=4),
                                               p[:, t, 1536:2048].rearrange("p (h n) -> p h n", h=4),
                                               arg4(2, 2 * t + d)[:, :, None].to_broadcast([P, 4, P]), ALU.mult).then_inc(S["wk_ready"], 1)

                        def decay(i):
                            t, d = ML_ORDER[i]
                            pool.wait_ge(S["num_mm"], i + 1)
                            C4 = Caug[:, 4 * d:4 * d + 4, :]
                            pool.tensor_tensor(C4, C4, arg4(3, 2 * t + d)[:, :, None].to_broadcast([P, 4, MLD + 1]), ALU.mult).then_inc(S["decayed"], 1)

                        def head_rsqrt(o):
                            m4 = ms2[:, 4 * o:4 * o + 4]
                            pool.wait_ge(S["sq_ready"], 7 + o)
                            c(pool.tensor_scalar(m4, m4, 1.0 / MLD, EPS, ALU.mult, ALU.add))
                            pool.tensor_tensor(m4, m4, nhalf[:, 0:4], ALU.pow).then_inc(S["r_ready"], 1)

                        weigh_keys(0)
                        weigh_keys(1)
                        pool.wait_ge(S["sig_e"], 1)
                        for t in OUT_ORDER:
                            mo = p[:, t, 2048:2560].rearrange("p (h n) -> p h n", h=4)
                            pool.tensor_tensor(mo, mo, prm[:, None, B_OUT:B_OUT + P].to_broadcast([P, 4, P]), ALU.mult).then_inc(S["gate_ready"], 1)
                        weigh_keys(2)
                        head_rsqrt(0)
                        decay(2)
                        weigh_keys(3)
                        decay(3)
                        pool.dma_start(O["new_ml_C"][0, l].rearrange("r h d e -> d (r h) e"), Cp[:, :, 0:MLD]).then_inc(stored, 16)
                        pool.dma_start(O["new_ml_n"][0, l].rearrange("r h d -> d (r h)"), Cp[:, :, MLD]).then_inc(stored, 16)
                        pool.dma_start(O["new_ml_m"][0, l].rearrange("r h -> h r"), mout).then_inc(stored, 16)
                        head_rsqrt(1)
                        head_rsqrt(2)
                        pool.wait_ge(stored, 16 * 7)

                    @block.scalar
                    def _(act):
                        a = Chain(act, chain_s)
                        norm_act(act, 0)
                        act.wait_ge(loaded, 16 * 11)
                        norm_ev_act(act, 0, hT)
                        act.wait_ge(S["exp_in"], 1)
                        a(act.activation(e1, e1, ACT.Exp, scale=-1.0))
                        act.activation(e1, e1, ACT.Ln, bias=ones[:, 0:1]).then_inc(S["exp_out"], 1)

                        def proj_evac(u, g, t):
                            act.wait_ge(S["proj_mm"], u + 1)
                            dst = {3: tok[:, t, 512:1024], 4: p[:, t, 1536:2048], 6: p[:, t, 2048:2560],
                                   5: vaug[:, t, :, 0:MLD]}.get(g)
                            if dst is None:
                                dst = p[:, t, g * 512:(g + 1) * 512]
                            src = PS[:, u % 2, :]
                            if g == 5:
                                src = src.rearrange("p (h d) -> p h d", h=4)
                            act.activation(dst, src, ACT.Copy).then_inc(S["proj_ev"], 1)

                        u = 0
                        for g in range(3):
                            for t in range(T):
                                proj_evac(u, g, t)
                                u += 1
                                if g == 0:
                                    act.wait_ge(S["proj_ev"], u)
                                    act.activation(nq[:, t * 512:(t + 1) * 512], p[:, t, 0:512], ACT.Square).then_inc(S["sq_ready"], 1)
                                if g == 2:
                                    act.wait_ge(S["proj_ev"], u)
                                    act.activation(dq[:, t * 512:(t + 1) * 512], p[:, t, 768:1280], ACT.Square).then_inc(S["sq_ready"], 1)
                            if g == 0:
                                act.wait_ge(S["ctx_tr"], 1)
                                for j, idx in enumerate((2, 3, 6, 7)):
                                    act.activation(attT[:, idx, 384:512], PS[:, 4, j * P:(j + 1) * P], ACT.Copy).then_inc(S["ctx_ev"], 1)

                        def exps(i):
                            t, kind = BATCHES[i]
                            nk = keys_of(t)[1] - keys_of(t)[0]
                            act.wait_ge(S["nm_ready"], i + 1)
                            for m in range(4):
                                src = W1[:, m, 0:nk] if kind == "na" else PS[:, 2 + m, 0:nk]
                                act.activation(W2[:, m, 0:nk], src, ACT.Exp, bias=nm[:, m:m + 1],
                                               scale=1.0 if kind == "na" else DFD ** -0.5,
                                               accum_out=rs[:, m:m + 1]).then_inc(S["ex_ready"], 1)

                        def pt_evac(i):
                            t, kind = BATCHES[i]
                            nk = keys_of(t)[1] - keys_of(t)[0]
                            for m in range(first_map[i], first_map[i + 1]):
                                act.wait_ge(S["pt_mm"], m + 1)
                                if m >= 2:
                                    act.wait_ge(S["pv_mm"], m - 1)
                                act.activation(PT[:, m % 2, 0:nk], PS[:, 6 + m % 2, 0:nk], ACT.Copy).then_inc(S["pt_ev"], 1)

                        for i, (g, t) in enumerate(UNITS):
                            proj_evac(u, g, t)
                            u += 1
                            b = i - LATE
                            if b == -1:
                                act.wait_ge(S["exp_in"], 2)
                                act.activation(arg, arg, ACT.Exp).then_inc(S["exp_out"], 1)
                                act.wait_ge(S["exp_in"], 3)
                                act.activation(lamt[:, 2:4], lamt[:, 0:2], ACT.Exp).then_inc(S["exp_out"], 1)
                                for t2 in range(T):
                                    act.wait_ge(S["att_tr"], t2 + 1)
                                    for j in range(2):
                                        act.activation(attT[:, 4 * j:4 * j + 4, t2 * P:(t2 + 1) * P],
                                                       PS[:, 2 + 2 * (t2 % 2) + j, :].rearrange("p (c n) -> p c n", c=4),
                                                       ACT.Copy).then_inc(S["att_ev"], 1)
                            if 0 <= b < len(BATCHES):
                                pt_evac(b)
                            if 0 <= b + 1 < len(BATCHES):
                                exps(b + 1)
                        for t in range(T):
                            act.wait_ge(S["mqk_tr"], t + 1)
                            for j in range(2):
                                act.activation(hT[:, 4 * j:4 * j + 4, t * P:(t + 1) * P],
                                               PS[:, 2 + 2 * t + j, :].rearrange("p (c n) -> p c n", c=4),
                                               ACT.Copy, scale=MLD ** -0.5 if j else 1.0).then_inc(S["mqk_ev"], 1)
                        for t in range(T):
                            act.wait_ge(S["st_mm"], t + 1)
                            act.activation(ST[:, t, :], PS[:, t, :], ACT.Copy).then_inc(S["st_ev"], 1)
                        mo = p[:, :, 2048:2560]
                        act.activation(mo, mo, ACT.Sigmoid).then_inc(S["sig_e"], 1)

                        def squares(o):
                            t = OUT_ORDER[o]
                            act.wait_ge(S["ml_done"], o + 1)
                            for h in range(MLH):
                                ins = act.activation(nq[:, o * 512 + h * P:o * 512 + (h + 1) * P], mlh[:, t, h * P:(h + 1) * P], ACT.Square,
                                                     accum_out=ms2[:, 4 * o + h:4 * o + h + 1])
                                if h < MLH - 1:
                                    ins.then_inc(S["sq_part"], 1)
                            ins.then_inc(S["sq_ready"], 1)

                        def mixed(o):
                            t = OUT_ORDER[o]
                            act.wait_ge(S["mix_tr"], o + 1)
                            for half in range(2):
                                act.activation(hT[:, 4 * half:4 * half + 4, t * P:(t + 1) * P],
                                               PS[:, 1 + half, :].rearrange("p (c n) -> p c n", c=4), ACT.Copy).then_inc(S["mixT"], 1)

                        for i in range(6):
                            act.wait_ge(S["d_ready"], i + 1)
                            act.activation(X[i % 2], X[i % 2], ACT.Exp, scale=-1.0).then_inc(S["e_ready"], 1)
                            if i == 2:
                                squares(0)
                        mixed(0)
                        squares(1)
                        squares(2)
                        mixed(1)
                        mixed(2)

                    @block.tensor
                    def _(pe):
                        n = 0

                        def slot(c, n0, n1):
                            return ring[:, n % NSA, c * 512 + n0:c * 512 + n1]

                        norm_pe(pe)
                        pe.wait_ge(landed[0], 16)
                        for t in range(T):
                            pe.wait_ge(S["hT_s"], 4 * (t + 1))
                            pe.wait_ge(S["hT_v"], 4 * (t + 1))
                            for k in range(KC):
                                mm = pe.matmul(PS[:, 6, t * 16:(t + 1) * 16], hT[:, k, t * P:(t + 1) * P],
                                               ring[:, 0, k * 16:(k + 1) * 16], start=(k == 0), stop=(k == KC - 1))
                        mm.then_inc(S["tail_mm"], 1)
                        pe.wait_ge(S["tail_mm"], 1)
                        pe.sem_inc(slot_used, 1)
                        n = 1

                        def project(u, t, last_chunk):
                            nonlocal n
                            if u >= 2:
                                pe.wait_ge(S["proj_ev"], u - 1)
                            for half in range(2):
                                s = (n + half) % NSA
                                pe.wait_ge(landed[s], 16 * ((n + half) // NSA + 1))
                                for c in range(4):
                                    k = half * 4 + c
                                    mm = pe.matmul(PS[:, u % 2, :], hT[:, k, t * P:(t + 1) * P],
                                                   ring[:, s, c * 512:(c + 1) * 512], start=(k == 0), stop=(k == 7))
                                if last_chunk and half == 0:
                                    mm.then_inc(slot_used, 1)
                            mm.then_inc(S["proj_mm"], 1)
                            if last_chunk:
                                pe.wait_ge(S["proj_mm"], u + 1)
                                pe.sem_inc(slot_used, 1)
                                n += 2

                        u = 0
                        for g in range(3):
                            for t in range(T):
                                project(u, t, t == T - 1)
                                u += 1
                            if g == 0:
                                pe.wait_ge(loaded2, 16 * 10)
                                for j, src in enumerate((ckv[:, 0, 0:P], ckv[:, 0, P:256], ckv[:, 2, 0:P], ckv[:, 2, P:256])):
                                    mm = pe.transpose(PS[:, 4, j * P:(j + 1) * P], src, ident)
                                mm.then_inc(S["ctx_tr"], 1)
                                pe.wait_ge(S["lf_ready"], 1)
                                for t in range(T):
                                    for q in range(4):
                                        mm = pe.transpose(PS[0:4, 5 + t, q * P:(q + 1) * P], gt[:, t, 4 * q:4 * q + 4], ident)
                                    mm.then_inc(S["rows_tr"], 1)
                            if g == 1:
                                pe.wait_ge(S["rows_v"], 1)
                                for q in range(3):
                                    for t in range(T):
                                        for d in range(2):
                                            src = (R[:, t, d, 0, :], R[:, t, d, 1, :], brow[:, t, d, :])[q]
                                            o = (q * 6 + 2 * t + d) * 4
                                            pe.transpose(PS[:, 5, o:o + 4], src, ident[0:4, 0:4])
                                pe.matmul(PS[:, 5, 128:176], ones[0:4, :], sm[0:4, 412:460], start=True, stop=True).then_inc(S["cols_mm"], 1)

                        def scores(i):
                            t, kind = BATCHES[i]
                            for m in (3, 2, 1, 0):
                                q, k = aps_of(BATCHES[i])[m]
                                if m == 0 and i:
                                    pe.wait_ge(S["pv_ev"], i)
                                mm = pe.matmul(PS[:, 2 + m, 0:k.shape[1]], q, k, start=True, stop=True)
                            mm.then_inc(S["sc_mm"], 1)

                        def weigh(i):
                            t, kind = BATCHES[i]
                            nc_ = 1 if t == 0 else 3
                            f = first_map[i]
                            nm_ = n_maps(BATCHES[i])

                            def turn(j):
                                m = f + j
                                if m >= 2:
                                    pe.wait_ge(S["pt_ev"], m - 1)
                                if kind == "na":
                                    pe.wait_ge(S["ex_ready"], 4 * i + j + 1)
                                else:
                                    pe.wait_ge(S["w_ready"], 2 * sum(b[1] != "na" for b in BATCHES[:i]) + j + 1)
                                src = (W2 if kind == "na" else W1)[:, j, :]
                                for c in range(nc_):
                                    mm = pe.transpose(PS[:, 6 + m % 2, c * P:(c + 1) * P], src[:, c * P:(c + 1) * P], ident)
                                mm.then_inc(S["pt_mm"], 1)

                            def product(j):
                                m = f + j
                                if j == 0:
                                    pe.wait_ge(S["ex_ready"], 4 * i + 4)
                                pe.wait_ge(S["pt_ev"], m + 1)
                                for c, val in enumerate(values_of(BATCHES[i], j)):
                                    mm = pe.matmul(PS[:, 2, j * 64:(j + 1) * 64], PT[:, m % 2, c * P:(c + 1) * P], val,
                                                   start=(c == 0), stop=(c == nc_ - 1))
                                mm.then_inc(S["pv_mm"], 1)

                            turn(0)
                            for j in range(nm_):
                                if j + 1 < nm_:
                                    turn(j + 1)
                                product(j)

                        for i, (g, t) in enumerate(UNITS):
                            project(u, t, t == T - 1)
                            u += 1
                            b = i - LATE
                            if b == -1:
                                for t2 in range(T):
                                    pe.wait_ge(S["qk_ready"], t2 + 1)
                                    if t2 == 2:
                                        pe.wait_ge(S["att_ev"], 2)
                                    for j in range(2):
                                        for c in range(4):
                                            at = j * 768 + c * P
                                            mm = pe.transpose(PS[:, 2 + 2 * (t2 % 2) + j, c * P:(c + 1) * P], p[:, t2, at:at + P], ident)
                                    mm.then_inc(S["att_tr"], 1)
                                pe.wait_ge(S["att_ev"], 6)
                                pe.wait_ge(S["ctx_ev"], 4)
                            if 0 <= b < len(BATCHES):
                                weigh(b)
                            if 0 <= b + 1 < len(BATCHES):
                                scores(b + 1)
                        pe.wait_ge(S["pv_ev"], len(BATCHES))
                        pe.wait_ge(S["proj_ev"], 21)
                        for t in range(T):
                            for j in range(2):
                                for h in range(MLH):
                                    src = tok[:, t, 512 + h * P:512 + (h + 1) * P] if j == 0 else p[:, t, 1536 + h * P:1536 + (h + 1) * P]
                                    mm = pe.transpose(PS[:, 2 + 2 * t + j, h * P:(h + 1) * P], src, ident)
                            mm.then_inc(S["mqk_tr"], 1)
                        for t in range(T):
                            pe.wait_ge(S["mqk_ev"], 2 * (t + 1))
                            for h in range(MLH):
                                mm = pe.matmul(PS[:, t, h * P:(h + 1) * P], hT[:, 4 + h, t * P:(t + 1) * P],
                                               hT[:, h, t * P:(t + 1) * P], start=True, stop=True)
                            mm.then_inc(S["st_mm"], 1)

                        def spread(i):
                            t, d = ML_ORDER[i]
                            if i >= 2:
                                pe.wait_ge(S["mb_free"], i - 1)
                            for h in range(MLH):
                                mm = pe.matmul(PS[:, 3 + i % 2, h * P:(h + 1) * P], tab[0:4, T_SEL + h * P:T_SEL + (h + 1) * P],
                                               R[:, t, d, 1, :], start=True, stop=True)
                            mm.then_inc(S["mb_mm"], 1)

                        def turn_mixed(o):
                            t = OUT_ORDER[o]
                            pe.wait_ge(S["mix_ready"], o + 1)
                            if o:
                                pe.wait_ge(S["mixT"], 2 * o)
                            else:
                                pe.wait_ge(S["c_ready"], 4)
                            for k in range(KC):
                                mm = pe.transpose(PS[:, 1 + k // 4, (k % 4) * P:(k % 4 + 1) * P], tok[:, t, k * P:(k + 1) * P], ident)
                            mm.then_inc(S["mix_tr"], 1)

                        def project_out(o, j):
                            t = OUT_ORDER[o]
                            pe.wait_ge(S["mixT"], 2 * (o + 1))
                            if o:
                                pe.wait_ge(S["x_done"], 2 * (o - 1) + j + 1)
                            else:
                                pe.wait_ge(S["mb_free"], 5 + j)
                            for half in range(2):
                                m = n + 2 * j + half
                                pe.wait_ge(landed[m % NSA], 16 * (m // NSA + 1))
                                for c in range(4):
                                    k = half * 4 + c
                                    mm = pe.matmul(PS[:, 3 + j, :], hT[:, k, t * P:(t + 1) * P],
                                                   ring[:, m % NSA, c * 512:(c + 1) * 512], start=(k == 0), stop=(k == 7))
                            mm.then_inc(S["out_mm"], 1)

                        pe.wait_ge(S["st_ev"], T)
                        spread(0)
                        for i, (t, d) in enumerate(ML_ORDER):
                            if i + 1 < 6:
                                spread(i + 1)
                            if i:
                                pe.wait_ge(S["num_ev"], i)
                            if t:
                                if i >= 4:
                                    pe.wait_ge(S["c_ready"], i - 1)
                                for h in range(MLH):
                                    b = (7, 0)[h // 2]
                                    pe.matmul(PS[:, b, (h % 2) * 129:(h % 2) * 129 + 129], hT[:, h, t * P:(t + 1) * P],
                                              Caug[:, 4 * d + h, :], start=True, stop=True)
                            pe.wait_ge(S["s_ready"], i + 1)
                            for h in range(MLH):
                                mm = pe.matmul(PS[:, 5 + h // 2, (h % 2) * 129:(h % 2) * 129 + 129], num[:, h, 0:P],
                                               vaug[:, t, h, :], start=True, stop=True)
                            mm.then_inc(S["num_mm"], 1)
                            if i < 4:
                                if i:
                                    pe.wait_ge(S["c_ready"], i)
                                pe.wait_ge(S["wk_ready"], i + 1)
                                for h in range(MLH):
                                    mm = pe.matmul(PS[:, 1 + h // 2, (h % 2) * 129:(h % 2) * 129 + 129], wks[i % 2][:, h * P:(h + 1) * P],
                                                   vaug[:, t, h, :], start=True, stop=True)
                                mm.then_inc(S["upd_mm"], 1)
                            if i == 4:
                                turn_mixed(0)
                                project_out(0, 0)
                        project_out(0, 1)
                        turn_mixed(1)
                        project_out(1, 0)
                        turn_mixed(2)
                        project_out(1, 1)
                        project_out(2, 0)
                        project_out(2, 1)

                    @block.vector
                    def _(dve):
                        v = Chain(dve, chain_v)
                        norm_dve(dve)
                        dve.wait_ge(loaded, 16 * 11)
                        norm_ev_dve(dve, 0, hT)
                        dve.memset(zrow, 0.0).then_inc(chain_v, 1)
                        v.n += 1
                        dve.memset(vaug[:, :, :, MLD], 1.0).then_inc(chain_v, 1)
                        v.n += 1
                        dve.wait_ge(S["tail_mm"], 1)
                        v(dve.tensor_tensor(gt, PS[:, 6, 0:48].rearrange("p (t g) -> p t g", t=T),
                                            prm[:, None, B_GB:B_GB + 16].to_broadcast([P, T, 16]), ALU.add))
                        f = gt.rearrange("p t (d k h) -> p t d k h", d=2, k=2)[:, :, :, 1, :]
                        dve.scalar_tensor_tensor(e1, f, -1.0, f, ALU.mult, ALU.max).then_inc(S["exp_in"], 1)
                        v(dve.tensor_scalar(e2, f, 0.0, None, ALU.min))
                        dve.wait_ge(S["exp_out"], 1)
                        dve.tensor_tensor(f, e2, e1, ALU.subtract).then_inc(S["lf_ready"], 1)
                        lam = prm[:, B_LAM:B_LAM + 128].rearrange("p (a b d) -> p a b d", a=2, b=2)
                        v(dve.tensor_tensor(lam[:, :, 0, :], lam[:, :, 0, :], lam[:, :, 1, :], ALU.mult))
                        v(dve.tensor_reduce(lamt[:, 0:2], lam[:, :, 0, :], AX.X, ALU.add))
                        v(dve.tensor_copy(small[:, 102:104], tab[:, bass.ds(T_LAM + 2 * l, 2)]))
                        v(dve.tensor_scalar(prm[:, B_SUB:B_SUB + 64], prm[:, B_SUB:B_SUB + 64], small[:, 103:104], None, ALU.mult))
                        for t in range(T):
                            dve.wait_ge(S["rows_tr"], t + 1)
                            v(dve.tensor_copy(R[:, t].rearrange("p d k n -> p (d k n)"), PS[0:4, 5 + t, :]))
                        v(dve.memset(scal, 0.0))
                        v(dve.tensor_copy(scal[:, 2, 0:1], m0[:, 0:1]))
                        v(dve.tensor_copy(scal[:, 5, 0:1], m0[:, 1:2]))
                        for t, d in ML_ORDER:
                            td, e = 2 * t + d, last(d)
                            way = slice(None, None, -1) if d else slice(None)
                            i_, f_, b_ = R[:, t, d, 0, :], R[:, t, d, 1, :], brow[:, t, d, :]
                            v(dve.tensor_tensor_scan(b_[:, way], ones[0:4, :], f_[:, way], 0.0, ALU.mult, ALU.add))
                            v(dve.tensor_tensor(i_, i_, b_, ALU.subtract))
                            v(dve.tensor_tensor_scan(f_[:, way], zrow, i_[:, way], scal[:, td, 0:1], ALU.add, ALU.max))
                            v(dve.tensor_copy(scal[:, td, 1:2], f_[:, e:e + 1]))
                            follow = {(0, 0): mout[:, 0:1], (0, 1): mout[:, 1:2], (1, 0): scal[:, 4, 0:1],
                                      (2, 1): scal[:, 3, 0:1]}.get((t, d))
                            if follow is not None:
                                v(dve.tensor_tensor(follow, b_[:, e:e + 1], f_[:, e:e + 1], ALU.add))
                        dve.tensor_tensor(diag, sm[0:4, 400:412, None].to_broadcast([4, 12, 4]),
                                          cst[0:4, None, C_ID:C_ID + 4].to_broadcast([4, 12, 4]), ALU.mult).then_inc(S["rows_v"], 1)
                        dve.wait_ge(S["cols_mm"], 1)
                        v(dve.tensor_copy(sm[:, 96:168], PS[:, 5, 0:72]))
                        v(dve.tensor_copy(sm[:, 168:216], PS[:, 5, 128:176]))
                        dve.wait_ge(S["sq_ready"], 3)
                        v(dve.tensor_reduce(ms[:, 0:24], nq.rearrange("p (g d) -> p g d", d=NAD), AX.X, ALU.add))
                        dve.tensor_scalar(ms[:, 0:24], ms[:, 0:24], 1.0 / NAD, EPS, ALU.mult, ALU.add).then_inc(S["ms_ready"], 1)
                        bv = bias[:, :, :, :].rearrange("p t h (j k) -> p (t h j) k", k=64)
                        dve.wait_ge(loaded2, 16 * 10)
                        v(dve.tensor_tensor(bv, bv, tab[:, None, T_COL:T_COL + 64].to_broadcast([P, 32, 64]), ALU.add))
                        dve.wait_ge(S["r_ready"], 1)
                        for t in range(T):
                            na = p[:, t, 0:512].rearrange("p (g d) -> p g d", d=NAD)
                            v(dve.tensor_tensor(na, na, ms[:, 8 * t:8 * t + 8, None].to_broadcast([P, 8, NAD]), ALU.mult))
                            na = p[:, t, 0:512].rearrange("p (a h d) -> p a h d", a=2, h=4)
                            gn_ = prm[:, B_NAG:B_NAG + 128].rearrange("p (a d) -> p a d", a=2)
                            v(dve.tensor_tensor(na, na, gn_[:, :, None, :].to_broadcast([P, 2, 4, NAD]), ALU.mult))
                        dve.wait_ge(S["sq_ready"], 6)
                        v(dve.tensor_reduce(ms[:, 24:72], dq.rearrange("p (g d) -> p g d", d=DFD), AX.X, ALU.add))
                        dve.tensor_scalar(ms[:, 24:72], ms[:, 24:72], 1.0 / DFD, EPS, ALU.mult, ALU.add).then_inc(S["ms_ready"], 1)
                        dve.wait_ge(S["r_ready"], 2)
                        for t in range(T):
                            df = p[:, t, 768:1280].rearrange("p (g d) -> p g d", d=DFD)
                            v(dve.tensor_tensor(df, df, ms[:, 24 + 16 * t:40 + 16 * t, None].to_broadcast([P, 16, DFD]), ALU.mult))
                            df = p[:, t, 768:1280].rearrange("p (a h d) -> p a h d", a=2, h=8)
                            gd = prm[:, B_DFG:B_DFG + 64].rearrange("p (a d) -> p a d", a=2)
                            ins = dve.tensor_tensor(df, df, gd[:, :, None, :].to_broadcast([P, 2, 8, DFD]), ALU.mult)
                            if t == 0:
                                ins.then_inc(S["qk_ready"], 1)
                                continue
                            v(ins)
                            co, si = T_COS + (t - 1) * DFD, T_SIN + (t - 1) * DFD
                            xr = p[:, t, 768:1280].rearrange("p (g r s f) -> p g r s f", r=2, s=2, f=8)
                            yr = tmp.rearrange("p a b -> p (a b)")[:, 0:512].rearrange("p (g r s f) -> p g r s f", r=2, s=2, f=8)
                            for s_ in range(2):
                                sn = tab[:, si:si + DFD].rearrange("p (r s f) -> p r s f", r=2, s=2)[:, None, :, s_, :]
                                v(dve.tensor_tensor(yr[:, :, :, s_, :], xr[:, :, :, 1 - s_, :], sn.to_broadcast([P, 16, 2, 8]), ALU.mult))
                            df = p[:, t, 768:1280].rearrange("p (g d) -> p g d", d=DFD)
                            v(dve.tensor_tensor(df, df, tab[:, None, co:co + DFD].to_broadcast([P, 16, DFD]), ALU.mult))
                            dve.tensor_tensor(p[:, t, 768:1280], p[:, t, 768:1280], tmp.rearrange("p a b -> p (a b)")[:, 0:512],
                                              ALU.add).then_inc(S["qk_ready"], 1)
                        mprev, mlast = bcs[:, :, 0, :], bcs[:, :, 1, :]
                        c3 = cols.rearrange("p q (n h) -> p q n h", h=4)
                        g3 = arg.rearrange("p q (n h) -> p q n h", h=4)
                        v(dve.scalar_tensor_tensor(arg[:, 0, :], cols[:, 2, :], -1.0, cols[:, 1, :], ALU.mult, ALU.subtract))
                        v(dve.tensor_tensor(g3[:, 1], mprev, c3[:, 1], ALU.subtract))
                        v(dve.tensor_tensor(g3[:, 2], c3[:, 0], mlast, ALU.subtract))
                        dve.tensor_tensor(g3[:, 3], mprev, mlast, ALU.subtract).then_inc(S["exp_in"], 1)
                        dve.wait_ge(S["exp_out"], 2)
                        v(dve.tensor_scalar(arg[:, 2, :], arg[:, 2, :], MLD ** -0.5, None, ALU.mult))
                        dve.sem_inc(S["exp_in"], 1)
                        dve.wait_ge(S["exp_out"], 3)
                        v(dve.tensor_tensor(lamt[:, 0:1], lamt[:, 3:4], lamt[:, 2:3], ALU.subtract))
                        v(dve.tensor_tensor(nlam, lamt[:, 0:1], small[:, 102:103], ALU.subtract))

                        def reduce_scores(i):
                            t, kind = BATCHES[i]
                            nk = keys_of(t)[1] - keys_of(t)[0]
                            dve.wait_ge(S["sc_mm"], i + 1)
                            if kind == "na":
                                if t:
                                    v(dve.scalar_tensor_tensor(W1[:, :, 0:256], PS[:, 2:6, 0:256], NAD ** -0.5, bias[:, t - 1], ALU.mult, ALU.add))
                                    v(dve.tensor_scalar(W1[:, :, 256:384], PS[:, 2:6, 256:384], NAD ** -0.5, None, ALU.mult))
                                else:
                                    v(dve.tensor_scalar(W1[:, :, 0:P], PS[:, 2:6, 0:P], NAD ** -0.5, None, ALU.mult))
                                dve.tensor_reduce(nm, W1[:, :, 0:nk], AX.X, ALU.max, negate=True).then_inc(S["nm_ready"], 1)
                            else:
                                v(dve.tensor_reduce(nm, PS[:, 2:6, 0:nk], AX.X, ALU.max, negate=True))
                                dve.tensor_scalar(nm, nm, DFD ** -0.5, None, ALU.mult).then_inc(S["nm_ready"], 1)

                        def combine(i):
                            t, kind = BATCHES[i]
                            nk = keys_of(t)[1] - keys_of(t)[0]
                            dve.wait_ge(S["ex_ready"], 4 * i + 4)
                            v(dve.reciprocal(rr, rs))
                            if kind == "na":
                                return
                            odd = rr.rearrange("p (h a) -> p h a", a=2)[:, :, 1]
                            v(dve.tensor_scalar(odd, odd, nlam, None, ALU.mult))
                            for j in range(2):
                                v(dve.tensor_scalar(W2[:, 2 * j + 1, 0:nk], W2[:, 2 * j + 1, 0:nk], rr[:, 2 * j + 1:2 * j + 2], None, ALU.mult))
                                dve.scalar_tensor_tensor(W1[:, j, 0:nk], W2[:, 2 * j, 0:nk], rr[:, 2 * j:2 * j + 1],
                                                         W2[:, 2 * j + 1, 0:nk], ALU.mult, ALU.add).then_inc(S["w_ready"], 1)

                        def outputs(i):
                            t, kind = BATCHES[i]
                            dve.wait_ge(S["pv_mm"], first_map[i + 1])
                            if kind == "na":
                                dve.tensor_tensor(tok[:, t, 0:256].rearrange("p (h d) -> p h d", h=4),
                                                  PS[:, 2, 0:256].rearrange("p (h d) -> p h d", h=4),
                                                  rr[:, :, None].to_broadcast([P, 4, 64]), ALU.mult).then_inc(S["pv_ev"], 1)
                            else:
                                at = 256 + 128 * int(kind[2])
                                dve.tensor_copy(tok[:, t, at:at + 128], PS[:, 2, 0:128]).then_inc(S["pv_ev"], 1)

                        for i in range(len(BATCHES)):
                            reduce_scores(i)
                            combine(i)
                            outputs(i)
                        dve.wait_ge(S["pv_ev"], len(BATCHES))
                        do = tok[:, :, 256:512].rearrange("p t (h d) -> p t h d", h=4)
                        sq = nq[:, 0:768].rearrange("p (t h d) -> p t h d", t=T, h=4)
                        v(dve.tensor_tensor(sq, do, do, ALU.mult))
                        v(dve.tensor_reduce(ms2, nq[:, 0:768].rearrange("p (g d) -> p g d", d=64), AX.X, ALU.add))
                        dve.tensor_scalar(ms2, ms2, 1.0 / DFV, EPS, ALU.mult, ALU.add).then_inc(S["ms_ready"], 1)
                        dve.wait_ge(S["r_ready"], 3)
                        v(dve.tensor_tensor(do, do, ms2.rearrange("p (t h) -> p t h", t=T)[:, :, :, None].to_broadcast([P, T, 4, 64]), ALU.mult))
                        do12 = [tok[:, t, 256:512].rearrange("p (h d) -> p h d", h=4) for t in range(T)]
                        for t in range(T):
                            v(dve.tensor_tensor(do12[t], do12[t], prm[:, None, B_SUB:B_SUB + 64].to_broadcast([P, 4, 64]), ALU.mult))
                        seen = set()
                        two = lambda b0: PS[:, b0:b0 + 2, 0:258].rearrange("p b (h e) -> p b h e", h=2)
                        n4 = num[:, :, :].rearrange("p (b h) e -> p b h e", b=2)
                        t4 = tmp[:, :, :].rearrange("p (b h) e -> p b h e", b=2)

                        def exponents(i):
                            t, d = ML_ORDER[i]
                            dve.wait_ge(S["mb_mm"], i + 1)
                            v(dve.tensor_tensor(X[i % 2], PS[:, 3 + i % 2, :].rearrange("p (h n) -> p h n", h=4),
                                                col4(0, 2 * t + d)[:, :, None].to_broadcast([P, 4, P]), ALU.subtract))
                            dve.sem_inc(S["mb_free"], 1)
                            mask = T_MF if d == 0 else T_MB
                            dve.tensor_tensor(X[i % 2], X[i % 2], tab[:, None, mask:mask + P].to_broadcast([P, 4, P]), ALU.max).then_inc(S["d_ready"], 1)

                        def finish(o):
                            t = OUT_ORDER[o]
                            dve.wait_ge(S["r_ready"], 4 + o)
                            dve.wait_ge(S["gate_ready"], o + 1)
                            for h in range(MLH):
                                at = slice(h * P, (h + 1) * P)
                                ins = dve.scalar_tensor_tensor(tok[:, t, 512 + h * P:512 + (h + 1) * P], mlh[:, t, at],
                                                               ms2[:, 4 * o + h:4 * o + h + 1], p[:, t, 2048 + h * P:2048 + (h + 1) * P],
                                                               ALU.mult, ALU.mult)
                            ins.then_inc(S["mix_ready"], 1)

                        def add_out(o, j):
                            t = OUT_ORDER[o]
                            n = 2 * o + j
                            dve.wait_ge(S["out_mm"], n + 1)
                            if n:
                                dve.wait_ge(S["x_done"], n)
                            v(dve.tensor_tensor(wk[:, :], PS[:, 3 + j, :], gate[:, min(t, 1), j * 512:(j + 1) * 512], ALU.mult))
                            xs = x[:, t, j * 512:(j + 1) * 512]
                            dve.tensor_tensor(xs, xs, wk[:, :], ALU.add).then_inc(S["x_done"], 1)

                        exponents(0)
                        for i, (t, d) in enumerate(ML_ORDER):
                            td = 2 * t + d
                            dve.wait_ge(S["e_ready"], i + 1)
                            dve.wait_ge(S["st_ev"], T)
                            dve.tensor_tensor(num[:, :, 0:P], X[i % 2], ST[:, t, :].rearrange("p (h n) -> p h n", h=4), ALU.mult).then_inc(S["s_ready"], 1)
                            if i + 1 < 6:
                                exponents(i + 1)
                            dve.wait_ge(S["num_mm"], i + 1)
                            if t:
                                for b, bank in enumerate((7, 0)):
                                    v(dve.tensor_tensor(t4[:, b], PS[:, bank, 0:258].rearrange("p (h e) -> p h e", h=2),
                                                        arg4(1, td)[:, 2 * b:2 * b + 2, None].to_broadcast([P, 2, 129]), ALU.mult))
                                v(dve.tensor_tensor(n4, two(5), t4, ALU.add))
                            else:
                                v(dve.tensor_copy(n4, two(5)))
                            dve.sem_inc(S["num_ev"], 1)
                            v(dve.scalar_tensor_tensor(den, num[:, :, MLD], -1.0, num[:, :, MLD], ALU.mult, ALU.max))
                            v(dve.tensor_tensor(den, den, arg4(0, td), ALU.max))
                            v(dve.reciprocal(den, den))
                            out = mlh[:, t, :].rearrange("p (h n) -> p h n", h=4)
                            r4 = den[:, :, None].to_broadcast([P, 4, P])
                            if t in seen:
                                v(dve.tensor_tensor(num[:, :, 0:P], num[:, :, 0:P], r4, ALU.mult))
                                v(dve.tensor_tensor(out, out, num[:, :, 0:P], ALU.add))
                            else:
                                v(dve.tensor_tensor(out, num[:, :, 0:P], r4, ALU.mult))
                            seen.add(t)
                            if i == FINISHED[t]:
                                dve.sem_inc(S["ml_done"], 1)
                            if i < 4:
                                dve.wait_ge(S["upd_mm"], i + 1)
                                if t == 0:
                                    dve.tensor_copy(Cp[:, 4 * d:4 * d + 4, :].rearrange("p (b h) e -> p b h e", b=2), two(1)).then_inc(S["c_ready"], 1)
                                else:
                                    C4 = Caug[:, 4 * d:4 * d + 4, :].rearrange("p (b h) e -> p b h e", b=2)
                                    dve.wait_ge(S["decayed"], i - 1)
                                    dve.tensor_tensor(C4, C4, two(1), ALU.add).then_inc(S["c_ready"], 1)
                            if i == 2:
                                finish(0)
                        finish(1)
                        add_out(0, 0)
                        add_out(0, 1)
                        finish(2)
                        for o in (1, 2):
                            for j in range(2):
                                add_out(o, j)
                        dve.wait_ge(S["x_done"], 6)
                end_section()
            with ExitStack() as layer:
                acc = sb("acc", [P, T, D], ctx=layer)
                tokh = sb("tokh", [P, T, D], ctx=layer)
                tokl = sb("tokl", [P, T, D], ctx=layer)
                posm = sb("posm", [P, T, NE + 2], ctx=layer)
                wts = sb("wts", [P, T, NE + 2, 2], ctx=layer)

                with ExitStack() as sec:
                    tok = sb("tokB", [P, T, D], ctx=sec)
                    ring = sb("ringB", [P, 3, SLOTF], ctx=sec)
                    high = sb("highB", [P, 3, SLOTF], ctx=sec)
                    low = sb("lowB", [P, 3, SLOTF], ctx=sec)
                    hTp = sb("hTp", [P, 2, KC, T * P], ctx=sec)
                    hT = sb("hTB", [P, KC, T * P], ctx=sec)
                    wr = sb("wr", [P, KC, NE], ctx=sec)
                    sg = sb("sg", [P, 2, DE], ctx=sec)
                    hid = sb("hid", [P, 2, DE], ctx=sec)
                    hidT = sb("hidT", [P, 2, 2, 2, P], ctx=sec)
                    rt = sb("rt", [P, 8, T, NE], ctx=sec)
                    r8 = sb("r8", [P, T, 8], ctx=sec)
                    rem = sb("rem", [P, 8], ctx=sec)
                    br = sb("br", [P, NE], ctx=sec)
                    wfull = sb("wfull", [P, T, NE + 2], ctx=sec)
                    s_, sel, gtm, eq, cum, mask = (rt[:, i] for i in range(6))

                    with nc.Block() as block:
                        @block.sync
                        def _(sp):
                            sp.dma_start(wr[:, :, :], A["w_router"][l].rearrange("(c p) n -> p c n", p=P)).then_inc(loaded, 16)
                            for half in range(2):
                                rows = slice(half * 512, (half + 1) * 512)
                                dst = ring[:, half, :].rearrange("p (c w n) -> p c w n", c=4, w=2)
                                for w in range(2):
                                    sp.dma_start(dst[:, :, w, :], A[("w_sh1", "w_sh3")[w]][l, rows, :]
                                                 .rearrange("(c p) n -> p c n", p=P)).then_inc(landed[half], 16)
                            sp.dma_start(ring[:, 2, :].rearrange("p (c n) -> p c n", c=2),
                                         A["w_sh2"][l].rearrange("(c p) n -> p c n", p=P)).then_inc(landed[2], 16)
                            sp.dma_start(br[:, :], bcast(A["b_router"][l], NE)).then_inc(landed[3], 16)
                            for i in range(2):
                                sp.dma_start(gate[:, i, :], bcast(modd[l, i, 5 * D:6 * D], D)).then_inc(loaded2, 16)
                            sp.wait_ge(loaded2, 32)

                        @block.gpsimd
                        def _(pool):
                            norm_pool(pool, Chain(pool, chain_p))
                            for t in range(T):
                                at = slice(t * P, (t + 1) * P)
                                pool.wait_ge(S["cut_s"], t + 1)
                                pool.tensor_tensor(hi(hTp[:, 1, :, at]), hT[:, :, at], hTp[:, 0, :, at], ALU.subtract).then_inc(S["low_p"], 1)
                            pool.wait_ge(S["cut_s"], T + 3)
                            pool.tensor_tensor(hi(low[:, 2, :]), ring[:, 2, :], high[:, 2, :], ALU.subtract).then_inc(S["low_p"], 1)

                        @block.scalar
                        def _(act):
                            norm_act(act, 1)
                            norm_ev_act(act, 1, hT)
                            act.wait_ge(S["hT_s"], 4 * T)
                            act.wait_ge(S["hT_v"], 4 * T)
                            for t in range(T):
                                at = slice(t * P, (t + 1) * P)
                                act.activation(hi(hTp[:, 0, :, at]), hT[:, :, at], ACT.Copy).then_inc(S["cut_s"], 1)
                            for k in range(3):
                                act.wait_ge(landed[k], 32 if k < 2 else 16)
                                act.activation(hi(high[:, k, :]), ring[:, k, :], ACT.Copy).then_inc(S["cut_s"], 1)
                            act.wait_ge(S["rt_mm"], 1)
                            act.activation(s_.rearrange("p t e -> p (t e)"), PS[:, 0, 0:T * NE], ACT.Exp, scale=-1.0).then_inc(S["rt_e"], 1)
                            for i in range(2 * T):
                                act.wait_ge(S["back_tr"], i + 1)
                                act.activation(hi(tokh[:, i // 2, (i % 2) * 512:(i % 2 + 1) * 512]), PS[:, 4 + i % 4, :], ACT.Copy).then_inc(S["back_high"], 1)

                            def silu(t):
                                act.wait_ge(S["sh_mm"], t + 1)
                                if t >= 2:
                                    act.wait_ge(S["sh_hid"], t - 1)
                                act.activation(sg[:, t % 2, :], PS[:, 2 + t % 2, 0:DE], ACT.Silu).then_inc(S["sh_silu"], 1)

                            def turned(t):
                                act.wait_ge(S["sh_tr"], t + 1)
                                if t >= 2:
                                    act.wait_ge(S["sh_down"], t - 1)
                                act.activation(hi(hidT[:, t % 2, 0].rearrange("p f n -> p (f n)")), PS[:, 4, 0:DE], ACT.Copy).then_inc(S["sh_trev"], 1)

                            silu(0)
                            silu(1)
                            turned(0)
                            silu(2)
                            turned(1)
                            turned(2)

                        @block.tensor
                        def _(pe):
                            norm_pe(pe)
                            pe.wait_ge(loaded, 16)
                            for t in range(T):
                                pe.wait_ge(S["hT_s"], 4 * (t + 1))
                                pe.wait_ge(S["hT_v"], 4 * (t + 1))
                                for k in range(KC):
                                    mm = pe.matmul(PS[:, 0, t * NE:(t + 1) * NE], hT[:, k, t * P:(t + 1) * P], wr[:, k, :],
                                                   start=(k == 0), stop=(k == KC - 1))
                            mm.then_inc(S["rt_mm"], 1)
                            def back(i):
                                t, half = i // 2, i % 2
                                if i >= 4:
                                    pe.wait_ge(S["back_ev"], i - 3)
                                for c in range(4):
                                    mm = pe.transpose(PS[:, 4 + i % 4, c * P:(c + 1) * P], hT[:, 4 * half + c, t * P:(t + 1) * P], ident)
                                mm.then_inc(S["back_tr"], 1)

                            for i in range(4):
                                back(i)
                            def three(out, ah, al, wh, wl, first, last):
                                pe.matmul(out, hi(ah), hi(wh), start=first, stop=False)
                                pe.matmul(out, hi(ah), hi(wl), start=False, stop=False)
                                return pe.matmul(out, hi(al), hi(wh), start=False, stop=last)

                            def up(t):
                                if t >= 2:
                                    pe.wait_ge(S["sh_hid"], t - 1)
                                pe.wait_ge(S["low_p"], t + 1)
                                at = slice(t * P, (t + 1) * P)
                                for half in range(2):
                                    pe.wait_ge(S["low_v"], half + 1)
                                    for c in range(4):
                                        k = 4 * half + c
                                        w = slice(c * 512, (c + 1) * 512)
                                        mm = three(PS[:, 2 + t % 2, :], hTp[:, 0, k, at], hTp[:, 1, k, at],
                                                   high[:, half, w], low[:, half, w], k == 0, k == 7)
                                mm.then_inc(S["sh_mm"], 1)

                            def turn(t):
                                pe.wait_ge(S["sh_hid"], t + 1)
                                if t:
                                    pe.wait_ge(S["sh_low"], t)
                                for f in range(2):
                                    mm = pe.transpose(PS[:, 4, f * P:(f + 1) * P], hid[:, t % 2, f * P:(f + 1) * P], ident)
                                mm.then_inc(S["sh_tr"], 1)

                            def down(t):
                                pe.wait_ge(S["sh_low"], t + 1)
                                pe.wait_ge(S["low_p"], T + 1)
                                if t >= 2:
                                    pe.wait_ge(S["sh_done"], t - 1)
                                if t == 1:
                                    pe.wait_ge(S["rt_e"], 1)
                                for half in range(2):
                                    bank = (5 + half, 7 * half)[t % 2]
                                    for f in range(2):
                                        w = slice(f * D + half * 512, f * D + (half + 1) * 512)
                                        mm = three(PS[:, bank, :], hidT[:, t % 2, 0, f], hidT[:, t % 2, 1, f],
                                                   high[:, 2, w], low[:, 2, w], f == 0, f == 1)
                                mm.then_inc(S["sh_down"], 1)

                            up(0)
                            back(4)
                            back(5)
                            up(1)
                            pe.wait_ge(S["back_ev"], 2 * T)
                            pe.wait_ge(S["mask_ready"], 1)
                            for u in range(T):
                                for w in range(u + 1):
                                    lhs = cst[:, C_TRIU:C_TRIU + P] if w == u else ones
                                    pe.matmul(PS[:, 1, u * NE:(u + 1) * NE], lhs, mask[:, w, :], start=(w == 0), stop=(w == u))
                            for w in range(T):
                                mm = pe.matmul(PS[:, 1, T * NE:(T + 1) * NE], ones, mask[:, w, :], start=(w == 0), stop=(w == T - 1))
                            mm.then_inc(S["pos_mm"], 1)
                            turn(0)
                            up(2)
                            turn(1)
                            down(0)
                            turn(2)
                            down(1)
                            down(2)

                        @block.vector
                        def _(dve):
                            v = Chain(dve, chain_v)
                            norm_dve(dve)
                            norm_ev_dve(dve, 1, hT)
                            for k in range(2):
                                dve.wait_ge(S["cut_s"], T + k + 1)
                                dve.tensor_tensor(hi(low[:, k, :]), ring[:, k, :], high[:, k, :], ALU.subtract).then_inc(S["low_v"], 1)
                            for t in range(T):
                                for half in range(2):
                                    i = 2 * t + half
                                    at = slice(half * 512, (half + 1) * 512)
                                    dve.wait_ge(S["back_high"], i + 1)
                                    dve.tensor_tensor(hi(tokl[:, t, at]), PS[:, 4 + i % 4, :], tokh[:, t, at], ALU.subtract).then_inc(S["back_ev"], 1)
                            dve.wait_ge(S["rt_e"], 1)
                            v(dve.tensor_scalar(s_, s_, 1.0, None, ALU.add))
                            v(dve.reciprocal(s_, s_))
                            dve.wait_ge(landed[3], 16)
                            v(dve.tensor_tensor(sel, s_, br[:, None, :].to_broadcast([P, T, NE]), ALU.add))
                            for t in range(T):
                                v(dve.max(r8[:, t, :], sel[:, t, :]))
                            thr = r8[:, :, TOPK - 1:TOPK].to_broadcast([P, T, NE])
                            v(dve.tensor_tensor(gtm, sel, thr, ALU.is_gt))
                            v(dve.tensor_tensor(eq, sel, thr, ALU.is_equal))
                            v(dve.tensor_reduce(rem[:, 0:T], gtm, AX.X, ALU.add))
                            v(dve.tensor_scalar(rem[:, 0:T], rem[:, 0:T], -1.0, float(TOPK), ALU.mult, ALU.add))
                            for t in range(T):
                                v(dve.tensor_tensor_scan(cum[:, t, :], ones[:, 0:NE], eq[:, t, :], 0.0, ALU.mult, ALU.add))
                            v(dve.tensor_tensor(cum, cum, rem[:, 0:T, None].to_broadcast([P, T, NE]), ALU.is_le))
                            v(dve.tensor_tensor(eq, eq, cum, ALU.mult))
                            dve.tensor_tensor(mask, gtm, eq, ALU.add).then_inc(S["mask_ready"], 1)
                            dve.wait_ge(S["mask_ready"], 1)
                            v(dve.memset(wfull[:, :, :], 0.0))
                            v(dve.memset(posm[:, :, :], -1.0))
                            v(dve.tensor_tensor(s_, s_, mask, ALU.mult))
                            v(dve.tensor_reduce(rem[:, 0:T], s_, AX.X, ALU.add))
                            v(dve.reciprocal(rem[:, 0:T], rem[:, 0:T]))
                            v(dve.tensor_scalar(rem[:, 0:T], rem[:, 0:T], ROUTED_SCALE, None, ALU.mult))
                            v(dve.tensor_tensor(wfull[:, :, 0:NE], s_, rem[:, 0:T, None].to_broadcast([P, T, NE]), ALU.mult))
                            v(round_high(dve, wts[:, :, :, 0], wfull[:, :, :]))
                            v(dve.tensor_tensor(hi(wts[:, :, :, 1]), wfull[:, :, :], wts[:, :, :, 0], ALU.subtract))

                            def gated(t):
                                dve.wait_ge(S["sh_silu"], t + 1)
                                if t >= 2:
                                    dve.wait_ge(S["sh_tr"], t - 1)
                                dve.tensor_tensor(hid[:, t % 2, :], PS[:, 2 + t % 2, DE:2 * DE], sg[:, t % 2, :], ALU.mult).then_inc(S["sh_hid"], 1)

                            def rest(t):
                                dve.wait_ge(S["sh_trev"], t + 1)
                                dve.tensor_tensor(hi(hidT[:, t % 2, 1].rearrange("p f n -> p (f n)")), PS[:, 4, 0:DE],
                                                  hidT[:, t % 2, 0].rearrange("p f n -> p (f n)"), ALU.subtract).then_inc(S["sh_low"], 1)

                            def keep(t):
                                dve.wait_ge(S["sh_down"], t + 1)
                                for half in range(2):
                                    bank = (5 + half, 7 * half)[t % 2]
                                    ins = dve.tensor_copy(acc[:, t, half * 512:(half + 1) * 512], PS[:, bank, :])
                                ins.then_inc(S["sh_done"], 1)

                            gated(0)
                            dve.wait_ge(S["pos_mm"], 1)
                            pos = PS[:, 1, 0:T * NE].rearrange("p (t e) -> p t e", t=T)
                            v(dve.scalar_tensor_tensor(posm[:, :, 0:NE], pos, 1.0, mask, ALU.add, ALU.mult))
                            v(dve.tensor_scalar(posm[:, :, 0:NE], posm[:, :, 0:NE], -1.0, None, ALU.add))
                            v(dve.tensor_reduce(rem[:, 4:5], PS[:, 1, T * NE:(T + 1) * NE], AX.X, ALU.max))
                            v(dve.tensor_scalar(rem[:, 5:6], rem[:, 4:5], float(SLOTS), 1.0, ALU.is_gt, ALU.add))
                            v(dve.tensor_scalar(rem[:, 6:7], rem[:, 4:5], 2.0 * SLOTS, None, ALU.is_gt))
                            v(dve.tensor_tensor(npass[:, :], rem[:, 5:6], rem[:, 6:7], ALU.add))
                            gated(1)
                            rest(0)
                            gated(2)
                            rest(1)
                            keep(0)
                            rest(2)
                            keep(1)
                            keep(2)
                            dve.wait_ge(S["sh_done"], T)
                    end_section()

                passes = nc.values_load(npass[0:1, 0:1], min_val=1, max_val=T)
                with ExitStack() as sec:
                    raw = sb("raw", [P, 3, SLOTF], ctx=sec)
                    high = sb("high", [P, 3, SLOTF], ctx=sec)
                    low = sb("low", [P, 3, SLOTF], ctx=sec)
                    Pb = sb("Pb", [P, 2, T, 2 * SLOTS], ctx=sec)
                    PTb = sb("PTb", [P, GROUP, T * P], ctx=sec)
                    hTe = sb("hTe", [P, 12, 2, 2 * SLOTS], ctx=sec)
                    idw = sb("idw", [P, 2, T, P + 2], ctx=sec)
                    gs = sb("gs", [P, 2], ctx=sec)
                    gparts = sb("gparts", [P, T, 2], ctx=sec)
                    sg = sb("sgC", [P, DE], ctx=sec)
                    hid = sb("hidC", [P, DE], ctx=sec)
                    hidT = sb("hidTC", [P, 2, 2, P], ctx=sec)
                    yh = sb("yh", [P, GROUP, D], ctx=sec)
                    yl = sb("yl", [P, GROUP, D], ctx=sec)
                    NG = NE // GROUP
                    SUM_BANK = (7, 3, 2, 7, 3, 7)
                    LOADS = (32, 32, 16)
                    CV, CP = 3, 1

                    wcol = lambda c: bass.ds(c, 1)

                    SPREAD = ((1, 2, 1),) * (GROUP - 1) + ((2, 2, 0),)

                    def chunks(j, when):
                        first = sum(SPREAD[j][:when])
                        return range(first, first + SPREAD[j][when])

                    def block_of(pair, k):
                        return 4 * (pair % 2) + k if k < 4 else 4 + k

                    def cut_done(eng, e, k):
                        if k == 1:
                            eng.wait_ge(S["low_p"], e + 1 + CP)
                        else:
                            eng.wait_ge(S["low_v"], 2 * e + (1 if k == 0 else 2) + CV)

                    def products_done(eng, e, k):
                        eng.wait_ge(slot_used, 3 * e + k + 4)

                    with nc.Fori(0, passes) as _pass:
                        with nc.Block() as block:

                            @block.sync
                            def _(sp):
                                with sp.Fori(0, NG) as g:
                                    for j in range(GROUP):
                                        e = GROUP * g + j
                                        for k in range(3):
                                            cut_done(sp, e - 1, k)
                                            if k < 2:
                                                rows = slice(k * 512, (k + 1) * 512)
                                                dst = raw[:, k, :].rearrange("p (c w n) -> p c w n", c=4, w=2)
                                                for w in range(2):
                                                    sp.dma_start(dst[:, :, w, :], A[("w_exp1", "w_exp3")[w]][l, e, rows, :]
                                                                 .rearrange("(c p) n -> p c n", p=P)).then_inc(landed[k], 16)
                                            else:
                                                sp.dma_start(raw[:, k, :].rearrange("p (c n) -> p c n", c=2),
                                                             A["w_exp2"][l, e].rearrange("(c p) n -> p c n", p=P)).then_inc(landed[k], 16)

                            @block.gpsimd
                            def _(pool):
                                def rest(e):
                                    pool.wait_ge(S["cut_p"], e + 1)
                                    pool.tensor_tensor(hi(low[:, 1, :]), raw[:, 1, :], high[:, 1, :], ALU.subtract).then_inc(S["low_p"], 1)

                                pool.sem_inc(S["low_p"], CP)

                                def token_weights(b, e):
                                    if not isinstance(e, int):
                                        pool.wait_ge(S["pt_mm"], e - 1)
                                    pool.tensor_copy(hi(idw[:, b, :, P:P + 2]), wts[:, :, wcol(e), :].rearrange("p t o w -> p t (o w)")).then_inc(S["idw_ready"], 1)

                                for b in range(2):
                                    for c in range(T):
                                        ins = pool.tensor_copy(hi(idw[:, b, c, 0:P]), ident)
                                        if c < T - 1:
                                            ins.then_inc(S["id_part"], 1)
                                    ins.then_inc(S["id_part"], 1)
                                for b in range(2):
                                    if b == 0:
                                        pool.wait_ge(S["id_part"], 2 * T)
                                    token_weights(b, b)
                                rest(0)
                                rest(1)
                                with pool.Fori(1, NE // 2) as h:
                                    for b in range(2):
                                        e = 2 * h + b
                                        token_weights(b, e)
                                        rest(e)

                            @block.scalar
                            def _(act):
                                def take(pair, k, n):
                                    act.wait_ge(S["ga_mm"], n + 1)
                                    act.activation(hi(hTe[:, block_of(pair, k)].rearrange("p a n -> p (a n)")), PS[:, k % 2, :],
                                                   ACT.Copy).then_inc(S["ga_ev"], 1)

                                def turned(j, n):
                                    act.wait_ge(S["pt_mm"], n)
                                    got = PS[:, 4, 0:T * (P + 2)].rearrange("p (c n) -> p c n", c=T)
                                    act.activation(gparts[:, :, :], got[:, :, P:P + 2], ACT.Copy, accum_out=gs[:, j % 2:j % 2 + 1]).then_inc(S["gs_ev"], 1)
                                    act.activation(hi(PTb[:, j, :].rearrange("p (c n) -> p c n", c=T)), got[:, :, 0:P], ACT.Copy).then_inc(S["pt_ev"], 1)

                                def cut_down(e):
                                    act.wait_ge(landed[2], LOADS[2] * (e + 1))
                                    products_done(act, e - 1, 2)
                                    act.activation(hi(high[:, 2, :]), raw[:, 2, :], ACT.Copy).then_inc(S["cut_s"], 1)

                                def step(g, last=False):
                                    for j in range(GROUP):
                                        e = GROUP * g + j
                                        more = not (last and j == GROUP - 1)
                                        pair = j // 2 + 1
                                        k0 = 4 * (j % 2)
                                        n0 = 16 * g + 8 * pair + k0
                                        gathering = not (last and pair == 2)
                                        products_done(act, e, 1)
                                        act.activation(sg[:, :], PS[:, 2, 0:DE], ACT.Silu).then_inc(S["silu"], 1)
                                        if gathering:
                                            for i in chunks(j, 0):
                                                take(pair, k0 + i, n0 + i)
                                        act.wait_ge(S["ht_mm"], e + 1)
                                        act.activation(hi(hidT[:, 0, :, :].rearrange("p b n -> p (b n)")), PS[:, 3, 0:DE], ACT.Copy).then_inc(S["ht_ev"], 1)
                                        if j < GROUP - 1:
                                            turned(j + 1, e + 2)
                                        if gathering:
                                            for i in chunks(j, 1):
                                                take(pair, k0 + i, n0 + i)
                                        products_done(act, e, 2)
                                        act.activation(hi(yh[:, j, :].rearrange("p (b n) -> p b n", b=2)), PS[:, 5:7, :], ACT.Copy).then_inc(S["y_high"], 1)
                                        if gathering:
                                            for i in chunks(j, 2):
                                                take(pair, k0 + i, n0 + i)
                                        if more:
                                            cut_down(e + 1)
                                        if more and j == GROUP - 1:
                                            act.wait_ge(S["sc_mm"], 6 * g + 6)
                                            turned(0, e + 2)

                                for k in range(KC):
                                    take(0, k, k)
                                turned(0, 1)
                                act.wait_ge(landed[2], LOADS[2])
                                act.activation(hi(high[:, 2, :]), raw[:, 2, :], ACT.Copy).then_inc(S["cut_s"], 1)
                                with act.Fori(0, NG - 1) as g:
                                    step(g)
                                step(NG - 1, last=True)

                            @block.tensor
                            def _(pe):
                                pe.sem_inc(slot_used, 3)

                                def gather(pair, k, n):
                                    if not (isinstance(n, int) and n < 2):
                                        pe.wait_ge(S["ga_ev"], n - 1)
                                    for part, src in enumerate((tokh, tokl)):
                                        for c in range(T):
                                            mm = pe.matmul(PS[:, k % 2, part * 256:(part + 1) * 256], hi(src[:, c, k * P:(k + 1) * P]),
                                                           hi(Pb[:, pair % 2, c, :]), start=(c == 0), stop=(c == T - 1))
                                    mm.then_inc(S["ga_mm"], 1)

                                def turn(j, e):
                                    pe.wait_ge(S["pt_ev"], e + 1)
                                    pe.wait_ge(S["gs_ev"], e + 1)
                                    at = slice((j % 2) * SLOTS, (j % 2 + 1) * SLOTS)
                                    pe.wait_ge(S["idw_ready"], e + 1)
                                    for c in range(T):
                                        mm = pe.matmul(PS[:, 4, c * (P + 2):(c + 1) * (P + 2)], hi(Pb[:, j // 2, c, at]),
                                                       hi(idw[:, j % 2, c, :]), start=True, stop=True)
                                    mm.then_inc(S["pt_mm"], 1)

                                def three(out, ah, al, wh, wl, first, last):
                                    pe.matmul(out, hi(ah), hi(wh), start=first, stop=False)
                                    pe.matmul(out, hi(ah), hi(wl), start=False, stop=False)
                                    return pe.matmul(out, hi(al), hi(wh), start=False, stop=last)

                                def step(g, last=False):
                                    for j in range(GROUP):
                                        e = GROUP * g + j
                                        own = j // 2
                                        pair, k0 = own + 1, 4 * (j % 2)
                                        gathering = not (last and pair == 2)
                                        n0 = 16 * g + 8 * pair + k0
                                        at = slice((j % 2) * SLOTS, (j % 2 + 1) * SLOTS)
                                        for half in range(2):
                                            pe.wait_ge(S["ga_ev"], 16 * g + 8 * own + 4 * half + 4)
                                            cut_done(pe, e, half)
                                            for c in range(4):
                                                k = 4 * half + c
                                                w = slice(c * 512, (c + 1) * 512)
                                                h = hTe[:, block_of(own, k)]
                                                mm = three(PS[:, 2, :], h[:, 0, at], h[:, 1, at], high[:, half, w], low[:, half, w], k == 0, k == 7)
                                            mm.then_inc(slot_used, 1)
                                        if gathering:
                                            if j % 2 == 0:
                                                pe.wait_ge(S["pb_ready"], 2 * g + pair + 1)
                                            for i in chunks(j, 0):
                                                gather(pair, k0 + i, n0 + i)
                                        if j < GROUP - 1:
                                            turn(j + 1, e + 1)
                                        pe.wait_ge(S["hid_ready"], e + 1)
                                        if j == 0:
                                            pe.wait_ge(S["sc_ev"], 6 * g + 1)
                                        for f in range(2):
                                            mm = pe.transpose(PS[:, 3, f * P:(f + 1) * P], hid[:, f * P:(f + 1) * P], ident)
                                        mm.then_inc(S["ht_mm"], 1)
                                        if gathering:
                                            for i in chunks(j, 1):
                                                gather(pair, k0 + i, n0 + i)
                                        pe.wait_ge(S["hidT_low"], e + 1)
                                        pe.wait_ge(S["y_low"], e + 1)
                                        cut_done(pe, e, 2)
                                        for half in range(2):
                                            for f in range(2):
                                                w = slice(f * D + half * 512, f * D + (half + 1) * 512)
                                                mm = three(PS[:, 5 + half, :], hidT[:, 0, f, :], hidT[:, 1, f, :],
                                                           high[:, 2, w], low[:, 2, w], f == 0, f == 1)
                                        mm.then_inc(slot_used, 1)
                                        if gathering:
                                            for i in chunks(j, 2):
                                                gather(pair, k0 + i, n0 + i)
                                    def scatter(q, js):
                                        c, half = q // 2, q % 2
                                        for j in js:
                                            for yy in (yh, yl):
                                                mm = pe.matmul(PS[:, SUM_BANK[q], :], hi(PTb[:, j, c * P:(c + 1) * P]),
                                                               hi(yy[:, j, half * 512:(half + 1) * 512]),
                                                               start=(j == 0 and yy is yh), stop=(j == GROUP - 1 and yy is yl))
                                        if j == GROUP - 1:
                                            mm.then_inc(S["sc_mm"], 1)

                                    pe.wait_ge(S["pt_ev"], GROUP * g + GROUP + 1)
                                    pe.wait_ge(S["y_low"], GROUP * g + GROUP)
                                    for q in range(3):
                                        scatter(q, range(GROUP - 1))
                                    pe.wait_ge(S["y_low"], GROUP * g + GROUP + 1)
                                    for q in range(3):
                                        scatter(q, (GROUP - 1,))
                                    for q in range(3, 2 * T):
                                        former = {3: 0, 4: 1, 5: 3}[q]
                                        pe.wait_ge(S["sc_ev"], 6 * g + former + 2)
                                        scatter(q, range(GROUP))
                                    if not last:
                                        turn(0, GROUP * g + GROUP)

                                pe.wait_ge(S["pb_ready"], 1)
                                for k in range(KC):
                                    gather(0, k, k)
                                turn(0, 0)
                                with pe.Fori(0, NG - 1) as g:
                                    step(g)
                                step(NG - 1, last=True)

                            @block.vector
                            def _(dve):
                                for name in ("pt_ev", "gs_ev", "y_low", "sc_ev"):
                                    dve.sem_inc(S[name], 1)
                                dve.sem_inc(S["low_v"], CV)

                                def one_hots(b, e):
                                    for c in range(T):
                                        for i in range(2):
                                            ins = dve.tensor_scalar(hi(Pb[:, b, c, i * SLOTS:(i + 1) * SLOTS]), cst[:, C_IOTA:C_IOTA + P],
                                                                    posm[:, c, wcol(e + i)], None, ALU.is_equal)
                                    ins.then_inc(S["pb_ready"], 1)

                                def cut_high(e, k, first=False):
                                    dve.wait_ge(landed[k], LOADS[k] * (e + 1))
                                    if not first:
                                        products_done(dve, e - 1, k)
                                    round_high(dve, high[:, k, :], raw[:, k, :]).then_inc(S["cut_p" if k else "cut_v"], 1)

                                def cut_low(e, k):
                                    dve.wait_ge(S["cut_s" if k else "cut_v"], e + 1)
                                    dve.tensor_tensor(hi(low[:, k, :]), raw[:, k, :], high[:, k, :], ALU.subtract).then_inc(S["low_v"], 1)

                                def step(g, last=False):
                                    for j in range(GROUP):
                                        e = GROUP * g + j
                                        b = j % 2
                                        more = not (last and j == GROUP - 1)
                                        dve.wait_ge(S["silu"], e + 1)
                                        dve.wait_ge(S["gs_ev"], e + 2)
                                        dve.scalar_tensor_tensor(hid[:, :], PS[:, 2, DE:2 * DE], gs[:, b:b + 1], sg[:, :],
                                                                 ALU.mult, ALU.mult).then_inc(S["hid_ready"], 1)
                                        if more:
                                            cut_high(e + 1, 0)
                                        dve.wait_ge(S["ht_ev"], e + 1)
                                        dve.tensor_tensor(hi(hidT[:, 1, :, :].rearrange("p b n -> p (b n)")), PS[:, 3, 0:DE],
                                                          hidT[:, 0, :, :].rearrange("p b n -> p (b n)"), ALU.subtract).then_inc(S["hidT_low"], 1)
                                        if more:
                                            cut_high(e + 1, 1)
                                            cut_low(e + 1, 0)
                                        dve.wait_ge(S["y_high"], e + 1)
                                        dve.tensor_tensor(hi(yl[:, j, :].rearrange("p (b n) -> p b n", b=2)), PS[:, 5:7, :],
                                                          yh[:, j, :].rearrange("p (b n) -> p b n", b=2), ALU.subtract).then_inc(S["y_low"], 1)
                                        if j % 2 and not last:
                                            dve.wait_ge(S["pt_mm"], e + 1)
                                            one_hots(j // 2, e + 3)
                                        if j < GROUP - 1:
                                            cut_low(e + 1, 2)
                                    for q in range(2 * T):
                                        c, half = q // 2, q % 2
                                        dve.wait_ge(S["sc_mm"], 6 * g + q + 1)
                                        at = acc[:, c, half * 512:(half + 1) * 512]
                                        dve.tensor_tensor(at, at, PS[:, SUM_BANK[q], :], ALU.add).then_inc(S["sc_ev"], 1)
                                    if not last:
                                        cut_low(GROUP * g + GROUP, 2)

                                one_hots(0, 0)
                                one_hots(1, 2)
                                for k in range(2):
                                    cut_high(0, k, first=True)
                                cut_low(0, 0)
                                cut_low(0, 2)
                                with dve.Fori(0, NG - 1) as g:
                                    step(g)
                                step(NG - 1, last=True)
                                dve.wait_ge(S["pb_ready"], NE // 2)
                                dve.tensor_scalar(posm[:, :, 0:NE], posm[:, :, 0:NE], -float(SLOTS), None, ALU.add).then_inc(chain_v, 1)
                                dve.wait_ge(chain_v, 1)
                                dve.wait_ge(S["sc_ev"], 6 * NG + 1)
                        end_section()

                with nc.Block() as block:
                    def add_experts(eng, chunks, steps):
                        for t in chunks:
                            eng.tensor_tensor(acc[:, t, :], acc[:, t, :], gate[:, min(t, 1), :], ALU.mult).then_inc(steps, 1)
                        for i, t in enumerate(chunks):
                            eng.wait_ge(steps, i + 1)
                            eng.tensor_tensor(x[:, t, :], x[:, t, :], acc[:, t, :], ALU.add).then_inc(steps, 1)
                        eng.wait_ge(steps, 2 * len(chunks))

                    @block.vector
                    def _(dve):
                        add_experts(dve, (0, 1), chain_v)

                    @block.gpsimd
                    def _(pool):
                        add_experts(pool, (2,), chain_p)
                end_section()

        with nc.Block() as block:
            @block.sync
            def _(sp):
                sp.dma_start(O["y_prompt"][0], x[:, 0, :]).then_inc(stored, 16)
                sp.dma_start(O["y_sample"][0].rearrange("(t p) d -> p t d", p=P), x[:, 1:3, :]).then_inc(stored, 16)
                sp.wait_ge(stored, 32)


OUTS = ["y_prompt", "y_sample", "new_na_k", "new_na_v", "new_df_k", "new_df_v", "new_ml_C", "new_ml_n", "new_ml_m"]
INS = ["x_prompt", "x_sample", "cache_na_k", "cache_na_v", "cache_df_k", "cache_df_v", "state_ml_C", "state_ml_n",
       "state_ml_m", "c", "c_ctx", "w_ada", "b_ada", "g_norm1", "g_norm2", "w_in", "w_out", "na_qn", "na_kn", "na_rpb",
       "df_qn", "df_kn", "df_lam", "df_subln", "ml_gate_b", "ml_outn", "w_router", "b_router", "w_exp1", "w_exp3",
       "w_exp2", "w_sh1", "w_sh3", "w_sh2"]
SHAPES = [(1, P, D), (1, 2 * P, D), (1, DEPTH, NAH, P, NAD), (1, DEPTH, NAH, P, NAD), (1, DEPTH, DFH, 2, P, DFD),
          (1, DEPTH, DFH, P, DFV), (1, DEPTH, 2, MLH, MLD, MLD), (1, DEPTH, 2, MLH, MLD), (1, DEPTH, 2, MLH)]


def kernel(**inputs):
    import concourse.bacc as bacc
    from concourse.bass_utils import run_bass_kernel_spmd

    nc = bacc.Bacc("TRN2", target_bir_lowering=False, num_devices=1)
    arrays = {f"in_{n}": np.ascontiguousarray(inputs[n]) for n in INS}
    arrays["in_consts"] = constants()
    A = {n[3:]: nc.dram_tensor(n, a.shape, mybir.dt.from_np(a.dtype), kind="ExternalInput").ap() for n, a in arrays.items()}
    O = {n: nc.dram_tensor(f"out_{n}", s, F32, kind="ExternalOutput").ap() for n, s in zip(OUTS, SHAPES)}
    program(nc, A, O)
    r = run_bass_kernel_spmd(nc, [arrays], core_ids=[0])
    return tuple(r.results[0][f"out_{n}"] for n in OUTS)
```
